# Optimizing a Trainium2 kernel written in Bass

```python
import math
import jax
import jax.numpy as jnp
from jax import lax
import numpy as np
import jax, jax.numpy as jnp

D_MODEL = 1024
BATCH = 1
SEQ = 256
DEPTH = 1

HEAD_DIM = 64
DSA_HEADS = 16
DSA_KV_DIM = 64
IDX_HEADS = 8
IDX_DIM = 32
DSA_TOPK = 256
NSA_HEADS = 16
NSA_KV_HEADS = 2
NSA_GROUP = NSA_HEADS // NSA_KV_HEADS
CMP_BLOCK = 32
CMP_STRIDE = 16
SEL_BLOCK = 64
SEL_TOPN = 4
WINDOW = 512
SSD_INNER = 2 * D_MODEL
SSD_HEAD_DIM = 64
SSD_HEADS = SSD_INNER // SSD_HEAD_DIM
SSD_GROUPS = 4
SSD_HPG = SSD_HEADS // SSD_GROUPS
SSD_STATE = 128
SSD_CONV_DIM = SSD_INNER + 2 * SSD_GROUPS * SSD_STATE
CONV_WIDTH = 4
SSD_CHUNK = 128
D_FF = 4 * D_MODEL
Q_BLOCK = 128
EPS = 1e-6
NEG = -1e30
IN_SPLITS = (DSA_HEADS * HEAD_DIM, DSA_KV_DIM, DSA_KV_DIM, IDX_HEADS * IDX_DIM, IDX_DIM, IDX_HEADS,
             NSA_HEADS * HEAD_DIM, 6 * NSA_KV_HEADS * HEAD_DIM, 3 * NSA_HEADS,
             SSD_INNER, SSD_CONV_DIM, SSD_HEADS, 3 * D_MODEL)
D_IN = sum(IN_SPLITS)


def rms_norm(x, g):
    xf = x.astype(jnp.float32)
    y = xf * lax.rsqrt(jnp.mean(xf * xf, axis=-1, keepdims=True) + EPS)
    return (y * g).astype(x.dtype)

def _to_blocks(a):
    b, s = a.shape[:2]
    return jnp.moveaxis(a.reshape((b, s // Q_BLOCK, Q_BLOCK) + a.shape[2:]), 1, 0)

def _from_blocks(a):
    nb, b = a.shape[:2]
    return jnp.moveaxis(a, 0, 1).reshape((b, nb * a.shape[2]) + a.shape[3:])

def dsa_mixer(q, k, v, iq, ik, iw):
    seq = q.shape[1]
    n_sel = min(DSA_TOPK, seq // 4)
    key_pos = jnp.arange(seq)
    scale = HEAD_DIM ** -0.5
    gather = jax.vmap(lambda a, i: a[i])

    def block(args):
        qb, iqb, iwb, start = args
        t = start + jnp.arange(Q_BLOCK)
        idx = jnp.einsum('bqhd,bsd->bqhs', iqb, ik)
        idx = jnp.einsum('bqh,bqhs->bqs', iwb, jax.nn.relu(idx)).astype(jnp.float32)
        idx = jnp.where((key_pos[None, :] <= t[:, None])[None], idx, -jnp.inf)
        _, sel = lax.top_k(idx, n_sel)
        k_sel = gather(k, sel)
        v_sel = gather(v, sel)
        s = jnp.einsum('bqhd,bqkd->bqhk', qb, k_sel).astype(jnp.float32) * scale
        s = jnp.where((sel <= t[None, :, None])[:, :, None, :], s, NEG)
        p = jax.nn.softmax(s, axis=-1).astype(v.dtype)
        return jnp.einsum('bqhk,bqkd->bqhd', p, v_sel)

    starts = jnp.arange(seq // Q_BLOCK) * Q_BLOCK
    out = lax.map(block, (_to_blocks(q), _to_blocks(iq), _to_blocks(iw), starts))
    return _from_blocks(out)

def nsa_mixer(q, kc, vc, ks, vs, kw, vw, gates, k_norm_g, cmp_pos, cmp_w):
    bsz, seq = q.shape[:2]
    scale = HEAD_DIM ** -0.5
    n_cmp = (seq - CMP_BLOCK) // CMP_STRIDE + 1
    win_idx = jnp.arange(n_cmp)[:, None] * CMP_STRIDE + jnp.arange(CMP_BLOCK)[None, :]

    def compress(a, pos, w):
        blocks = a[:, win_idx] + pos[None, None, :, None, :]
        return jnp.einsum('bnlgd,lde->bnge', blocks, w)

    k_cmp = rms_norm(compress(kc, cmp_pos[0], cmp_w[0]), k_norm_g[0])
    v_cmp = compress(vc, cmp_pos[1], cmp_w[1])
    cmp_start = jnp.arange(n_cmp) * CMP_STRIDE
    cmp_end = cmp_start + CMP_BLOCK - 1
    n_blk = seq // SEL_BLOCK
    n_sel = min(SEL_TOPN, n_blk)
    blk_start = jnp.arange(n_blk) * SEL_BLOCK
    cover = ((cmp_start[:, None] < blk_start[None, :] + SEL_BLOCK)
             & (cmp_start[:, None] + CMP_BLOCK > blk_start[None, :])).astype(jnp.float32)
    ks = rms_norm(ks, k_norm_g[1])
    ks_blocks = ks.reshape(bsz, n_blk, SEL_BLOCK, NSA_KV_HEADS, HEAD_DIM).transpose(0, 3, 1, 2, 4)
    vs_blocks = vs.reshape(bsz, n_blk, SEL_BLOCK, NSA_KV_HEADS, HEAD_DIM).transpose(0, 3, 1, 2, 4)
    gather_blocks = jax.vmap(jax.vmap(lambda blk, i: blk[i]))
    kw = rms_norm(kw, k_norm_g[2])
    pad = ((0, 0), (WINDOW, 0), (0, 0), (0, 0))
    kw_pad = jnp.pad(kw, pad)
    vw_pad = jnp.pad(vw, pad)
    n_slc_keys = n_sel * SEL_BLOCK

    def block(args):
        qb, gb, start = args
        t = start + jnp.arange(Q_BLOCK)
        s = jnp.einsum('bqghd,bngd->bqghn', qb, k_cmp).astype(jnp.float32) * scale
        vis = (cmp_end[None, :] <= t[:, None])[None, :, None, None, :]
        s = jnp.where(vis, s, NEG)
        p_cmp = jax.nn.softmax(s, axis=-1) * vis
        o_cmp = jnp.einsum('bqghn,bngd->bqghd', p_cmp.astype(v_cmp.dtype), v_cmp)
        imp = jnp.einsum('bqghn,nj->bqgj', p_cmp, cover)
        cur = t // SEL_BLOCK
        j = jnp.arange(n_blk)
        forced = ((j[None, :] == cur[:, None]) | (j[None, :] == 0))[None, :, None, :]
        future = (j[None, :] > cur[:, None])[None, :, None, :]
        imp = jnp.where(forced, jnp.inf, jnp.where(future, -jnp.inf, imp))
        _, sel = lax.top_k(imp, n_sel)
        sel_t = sel.transpose(0, 2, 1, 3)
        bq = qb.shape[0]
        k_sel = gather_blocks(ks_blocks, sel_t).reshape(bq, NSA_KV_HEADS, Q_BLOCK, n_slc_keys, HEAD_DIM)
        v_sel = gather_blocks(vs_blocks, sel_t).reshape(bq, NSA_KV_HEADS, Q_BLOCK, n_slc_keys, HEAD_DIM)
        pos = (sel_t[..., None] * SEL_BLOCK + jnp.arange(SEL_BLOCK)).reshape(bq, NSA_KV_HEADS, Q_BLOCK, n_slc_keys)
        ok = (pos <= t[None, None, :, None]).transpose(0, 2, 1, 3)[:, :, :, None, :]
        s = jnp.einsum('bqghd,bgqkd->bqghk', qb, k_sel).astype(jnp.float32) * scale
        s = jnp.where(ok, s, NEG)
        p = jax.nn.softmax(s, axis=-1).astype(v_sel.dtype)
        o_slc = jnp.einsum('bqghk,bgqkd->bqghd', p, v_sel)
        kwb = lax.dynamic_slice_in_dim(kw_pad, start, WINDOW + Q_BLOCK, axis=1)
        vwb = lax.dynamic_slice_in_dim(vw_pad, start, WINDOW + Q_BLOCK, axis=1)
        pos_w = start - WINDOW + jnp.arange(WINDOW + Q_BLOCK)
        ok_w = ((pos_w[None, :] <= t[:, None]) & (pos_w[None, :] > t[:, None] - WINDOW)
                & (pos_w[None, :] >= 0))[None, :, None, None, :]
        s = jnp.einsum('bqghd,bkgd->bqghk', qb, kwb).astype(jnp.float32) * scale
        s = jnp.where(ok_w, s, NEG)
        p = jax.nn.softmax(s, axis=-1).astype(vwb.dtype)
        o_win = jnp.einsum('bqghk,bkgd->bqghd', p, vwb)
        return gb[..., 0:1] * o_cmp + gb[..., 1:2] * o_slc + gb[..., 2:3] * o_win

    starts = jnp.arange(seq // Q_BLOCK) * Q_BLOCK
    out = lax.map(block, (_to_blocks(q), _to_blocks(gates), starts))
    return _from_blocks(out)

def causal_conv(x, w, b):
    out = lax.conv_general_dilated(x, w[:, None, :], window_strides=(1,), padding=[(CONV_WIDTH - 1, 0)],
                                   dimension_numbers=('NWC', 'WIO', 'NWC'), feature_group_count=x.shape[-1])
    return out + b

def ssd_mixer(z, xbc, dt, conv_w, conv_b, dt_bias, a_log, d_skip, norm_g):
    bsz, seq = z.shape[:2]
    nc = seq // SSD_CHUNK
    xbc = jax.nn.silu(causal_conv(xbc, conv_w, conv_b))
    gn = SSD_GROUPS * SSD_STATE
    xs = xbc[..., :SSD_INNER].reshape(bsz, nc, SSD_CHUNK, SSD_GROUPS, SSD_HPG, SSD_HEAD_DIM)
    bm = xbc[..., SSD_INNER:SSD_INNER + gn].reshape(bsz, nc, SSD_CHUNK, SSD_GROUPS, SSD_STATE)
    cm = xbc[..., SSD_INNER + gn:].reshape(bsz, nc, SSD_CHUNK, SSD_GROUPS, SSD_STATE)
    dtc = jax.nn.softplus(dt.astype(jnp.float32) + dt_bias).reshape(bsz, nc, SSD_CHUNK, SSD_GROUPS, SSD_HPG)
    a = -jnp.exp(a_log.astype(jnp.float32)).reshape(SSD_GROUPS, SSD_HPG)
    a_cum = jnp.cumsum(dtc * a, axis=2)
    seg = a_cum[:, :, :, None] - a_cum[:, :, None, :]
    tril = jnp.tril(jnp.ones((SSD_CHUNK, SSD_CHUNK), dtype=bool))[None, None, :, :, None, None]
    lmat = jnp.exp(jnp.where(tril, seg, -jnp.inf))
    cb = jnp.einsum('bcign,bcjgn->bcijg', cm, bm)
    y_diag = jnp.einsum('bcijg,bcijgh,bcjgh,bcjghp->bcighp', cb, lmat, dtc, xs)
    decay_states = jnp.exp(a_cum[:, :, -1:] - a_cum)
    states = jnp.einsum('bcjgn,bcjgh,bcjghp->bcghpn', bm, decay_states * dtc, xs)
    chunk_decay = jnp.exp(a_cum[:, :, -1])

    def step(h, inp):
        s_c, d_c = inp
        return h * d_c[..., None, None] + s_c, h

    h0 = jnp.zeros((bsz, SSD_GROUPS, SSD_HPG, SSD_HEAD_DIM, SSD_STATE), states.dtype)
    _, h_in = lax.scan(step, h0, (jnp.moveaxis(states, 1, 0), jnp.moveaxis(chunk_decay, 1, 0)))
    h_in = jnp.moveaxis(h_in, 0, 1)
    y_off = jnp.einsum('bcign,bcghpn,bcigh->bcighp', cm, h_in, jnp.exp(a_cum))
    y = y_diag + y_off + xs * d_skip.reshape(SSD_GROUPS, SSD_HPG)[:, :, None]
    y = y.reshape(bsz, seq, SSD_INNER)
    y = rms_norm(y * jax.nn.silu(z.astype(jnp.float32)), norm_g)
    return y.astype(z.dtype)

def first_inputs(seed: int = 0) -> dict:
    key = jax.random.key(seed)
    ks = jax.random.split(key, 24)
    f32 = jnp.float32

    def nrm(k, shape, scale):
        return jax.random.normal(k, shape, f32) * scale

    def gain(k, shape):
        return 1.0 + 0.02 * jax.random.normal(k, shape, f32)

    dt0 = jnp.exp(jax.random.uniform(ks[12], (DEPTH, SSD_HEADS), f32, math.log(1e-3), math.log(1e-1)))
    return {
        'x': nrm(ks[0], (BATCH, SEQ, D_MODEL), 1.0),
        'norm1_g': gain(ks[1], (DEPTH, D_MODEL)),
        'w_in': nrm(ks[2], (DEPTH, D_MODEL, D_IN), D_MODEL ** -0.5),
        'dsa_q_norm': gain(ks[3], (DEPTH, HEAD_DIM)),
        'dsa_k_norm': gain(ks[4], (DEPTH, DSA_KV_DIM)),
        'nsa_q_norm': gain(ks[5], (DEPTH, HEAD_DIM)),
        'nsa_k_norm': gain(ks[6], (DEPTH, 3, HEAD_DIM)),
        'nsa_cmp_pos': nrm(ks[7], (DEPTH, 2, CMP_BLOCK, HEAD_DIM), 0.02),
        'nsa_cmp_w': nrm(ks[8], (DEPTH, 2, CMP_BLOCK, HEAD_DIM, HEAD_DIM), (CMP_BLOCK * HEAD_DIM) ** -0.5),
        'ssd_conv_w': nrm(ks[9], (DEPTH, CONV_WIDTH, SSD_CONV_DIM), CONV_WIDTH ** -0.5),
        'ssd_conv_b': nrm(ks[10], (DEPTH, SSD_CONV_DIM), 0.02),
        'ssd_dt_bias': dt0 + jnp.log(-jnp.expm1(-dt0)),
        'ssd_a_log': jnp.log(jax.random.uniform(ks[11], (DEPTH, SSD_HEADS), f32, 1.0, 16.0)),
        'ssd_d': gain(ks[13], (DEPTH, SSD_HEADS)),
        'ssd_norm_g': gain(ks[14], (DEPTH, SSD_INNER)),
        'w_br_dsa': nrm(ks[15], (DEPTH, DSA_HEADS * HEAD_DIM, D_MODEL), (DSA_HEADS * HEAD_DIM) ** -0.5),
        'w_br_nsa': nrm(ks[16], (DEPTH, NSA_HEADS * HEAD_DIM, D_MODEL), (NSA_HEADS * HEAD_DIM) ** -0.5),
        'w_br_ssd': nrm(ks[17], (DEPTH, SSD_INNER, D_MODEL), SSD_INNER ** -0.5),
        'w_out': nrm(ks[18], (DEPTH, D_MODEL, D_MODEL), D_MODEL ** -0.5),
        'norm2_g': gain(ks[19], (DEPTH, D_MODEL)),
        'w_ff1': nrm(ks[20], (DEPTH, D_MODEL, D_FF), D_MODEL ** -0.5),
        'w_ff2': nrm(ks[21], (DEPTH, D_FF, D_MODEL), D_FF ** -0.5),
    }

def first_block(x, norm1_g, w_in, dsa_q_norm, dsa_k_norm, nsa_q_norm, nsa_k_norm, nsa_cmp_pos, nsa_cmp_w,
              ssd_conv_w, ssd_conv_b, ssd_dt_bias, ssd_a_log, ssd_d, ssd_norm_g,
              w_br_dsa, w_br_nsa, w_br_ssd, w_out, norm2_g, w_ff1, w_ff2):
    bsz, seq = x.shape[:2]
    offsets = [int(o) for o in np.cumsum(IN_SPLITS)[:-1]]
    for l in range(DEPTH):
        h = rms_norm(x, norm1_g[l])
        u = h @ w_in[l]
        (dq, dk, dv, iq, ik, iw, nq, nkv, ng, sz, sxbc, sdt, mg) = jnp.split(u, offsets, axis=-1)
        y_a = dsa_mixer(rms_norm(dq.reshape(bsz, seq, DSA_HEADS, HEAD_DIM), dsa_q_norm[l]),
                        rms_norm(dk, dsa_k_norm[l]), dv,
                        iq.reshape(bsz, seq, IDX_HEADS, IDX_DIM), ik, iw)
        y_a = y_a.reshape(bsz, seq, DSA_HEADS * HEAD_DIM)
        nkv = nkv.reshape(bsz, seq, 6, NSA_KV_HEADS, HEAD_DIM)
        y_b = nsa_mixer(rms_norm(nq.reshape(bsz, seq, NSA_KV_HEADS, NSA_GROUP, HEAD_DIM), nsa_q_norm[l]),
                        nkv[:, :, 0], nkv[:, :, 1], nkv[:, :, 2], nkv[:, :, 3], nkv[:, :, 4], nkv[:, :, 5],
                        jax.nn.sigmoid(ng.reshape(bsz, seq, NSA_KV_HEADS, NSA_GROUP, 3)),
                        nsa_k_norm[l], nsa_cmp_pos[l], nsa_cmp_w[l])
        y_b = y_b.reshape(bsz, seq, NSA_HEADS * HEAD_DIM)
        y_c = ssd_mixer(sz, sxbc, sdt, ssd_conv_w[l], ssd_conv_b[l], ssd_dt_bias[l], ssd_a_log[l],
                        ssd_d[l], ssd_norm_g[l])
        gates = jax.nn.sigmoid(mg.reshape(bsz, seq, 3, D_MODEL))
        mix = (gates[:, :, 0] * (y_a @ w_br_dsa[l]) + gates[:, :, 1] * (y_b @ w_br_nsa[l])
               + gates[:, :, 2] * (y_c @ w_br_ssd[l]))
        x = x + mix @ w_out[l]
        h = rms_norm(x, norm2_g[l])
        x = x + jnp.square(jax.nn.relu(h @ w_ff1[l])) @ w_ff2[l]
    return x


DEPTH_2 = 2

EPS_RMS = 1e-6
EPS_LN = 1e-5
W_CONV = D_MODEL
CONV_K = 31
W_POOL = D_MODEL
POOL_WINDOWS = (2, 4, 8, 16)
POOL_GROUPS = len(POOL_WINDOWS)
POOL_GW = W_POOL // POOL_GROUPS
W_EVEN_IN = 3 * W_CONV + 2 * W_POOL
W_EVEN_MIX = W_CONV + W_POOL
LRU_HEADS = 12
LRU_HD = 128
W_LRU = LRU_HEADS * LRU_HD
LRU_CONV_K = 4
LRU_C = 8.0
N_EVEN = (DEPTH_2 + 1) // 2
N_ODD = DEPTH_2 // 2


def rmsnorm(x, g):
    xf = x.astype(jnp.float32)
    y = xf * lax.rsqrt(jnp.mean(xf * xf, axis=-1, keepdims=True) + EPS_RMS)
    return (y * g.astype(jnp.float32)).astype(x.dtype)

def layernorm(x, g, b):
    xf = x.astype(jnp.float32)
    mu = jnp.mean(xf, axis=-1, keepdims=True)
    var = jnp.mean(jnp.square(xf - mu), axis=-1, keepdims=True)
    y = (xf - mu) * lax.rsqrt(var + EPS_LN)
    return (y * g.astype(jnp.float32) + b.astype(jnp.float32)).astype(x.dtype)

def causal_depthwise_conv(x, w, b):
    k = w.shape[0]
    y = lax.conv_general_dilated(
        x, w[:, None, :].astype(x.dtype), window_strides=(1,), padding=[(k - 1, 0)],
        dimension_numbers=("NWC", "WIO", "NWC"), feature_group_count=x.shape[-1])
    return y + b.astype(x.dtype)

def multiscale_pool_diff(v):
    bsz, t, _ = v.shape
    vf = v.astype(jnp.float32)
    cs_pad = jnp.pad(jnp.cumsum(vf, axis=1), ((0, 0), (1, 0), (0, 0)))
    pos = jnp.arange(1, t + 1, dtype=jnp.float32)
    outs = []
    for g, w in enumerate(POOL_WINDOWS):
        seg = cs_pad[:, :, g * POOL_GW:(g + 1) * POOL_GW]
        upper = seg[:, 1:]
        lower = jnp.pad(seg[:, :t - w + 1], ((0, 0), (w - 1, 0), (0, 0)))
        cnt = jnp.minimum(pos, jnp.float32(w))[None, :, None]
        outs.append((upper - lower) / cnt)
    return jnp.concatenate(outs, axis=-1) - vf

def even_mixer(h, w_in, conv_w, conv_b, ln_g, ln_b, pool_w, pool_b, pool_scale, w_out):
    bsz, t, _ = h.shape
    p = jnp.einsum("btd,dn->btn", h, w_in)
    a_val, a_glu, a_gate, b_val, b_gate = jnp.split(
        p, [W_CONV, 2 * W_CONV, 3 * W_CONV, 3 * W_CONV + W_POOL], axis=-1)
    u = a_val * jax.nn.sigmoid(a_glu)
    u = causal_depthwise_conv(u, conv_w, conv_b)
    u = jax.nn.silu(layernorm(u, ln_g, ln_b))
    ya = u * jax.nn.silu(a_gate)
    d = multiscale_pool_diff(b_val).reshape(bsz, t, POOL_GROUPS, POOL_GW)
    d = jnp.einsum("btgc,gce->btge", d, pool_w.astype(jnp.float32)) + pool_b.astype(jnp.float32)
    yb = (d.reshape(bsz, t, W_POOL) * pool_scale.astype(jnp.float32)).astype(h.dtype)
    yb = yb * jax.nn.silu(b_gate)
    y = jnp.concatenate([ya, yb], axis=-1)
    return jnp.einsum("btn,nd->btd", y, w_out)

def _lin_combine(c1, c2):
    a1, b1 = c1
    a2, b2 = c2
    return a1 * a2, a2 * b1 + b2

def odd_mixer(h, w_in, conv_w, conv_b, w_rg, b_rg, w_ig, b_ig, lam, w_out):
    bsz, t, _ = h.shape
    p = jnp.einsum("btd,dn->btn", h, w_in)
    xr, gate = jnp.split(p, [W_LRU], axis=-1)
    xc = causal_depthwise_conv(xr, conv_w, conv_b)
    xh = xc.reshape(bsz, t, LRU_HEADS, LRU_HD)
    r = jax.nn.sigmoid(jnp.einsum("bthi,hij->bthj", xh, w_rg).reshape(bsz, t, W_LRU).astype(jnp.float32)
                       + b_rg.astype(jnp.float32))
    i = jax.nn.sigmoid(jnp.einsum("bthi,hij->bthj", xh, w_ig).reshape(bsz, t, W_LRU).astype(jnp.float32)
                       + b_ig.astype(jnp.float32))
    log_a = -LRU_C * r * jax.nn.softplus(-lam.astype(jnp.float32))
    a = jnp.exp(log_a)
    mult = jnp.sqrt(-jnp.expm1(2.0 * log_a))
    bterm = mult * (i * xc.astype(jnp.float32))
    _, hs = lax.associative_scan(_lin_combine, (a, bterm), axis=1)
    y = hs.astype(h.dtype) * jax.nn.silu(gate)
    return jnp.einsum("btn,nd->btd", y, w_out)

def second_inputs(seed: int = 0) -> dict:
    key = jax.random.key(seed)
    ks = iter(jax.random.split(key, 32))
    f32 = jnp.float32

    def nrm(shape, scale):
        return jax.random.normal(next(ks), shape, f32) * scale

    x = jax.random.normal(next(ks), (BATCH, SEQ, D_MODEL), f32)
    a0 = jax.random.uniform(next(ks), (N_ODD, W_LRU), f32, 0.9, 0.999)
    s = a0 ** (1.0 / LRU_C)
    lru_lambda = jnp.log(s) - jnp.log1p(-s)
    return {
        "x": x,
        "norm_even": 1.0 + nrm((N_EVEN, D_MODEL), 0.02),
        "w_in_even": nrm((N_EVEN, D_MODEL, W_EVEN_IN), D_MODEL ** -0.5),
        "conv_a_w": nrm((N_EVEN, CONV_K, W_CONV), CONV_K ** -0.5),
        "conv_a_b": nrm((N_EVEN, W_CONV), 0.01),
        "ln_a_g": 1.0 + nrm((N_EVEN, W_CONV), 0.02),
        "ln_a_b": nrm((N_EVEN, W_CONV), 0.01),
        "pool_w": nrm((N_EVEN, POOL_GROUPS, POOL_GW, POOL_GW), POOL_GW ** -0.5),
        "pool_b": nrm((N_EVEN, POOL_GROUPS, POOL_GW), 0.01),
        "pool_scale": 1.0 + nrm((N_EVEN, W_POOL), 0.1),
        "w_out_even": nrm((N_EVEN, W_EVEN_MIX, D_MODEL), W_EVEN_MIX ** -0.5),
        "norm_odd": 1.0 + nrm((N_ODD, D_MODEL), 0.02),
        "w_in_odd": nrm((N_ODD, D_MODEL, 2 * W_LRU), D_MODEL ** -0.5),
        "conv_c_w": nrm((N_ODD, LRU_CONV_K, W_LRU), LRU_CONV_K ** -0.5),
        "conv_c_b": nrm((N_ODD, W_LRU), 0.01),
        "w_rg": nrm((N_ODD, LRU_HEADS, LRU_HD, LRU_HD), LRU_HD ** -0.5),
        "b_rg": nrm((N_ODD, W_LRU), 0.01),
        "w_ig": nrm((N_ODD, LRU_HEADS, LRU_HD, LRU_HD), LRU_HD ** -0.5),
        "b_ig": nrm((N_ODD, W_LRU), 0.01),
        "lru_lambda": lru_lambda,
        "w_out_odd": nrm((N_ODD, W_LRU, D_MODEL), W_LRU ** -0.5),
        "final_norm": 1.0 + nrm((D_MODEL,), 0.02),
    }

def second_block(x, norm_even, w_in_even, conv_a_w, conv_a_b, ln_a_g, ln_a_b, pool_w, pool_b,
              pool_scale, w_out_even, norm_odd, w_in_odd, conv_c_w, conv_c_b, w_rg, b_rg,
              w_ig, b_ig, lru_lambda, w_out_odd, final_norm):
    h = x
    for layer in range(DEPTH_2):
        if layer % 2 == 0:
            j = layer // 2
            h = h + even_mixer(rmsnorm(h, norm_even[j]), w_in_even[j], conv_a_w[j], conv_a_b[j],
                               ln_a_g[j], ln_a_b[j], pool_w[j], pool_b[j], pool_scale[j],
                               w_out_even[j])
        else:
            j = layer // 2
            h = h + odd_mixer(rmsnorm(h, norm_odd[j]), w_in_odd[j], conv_c_w[j], conv_c_b[j],
                              w_rg[j], b_rg[j], w_ig[j], b_ig[j], lru_lambda[j], w_out_odd[j])
    return rmsnorm(h, final_norm)


def setup_inputs(seed=0):
    out = dict(first_inputs(seed))
    for name, value in second_inputs(seed + 1).items():
        if name != "x":
            out[name + "_2"] = value
    return out


def reference(
    x, norm1_g, w_in, dsa_q_norm, dsa_k_norm, nsa_q_norm, nsa_k_norm, nsa_cmp_pos, nsa_cmp_w,
    ssd_conv_w, ssd_conv_b, ssd_dt_bias, ssd_a_log, ssd_d, ssd_norm_g, w_br_dsa, w_br_nsa,
    w_br_ssd, w_out, norm2_g, w_ff1, w_ff2, norm_even_2, w_in_even_2, conv_a_w_2, conv_a_b_2,
    ln_a_g_2, ln_a_b_2, pool_w_2, pool_b_2, pool_scale_2, w_out_even_2, norm_odd_2, w_in_odd_2,
    conv_c_w_2, conv_c_b_2, w_rg_2, b_rg_2, w_ig_2, b_ig_2, lru_lambda_2, w_out_odd_2,
    final_norm_2,
):
    x = first_block(
        x, norm1_g, w_in, dsa_q_norm, dsa_k_norm, nsa_q_norm, nsa_k_norm, nsa_cmp_pos,
        nsa_cmp_w, ssd_conv_w, ssd_conv_b, ssd_dt_bias, ssd_a_log, ssd_d, ssd_norm_g, w_br_dsa,
        w_br_nsa, w_br_ssd, w_out, norm2_g, w_ff1, w_ff2,
    )
    return second_block(
        x, norm_even_2, w_in_even_2, conv_a_w_2, conv_a_b_2, ln_a_g_2, ln_a_b_2, pool_w_2,
        pool_b_2, pool_scale_2, w_out_even_2, norm_odd_2, w_in_odd_2, conv_c_w_2, conv_c_b_2,
        w_rg_2, b_rg_2, w_ig_2, b_ig_2, lru_lambda_2, w_out_odd_2, final_norm_2,
    )


_drawn_inputs = setup_inputs


def setup_inputs(seed=0):
    import zlib

    import numpy as np

    out = dict(_drawn_inputs(seed))
    spreads = {}
    factors = {'dsa_q_norm': 8.0,
     'dsa_k_norm': 8.0,
     'nsa_q_norm': 8.0,
     'nsa_k_norm': 8.0,
     'nsa_cmp_pos': 8.0,
     'ssd_conv_b': 3.809,
     'ssd_d': 6.833,
     'ssd_norm_g': 5.202,
     'norm2_g': 3.207,
     'norm_even_2': 7.798,
     'conv_a_b_2': 61.642,
     'ln_a_g_2': 64.0,
     'ln_a_b_2': 64.0,
     'pool_b_2': 31.372,
     'pool_scale_2': 2.826,
     'norm_odd_2': 39.04,
     'conv_c_b_2': 36.08,
     'b_rg_2': 195.674,
     'b_ig_2': 64.0,
     'final_norm_2': 23.088}
    for name, (base, spread) in spreads.items():
        noise = np.random.default_rng([zlib.crc32(name.encode()), seed]).standard_normal(out[name].shape)
        drawn = base * np.exp(spread * noise) if base else spread * noise
        out[name] = jnp.asarray(drawn.astype(out[name].dtype))
    for name, factor in factors.items():
        out[name] = (out[name] * factor).astype(out[name].dtype)
    return out
```

```python
from contextlib import ExitStack

import concourse.bass as bass
from concourse import mybir

F32 = mybir.dt.float32
ALU = mybir.AluOpType
ACT = mybir.ActivationFunctionType
AX = mybir.AxisListType

P = 128
S = 256
NT = S // P
D = 1024
KD = D // P
HD = 64
NEG = -1e30
MARK = -3e38
TOPK = 64
SCALE = HD ** -0.5
N_CMP = 15
SSD_H = 32
FFC = 4 * D // P
LRU_H = 12
CONV_K = 31
WINDOWS = (2, 4, 8, 16)
RING = 6
TOK = 408
TOK_IW, TOK_NG, TOK_DT, TOK_DV, TOK_VS, TOK_VW = 0, 8, 56, 88, 152, 280

COLUMNS = [("norm1", 8), ("dq_g", 1), ("dk_g", 1), ("nq_g", 1), ("nk_g", 3), ("cmp_pos", 64),
           ("ssd_cw", 96), ("ssd_cb", 24), ("ssd_d", 16), ("ssd_g", 16), ("norm2", 8),
           ("even_g", 8), ("even_cw", 248), ("even_cb", 8), ("ln_g", 8), ("ln_b", 8), ("pool_b", 8),
           ("pool_s", 8), ("odd_g", 8), ("odd_cw", 48), ("odd_cb", 12), ("b_rg", 12), ("b_ig", 12),
           ("lam", 12), ("final_g", 8)]
AT, _n = {}, 0
for _name, _w in COLUMNS:
    AT[_name] = _n
    _n += _w
NCOLS = _n

PHASES = [("iq", 2, 8), ("ik", 1, 8), ("dk", 1, 8), ("kc", 1, 8), ("vc", 1, 8), ("ks", 1, 8), ("kw", 1, 8),
          ("dq", 8, 8), ("nq", 8, 8), ("xbc", 24, 8), ("sz", 16, 8), ("mg", 24, 8),
          ("br_dsa", 8, 8), ("br_nsa", 8, 8), ("br_ssd", 8, 16), ("w_out", 8, 8),
          ("ff1", 32, 8), ("ff2", 8, 32), ("val_glu", 16, 8), ("b_val", 8, 8), ("b_gate", 8, 8),
          ("a_gate", 8, 8), ("pool", 8, 2), ("even_out", 8, 16), ("xr", 12, 8), ("gate", 12, 8),
          ("rg_ig", 24, 1), ("odd_out", 8, 12)]
ON_VECTOR = {"br_dsa", "br_nsa", "br_ssd", "w_out", "ff2", "pool", "even_out", "odd_out"}

XT, HT, DQ, NQ, SZ, XB, MG, XD, MISC = 0, 8, 16, 24, 32, 48, 72, 96, 112
KCP, DK, KC, VC, KS, KW = 32, 36, 37, 38, 39, 40
WTOK = 48
WCMP = 80
IQ, IKZ, RL, IDX = 112, 114, 118, 122
XW, HST = 112, 120
FF = 32
UB, AC, GA, GB, BV, DP, YA, YB, VA, TA, SQ = 16, 32, 40, 48, 56, 65, 73, 81, 89, 97, 105
XC, U2, TI, GG, LA, LY, R2, W1 = 16, 28, 40, 52, 64, 76, 88, 100
ARENA = 128


def schedule():
    out = []
    jobs = {name: [("job", name, i) for i in range(n)] for name, n, _ in PHASES}
    out += [("norm", 0), ("tok", 0), ("tok", 1), ("softplus",)]
    for name in ("iq", "ik", "dk", "kc", "vc", "ks", "kw"):
        out += jobs[name]
    out += [("acum",), ("cmp_in",), ("cmp_mm",)]
    norms = list(range(20))
    out += [("qsq", 0), ("qsq", 1), ("qap", 0), ("qsq", 2), ("qap", 1), ("qsq", 3), ("qap", 2)]
    idx = [("idx", i) for i in range(8)]
    big = jobs["dq"] + jobs["nq"]
    for n, job in enumerate(big):
        out.append(job)
        if n % 2 == 1:
            out.append(idx[n // 2])
        if n % 8 == 0 and n:
            out.append(("select", n // 8 - 1))
        if n >= 1:
            out.append(("qsq", n + 3))
            out.append(("qap", n + 2))
    out += [("qsq", 19), ("qap", 18), ("qap", 19), ("select", 1)]
    out += [("vcmp",), ("pcmp", 0), ("pcmp", 1)]
    soft = []
    for i in range(48 + 3):
        s = []
        if i < 48:
            s.append(("sA", i))
        if 1 <= i < 49:
            s.append(("sR", i - 1))
        if 2 <= i < 50:
            s.append(("sB", i - 2))
        if 3 <= i:
            s.append(("sC", i - 3))
        soft.append(s)
    prep = [[("xtr", i)] for i in range(8)] + [[("btr",)], [("cbt", 0)], [("cbt", 1)], [("st", 0)], [("st", 1)],
                                               [("st", 2)], [("st", 3)]]
    quads = []
    for i in range(16 + 2):
        s = []
        if i < 16:
            s.append(("uA", i))
        if i >= 2:
            s.append(("uB", i - 2))
        quads.append(s)
    filler = soft + prep + quads
    wide = jobs["xbc"] + jobs["sz"] + jobs["mg"] + jobs["br_dsa"] + jobs["br_nsa"]
    at = 0
    for n, job in enumerate(wide):
        if n == 24:
            out.append(("xsilu", 23))
        out.append(job)
        if job[1] == "xbc":
            out.append(("xconv", job[2]))
            if job[2] >= 1:
                out.append(("xsilu", job[2] - 1))
        want = (n + 1) * len(filler) // (len(wide) - 8)
        while at < min(want, len(filler)):
            out += filler[at]
            at += 1
    while at < len(filler):
        out += filler[at]
        at += 1
    out += [("ynorm",)] + jobs["br_ssd"] + jobs["w_out"]
    out += [("norm", 1)] + jobs["ff1"] + jobs["ff2"]
    out += [("norm", 2), ("pads",)]
    vg = jobs["val_glu"]
    for c in range(8):
        out += [vg[2 * c], vg[2 * c + 1]]
    for c in range(8):
        out += [jobs["b_val"][c], ("winsum", c)]
    out += jobs["b_gate"] + jobs["a_gate"] + [("econv", c) for c in range(8)] + jobs["pool"]
    out += [("ln",)] + jobs["even_out"]
    out += [("norm", 3)]
    for j in range(12):
        out += [jobs["xr"][j], ("oconv", j)]
    for j in range(12):
        out += [jobs["gate"][j], jobs["rg_ig"][2 * j], jobs["rg_ig"][2 * j + 1], ("lru", j)]
    out += [("scan",)] + jobs["odd_out"] + [("norm", 4), ("store",)]
    assert len(set(out)) == len(out)
    return out


def psum_tenants(steps):
    turns = {"proj": [], "score": [], "turn": [], "pv": [], "mean": []}
    where = {}

    def add(group, key, readers):
        where[key] = (group, len(turns[group]))
        turns[group].append(readers)

    for s in steps:
        k = s[0]
        if k == "job":
            add("proj", s, "D" if s[1] in ON_VECTOR else "A")
        elif k in ("tok", "cmp_mm", "idx", "cbt", "st"):
            add("score", s, "A")
        elif k in ("sA", "pcmp"):
            add("score", s, "D")
            if k == "pcmp":
                add("turn", ("pcmpT", s[1]), "A")
        elif k == "uA":
            add("score", s, "AD" if s[1] >= 8 else "D")
        elif k in ("vcmp", "sB", "btr"):
            add("turn", s, "A")
        elif k == "xtr":
            add("turn", s, "D")
        elif k == "sC" and (s[1] < 16 or s[1] % 2 == 1):
            add("pv", s, "A")
        elif k == "uB":
            add("pv", s, "D")
        elif k in ("norm", "qsq", "acum", "ynorm"):
            add("mean", s, "A")
        elif k == "ln":
            add("mean", ("ln", 0), "A")
            add("mean", ("ln", 1), "A")
    return where, turns


def program(nc, x_t, w_stream, w_tok, w_cmp, cols, rows, out):
    steps = schedule()
    where, turns = psum_tenants(steps)
    slots = {"proj": 3, "score": 2, "turn": 1, "pv": 1, "mean": 1}

    blocks, first = {}, {}
    at = 0
    order = [s for s in steps if s[0] == "job"]
    for s in order:
        n = next(k for name, _, k in PHASES if name == s[1])
        first[s], blocks[s] = at, n
        at += n
    n_units = at // 8
    assert at % 8 == 0 and w_stream.shape[0] == n_units
    milestone, used, filled_at = 0, {}, {}
    for s in order:
        for b in range(first[s], first[s] + blocks[s]):
            if b % 8 == 7 or b == first[s] + blocks[s] - 1:
                milestone += 1
            if b % 8 == 7:
                used[b // 8] = milestone
        filled_at[s] = milestone

    with ExitStack() as ctx:
        def sb(name, shape):
            return ctx.enter_context(nc.sbuf_tensor(name, shape, F32))

        def psum(name, shape):
            return ctx.enter_context(nc.psum_tensor(name, shape, F32))

        sems = {}

        def sem(name):
            if name not in sems:
                sems[name] = ctx.enter_context(nc.semaphore(name))
            return sems[name]

        arena = sb("arena", [P, ARENA, S])
        ring = sb("ring", [P, RING, 8, P])
        par = sb("par", [P, NCOLS])
        row = sb("row", [P, 2 * SSD_H])
        tok = sb("tok", [P, NT, TOK])
        sbuf_s = sb("sbuf_s", [P, 4, 512])
        sbuf_t = sb("sbuf_t", [P, 2, 512])
        raw = sb("raw", [P, 3, 3 + S])
        th = sb("th", [P, 3, S])
        sqb = sb("sqb", [P, 2, S])
        root = sb("root", [P, 2, S])
        rinv = sb("rinv", [P, S])
        kk_d = sb("kk_d", [P, 2, S])
        kk_s = sb("kk_s", [P, 2, 2, S])
        kk_w = sb("kk_w", [P, 2, 2, S])
        kk_c = sb("kk_c", [P, 2, 2, N_CMP])
        kcr = sb("kcr", [P, 2, 16])
        vcl = sb("vcl", [P, 4, P])
        pc = sbuf_t[:, 1, :].rearrange("p (h n) -> p h n", n=32)
        ec = sbuf_t[:, 0, 0:256].rearrange("p (h n) -> p h n", n=16)
        pct = sb("pct", [P, NT, 512])
        bmt = kk_d[:, :, :].rearrange("p a s -> p (a s)").rearrange("p (g n) -> p g n", g=4)
        cbt = kk_s[:, :, :, :].rearrange("p t a s -> p t (a s)")
        caus = sb("caus", [P, NT, S])
        jneg = sb("jneg", [P, P])
        dmask = arena[:, IDX + 2:IDX + 4, :]
        ident = sb("ident", [P, P])
        ones = sb("ones", [P, P])
        mean_d = sb("mean_d", [P, P])
        mean_i = sb("mean_i", [P, P])
        mean_h = sb("mean_h", [P, P])
        upper = sb("upper", [P, P])
        cneg = sb("cneg", [P, NT, 16])
        cvis = sb("cvis", [P, NT, 16])
        icnt = sb("icnt", [P, 4, 16])
        small = sb("small", [P, 64])
        gates = sb("gates", [P, NT, 48])
        sp = sb("sp", [P, 6, 76])
        dta = sb("dta", [P, 64])
        ea = sb("ea", [P, 32])
        ac = sb("ac", [P, 96])
        dec = sb("dec", [P, 32])
        half = sb("half", [P, 160])
        m8 = sb("m8", [P, 8])
        srow = sb("srow", [P, 4, 8])
        crow = sb("crow", [P, 3, 16])
        ytmp = pct[:, 0, 0:2 * P].rearrange("p (c i) -> p c i", c=2)
        wtmp = kk_w[:, :, :, :].rearrange("p a b s -> p a (b s)")[:, :, 0:272]

        bank = {"proj": [psum(f"p_proj{i}", [P, 512]) for i in range(3)],
                "score": [psum(f"p_score{i}", [P, 512]) for i in range(2)],
                "turn": [psum("p_turn", [P, 512])]}
        bank["pv"] = [psum("p_pv", [P, 512])]
        bank["mean"] = [psum("p_mean", [P, 512])]

        filled = {g: sem(f"{g}_filled") for g in turns}
        read = {(g, e): sem(f"{g}_read_{'act' if e == 'A' else 'dve'}") for g in turns for e in "AD"}
        w_in = [sem(f"w_in{i}") for i in range(RING)]

        def A(c, n=1):
            return arena[:, c, :] if n == 1 else arena[:, c:c + n, :]

        def flat(c, n):
            return arena[:, c:c + n, :].rearrange("p c s -> p (c s)")

        wtok = flat(WTOK, 13)[:, 0:8 * TOK].rearrange("p (k n) -> p k n", k=8)
        wcmp = flat(WCMP, 32).rearrange("p (v l e) -> p v l e", v=2, l=32)
        kcp = flat(KCP, 4)[:, 0:2 * 32 * N_CMP].rearrange("p (v l n) -> p v l n", v=2, l=32)
        ikz = arena[:, IKZ:IKZ + 4, :]
        xd = [flat(XD + 8 * t, 8) for t in range(NT)]
        xw, hst = flat(XW, 8), flat(HST, 8)
        ub = flat(UB, 9)[:, 0:8 * (S + 30)].rearrange("p (c s) -> p c s", c=8)
        bv = flat(BV, 9)[:, 0:8 * (S + 16)].rearrange("p (c s) -> p c s", c=8)

        def col(name, i=0):
            return par[:, AT[name] + i:AT[name] + i + 1]

        def slot(key):
            g, n = where[key]
            return bank[g][n % slots[g]][:, 0:256 if g == "mean" else 512]

        def turn(key):
            return where[key][1]

        def readers_done(eng, key):
            g, n = where[key]
            prev = n - slots[g]
            if prev >= 0:
                for e in turns[g][prev]:
                    eng.wait_ge(read[g, e], sum(e in r for r in turns[g][:prev + 1]))

        def was_read(eng, key, reader="A"):
            g, n = where[key]
            eng.wait_ge(read[g, reader], sum(reader in r for r in turns[g][:n + 1]))

        qn = [(A(DK), S, "dk_g", 0), (A(KS), S, "nk_g", 1), (A(KW), S, "nk_g", 2),
              (kcr[:, 0, 0:N_CMP], N_CMP, "nk_g", 0)]
        qn += [(A(DQ + c), S, "dq_g", 0) for c in range(8)] + [(A(NQ + c), S, "nq_g", 0) for c in range(8)]

        def soft(i):
            if i < 16:
                return i // 8, i % 8, kk_d[:, :, :], DQ, dmask, TOK_DV, None
            u, kind = (i - 16) // 2, (i - 16) % 2
            t, c = u // 8, u % 8
            g = c // 4
            kk = (kk_w if kind else kk_s)[:, g, :, :]
            return t, c, kk, NQ, caus, (TOK_VW if kind else TOK_VS) + 64 * g, kind + 1

        CONSTS, ZEROS = 6 + 4 * 16, 24

        block = ctx.enter_context(nc.Block())

        @block.sync
        def _(sp_eng):
            sp_eng.dma_start(arena[:, XT:XT + 8, :], x_t).then_inc(sem("x_in"), 16)
            sp_eng.dma_start(par[:, :], cols).then_inc(sem("par_in"), 16)
            sp_eng.dma_start(wtok, w_tok).then_inc(sem("wtok_in"), 16)
            for u in range(n_units):
                if u >= RING:
                    sp_eng.wait_ge(filled["proj"], used[u - RING])
                sp_eng.dma_start(ring[:, u % RING, :, :].rearrange("p k n -> p (k n)"),
                                 w_stream[u]).then_inc(w_in[u % RING], 16)
            sp_eng.wait_ge(sem("h_ready"), 40)
            sp_eng.dma_start(out, arena[:, HT:HT + 8, :]).then_inc(sem("stored"), 16)
            sp_eng.wait_ge(sem("stored"), 16)

        @block.gpsimd
        def _(pool):
            consts = sem("consts")
            counts, last = {}, []

            def note(semaphore):
                n = str(semaphore.name)
                counts[n] = counts.get(n, 0) + 1
                last[:] = [semaphore, counts[n]]

            def settle():
                if last:
                    pool.wait_ge(*last)

            def link(ins):
                ins.then_inc(sem("pool_chain"), 1)
                note(sem("pool_chain"))
                settle()

            n = [0]

            def const(ins):
                ins.then_inc(consts, 1)
                note(consts)
                n[0] += 1

            pool.wait_ge(sem("zeros"), ZEROS)
            const(pool.affine_select(out=upper[:, :], in_=ones[:, :], compare_op=ALU.is_ge, fill=0.0,
                                     base=0, pattern=[[1, P]], channel_multiplier=-1))
            const(pool.affine_select(out=ident[:, :], in_=ident[:, :], compare_op=ALU.not_equal, fill=1.0,
                                     base=0, pattern=[[-1, P]], channel_multiplier=1))
            const(pool.affine_select(out=caus[:, :, :], in_=caus[:, :, :], compare_op=ALU.is_ge, fill=NEG,
                                     base=0, pattern=[[P, NT], [-1, S]], channel_multiplier=1))
            const(pool.affine_select(out=jneg[:, :], in_=jneg[:, :], compare_op=ALU.is_ge, fill=NEG,
                                     base=0, pattern=[[1, P]], channel_multiplier=-1))
            const(pool.affine_select(out=cneg[:, :, :], in_=cneg[:, :, :], compare_op=ALU.is_ge, fill=NEG,
                                     base=-31, pattern=[[P, NT], [-16, 16]], channel_multiplier=1))
            const(pool.affine_select(out=cvis[:, :, :], in_=cvis[:, :, :], compare_op=ALU.is_ge, fill=0.0,
                                     base=-31, pattern=[[P, NT], [-16, 16]], channel_multiplier=1))
            for g, w in enumerate(WINDOWS):
                for k in range(16):
                    ins = pool.memset(icnt[:, g, k:k + 1], 1.0 / min(k + 1, w))
                    const(ins)
            assert n[0] == CONSTS, n[0]

            for s in steps:
                k = s[0]
                settle()
                if k == "sR":
                    i = s[1]
                    t, c, kk, q, mask, v, gate = soft(i)
                    kl = P * (t + 1)
                    p = sbuf_s[:, i % 4, :].rearrange("p (h k) -> p h k", h=2)[:, :, 0:kl]
                    pool.wait_ge(sem("scale_ready"), i + 1)
                    r = srow[:, i % 4, 6:8]
                    pool.tensor_tensor(p, p, r.unsqueeze(2).to_broadcast([P, 2, kl]), ALU.mult)\
                        .then_inc(sem("p_ready"), 1); note(sem("p_ready"))
                elif k == "xtr" and s[1] < 4:
                    i = s[1]
                    was_read(pool, s, "D")
                    pool.wait_ge(sem("dec_ready"), 1)
                    if i == 0:
                        pool.wait_ge(sem("select_done"), 2)
                    pool.tensor_tensor(
                        xw[:, 512 * i:512 * i + 512].rearrange("p (h e) -> p h e", h=8),
                        xd[0][:, 512 * i:512 * i + 512].rearrange("p (h e) -> p h e", h=8),
                        dec[:, 8 * i:8 * i + 8].unsqueeze(2).to_broadcast([P, 8, 64]), ALU.mult)\
                        .then_inc(sem("xw_ready"), 1); note(sem("xw_ready"))
                elif k == "uA":
                    i = s[1]
                    t, hq = i // 8, i % 8
                    g = hq // 2
                    l = sbuf_s[:, i % 4, :].rearrange("p (h i) -> p h i", h=4)
                    pool.wait_ge(sem("l_ready"), i + 1)
                    if t == 1:
                        e = sbuf_t[:, i % 2, :].rearrange("p (h i) -> p h i", h=4)
                        link(pool.tensor_tensor(e, e, A(XB + 20 + g)[:, P:S].unsqueeze(1).to_broadcast([P, 4, P]),
                                                ALU.mult))
                    if i == 0:
                        was_read(pool, ("cbt", 1))
                    pool.tensor_tensor(
                        l, l, cbt[:, t, P * g:P * g + P].unsqueeze(1).to_broadcast([P, 4, P]),
                        ALU.mult).then_inc(sem("m_ready"), 1); note(sem("m_ready"))
                elif k == "job" and s[1] == "mg":
                    j = s[2]
                    was_read(pool, s)
                    pool.tensor_scalar(A(MG + j), A(MG + j), 0.5, 0.5, ALU.mult, ALU.add)\
                        .then_inc(sem("mg_ready"), 1); note(sem("mg_ready"))
                elif k == "job" and s[1] == "ff1":
                    j = s[2]
                    was_read(pool, s)
                    pool.tensor_tensor(A(FF + j), A(FF + j), A(FF + j), ALU.mult).then_inc(sem("ff_ready"), 1); note(sem("ff_ready"))
                elif k == "pads":
                    pool.wait_ge(sem("h_ready"), 17)
                    pool.memset(ub[:, :, 0:30], 0.0).then_inc(sem("pads_ready"), 1); note(sem("pads_ready"))
                    pool.memset(bv[:, :, 0:16], 0.0).then_inc(sem("pads_ready"), 1); note(sem("pads_ready"))
                elif k == "winsum":
                    c = s[1]
                    g, w = c // 2, WINDOWS[c // 2]
                    was_read(pool, ("job", "b_val", c))
                    if c == 0:
                        pool.wait_ge(sem("pads_ready"), 2)
                    src, reach, flip = bv[:, c, :], 1, 0
                    while reach < w:
                        dst = wtmp[:, flip, :]
                        lo = 2 * reach - 1
                        link(pool.tensor_tensor(dst[:, lo:272], src[:, lo:272], src[:, lo - reach:272 - reach],
                                                ALU.add))
                        src, reach, flip = dst, 2 * reach, 1 - flip
                    link(pool.tensor_tensor(wtmp[:, flip, 16:32], src[:, 16:32], icnt[:, g, :], ALU.mult))
                    link(pool.tensor_scalar(wtmp[:, flip, 32:272], src[:, 32:272], 1.0 / w, 1.0, ALU.mult, ALU.mult))
                    pool.tensor_tensor(A(DP + c), wtmp[:, flip, 16:272], bv[:, c, 16:272], ALU.subtract)\
                        .then_inc(sem("dp_ready"), 1); note(sem("dp_ready"))
                    pool.wait_ge(sem("dp_ready"), c + 1)

        @block.scalar
        def _(act):
            act.dma_start(row[:, :], rows).then_inc(sem("row_in"), 16)
            act.dma_start(wcmp[0:64, :, :, 0:64], w_cmp).then_inc(sem("wcmp_in"), 16)
            act.dma_start(wcmp[64:128, :, :, 64:128], w_cmp).then_inc(sem("wcmp_in"), 16)
            counts, last = {}, []

            def note(semaphore):
                n = str(semaphore.name)
                counts[n] = counts.get(n, 0) + 1
                last[:] = [semaphore, counts[n]]

            def settle():
                if last:
                    act.wait_ge(*last)

            def link(ins):
                ins.then_inc(sem("act_chain"), 1)
                note(sem("act_chain"))
                settle()

            def take(key):
                act.wait_ge(filled[where[key][0]], turn(key) + 1)
                return slot(key)

            act.wait_ge(sem("zeros"), ZEROS)
            ths = [0]
            for s in steps:
                k = s[0]
                settle()
                if k == "norm":
                    ps = take(s)
                    act.activation(root[:, 0, :], ps, ACT.Sqrt, bias=small[:, 0:1]).then_inc(read["mean", "A"], 1); note(read["mean", "A"])
                elif k == "tok":
                    ps = take(s)
                    act.activation(tok[:, s[1], :], ps[:, 0:TOK], ACT.Copy).then_inc(read["score", "A"], 1); note(read["score", "A"])
                elif k == "softplus":
                    act.wait_ge(read["score", "A"], 2)
                    act.activation(gates[:, :, :], tok[:, :, TOK_NG:TOK_NG + 48], ACT.Tanh, scale=0.5)\
                        .then_inc(sem("gate_tanh"), 1); note(sem("gate_tanh"))
                    act.wait_ge(sem("row_in"), 16)
                    act.activation(ea[:, :], row[:, 32:64], ACT.Exp).then_inc(sem("ea_ready"), 1); note(sem("ea_ready"))
                    act.wait_ge(sem("abs_ready"), 1)
                    act.activation(sp[:, 1, :], sp[:, 1, :], ACT.Exp, scale=-1.0).then_inc(sem("expabs_ready"), 1); note(sem("expabs_ready"))
                elif k == "acum":
                    ps = take(s)
                    act.activation(ac[:, :], ps[:, 0:96], ACT.Copy).then_inc(read["mean", "A"], 1); note(read["mean", "A"])
                    act.wait_ge(sem("decarg_ready"), 1)
                    act.activation(dec[:, :], dec[:, :], ACT.Exp).then_inc(sem("dec_ready"), 1); note(sem("dec_ready"))
                elif k == "cmp_mm":
                    ps = take(s)
                    act.activation(kcr[:, 0, 0:N_CMP], ps[:, 0:N_CMP], ACT.Copy)
                    act.activation(kcr[:, 1, 0:N_CMP], ps[:, 256:256 + N_CMP], ACT.Copy)\
                        .then_inc(read["score", "A"], 1); note(read["score", "A"])
                elif k == "qsq":
                    i = s[1]
                    ps = take(s)
                    act.activation(root[:, i % 2, 0:qn[i][1]], ps[:, 0:qn[i][1]], ACT.Sqrt, bias=small[:, 0:1])\
                        .then_inc(read["mean", "A"], 1); note(read["mean", "A"])
                elif k == "idx":
                    i = s[1]
                    kl = P * (i // 4 + 1)
                    ps = take(s).rearrange("p (h k) -> p h k", h=2)[:, :, 0:kl]
                    if i >= 2:
                        act.wait_ge(sem("rl_used"), i - 1)
                    act.activation(arena[:, RL + 2 * (i % 2):RL + 2 * (i % 2) + 2, 0:kl], ps, ACT.Relu)\
                        .then_inc(read["score", "A"], 1); note(read["score", "A"])
                elif k == "vcmp":
                    ps = take(s)
                    for b in range(2):
                        for g in range(2):
                            for h in range(2):
                                r = 32 * (2 * b + h)
                                ins = act.activation(vcl[r:r + N_CMP, 2 * b + g, 64 * h:64 * h + 64],
                                                     ps[0:N_CMP, 64 * g:64 * g + 64], ACT.Copy)
                    ins.then_inc(read["turn", "A"], 1); note(read["turn", "A"])
                elif k == "pcmp":
                    t = s[1]
                    act.wait_ge(sem("carg_ready"), t + 1)
                    act.activation(ec[:, :, 0:N_CMP], ec[:, :, 0:N_CMP], ACT.Exp, scale=SCALE)\
                        .then_inc(sem("ce_ready"), 1); note(sem("ce_ready"))
                    ps = take(("pcmpT", t))
                    act.activation(pct[:, t, :], ps, ACT.Copy).then_inc(read["turn", "A"], 1); note(read["turn", "A"])
                elif k == "sA":
                    i = s[1]
                    t = soft(i)[0]
                    kl = P * (t + 1)
                    act.wait_ge(sem("nmax_ready"), i + 1)
                    for h in range(2):
                        p = sbuf_s[:, i % 4, 256 * h:256 * h + kl]
                        ins = act.activation(p, p, ACT.Exp, bias=srow[:, i % 4, 2 + h:3 + h], scale=SCALE,
                                             accum_out=srow[:, i % 4, 4 + h:5 + h])
                    ins.then_inc(sem("e_ready"), 1); note(sem("e_ready"))
                elif k == "sB":
                    i = s[1]
                    t = soft(i)[0]
                    ps = take(s)
                    if i >= 2:
                        act.wait_ge(sem("pv_done"), i - 1)
                    act.activation(sbuf_t[:, i % 2, 0:256 * (t + 1)], ps[:, 0:256 * (t + 1)], ACT.Copy)\
                        .then_inc(read["turn", "A"], 1); note(read["turn", "A"])
                elif k == "sC" and s in where:
                    i = s[1]
                    t, c, _, q, _, _, _ = soft(i)
                    act.wait_ge(sem("pv_done"), i + 1)
                    act.activation(A(q + c)[:, P * t:P * t + P], slot(s)[:, 0:P], ACT.Copy)\
                        .then_inc(read["pv", "A"], 1); note(read["pv", "A"])
                elif k == "xsilu":
                    j = s[1]
                    act.wait_ge(sem("conv_done"), j + 1)
                    if j >= 3:
                        act.wait_ge(sem("silu_done"), j - 2)
                    act.activation(th[:, j % 3, :], A(XB + j), ACT.Tanh).then_inc(sem("xtanh"), 1); note(sem("xtanh"))
                elif k == "btr":
                    ps = take(s)
                    act.activation(bmt[:, :, :].rearrange("p g n -> p (g n)"), ps, ACT.Copy)\
                        .then_inc(read["turn", "A"], 1); note(read["turn", "A"])
                elif k == "cbt":
                    ps = take(s)
                    act.activation(cbt[:, s[1], :], ps, ACT.Copy).then_inc(read["score", "A"], 1); note(read["score", "A"])
                elif k == "st":
                    g = s[1]
                    ps = take(s)
                    act.activation(hst[:, 512 * g:512 * g + 512], ps, ACT.Copy).then_inc(read["score", "A"], 1); note(read["score", "A"])
                elif k == "uA":
                    i = s[1]
                    if i >= 8:
                        ps = take(s)
                        was_read(act, s, "D")
                        if i == 8:
                            act.wait_ge(sem("pv_done"), 48)
                        elif i >= 10:
                            act.wait_ge(sem("pv_done"), 48 + i - 1)
                        act.activation(sbuf_t[:, i % 2, :], ps, ACT.Exp).then_inc(read["score", "A"], 1); note(read["score", "A"])
                    act.wait_ge(sem("seg_ready"), i + 1)
                    l = sbuf_s[:, i % 4, :]
                    act.activation(l, l, ACT.Exp).then_inc(sem("l_ready"), 1); note(sem("l_ready"))
                elif k == "ynorm":
                    ps = take(s)
                    act.activation(root[:, 0, :], ps, ACT.Sqrt, bias=small[:, 0:1]).then_inc(read["mean", "A"], 1); note(read["mean", "A"])
                elif k == "ln":
                    ps = take(("ln", 0))
                    act.activation(root[:, 1, :], ps, ACT.Copy).then_inc(read["mean", "A"], 1); note(read["mean", "A"])
                    ps = take(("ln", 1))
                    act.activation(root[:, 0, :], ps, ACT.Sqrt, bias=small[:, 1:2]).then_inc(read["mean", "A"], 1); note(read["mean", "A"])
                    for c in range(8):
                        act.wait_ge(sem("ln_z"), c + 1)
                        link(act.activation(A(AC + c), A(AC + c), ACT.Identity, bias=half[:, 8 + c:9 + c],
                                            scale=half[:, c:c + 1]))
                        act.activation(A(SQ + c), A(AC + c), ACT.Tanh).then_inc(sem("ln_tanh"), 1); note(sem("ln_tanh"))
                elif k == "scan":
                    for h in range(LRU_H):
                        act.wait_ge(sem("r2_ready"), h + 1)
                        act.activation(A(U2 + h), A(U2 + h), ACT.Sqrt).then_inc(sem("usqrt"), 1); note(sem("usqrt"))
                elif k == "job" and s[1] not in ON_VECTOR:
                    _, name, j = s
                    act.wait_ge(filled["proj"], filled_at[s])
                    ps = slot(s)[:, 0:S]
                    done = read["proj", "A"]
                    if name == "iq":
                        act.activation(A(IQ + j), ps, ACT.Copy).then_inc(done, 1); note(done)
                    elif name == "ik":
                        for a in range(4):
                            ins = act.activation(ikz[32 * a:32 * a + 32, a, :], ps[32 * a:32 * a + 32, :], ACT.Copy)
                        ins.then_inc(done, 1); note(done)
                    elif name in ("dk", "kc", "vc", "ks", "kw"):
                        to = {"dk": DK, "kc": KC, "vc": VC, "ks": KS, "kw": KW}[name]
                        act.activation(A(to), ps, ACT.Copy).then_inc(done, 1); note(done)
                    elif name in ("dq", "nq"):
                        act.activation(A((DQ if name == "dq" else NQ) + j), ps, ACT.Copy).then_inc(done, 1); note(done)
                    elif name in ("xbc", "xr"):
                        n = j if name == "xbc" else 24 + j
                        if n >= 3:
                            act.wait_ge(sem("conv_done"), n - 2)
                        act.activation(raw[:, n % 3, 3:3 + S], ps, ACT.Copy).then_inc(done, 1); note(done)
                    elif name == "mg":
                        act.activation(A(MG + j), ps, ACT.Tanh, scale=0.5).then_inc(done, 1); note(done)
                    elif name == "ff1":
                        act.activation(A(FF + j), ps, ACT.Relu).then_inc(done, 1); note(done)
                    elif name == "val_glu":
                        c = j // 2
                        if j % 2 == 0:
                            act.activation(A(VA + c), ps, ACT.Copy, scale=0.5).then_inc(done, 1); note(done)
                        else:
                            act.activation(A(TA + c), ps, ACT.Tanh, scale=0.5).then_inc(done, 1); note(done)
                    elif name == "b_val":
                        if j == 0:
                            act.wait_ge(sem("pads_ready"), 2)
                        act.activation(bv[:, j, 16:16 + S], ps, ACT.Copy).then_inc(done, 1); note(done)
                    elif name in ("sz", "a_gate", "b_gate", "gate"):
                        to = {"sz": SZ, "a_gate": GA, "b_gate": GB, "gate": GG}[name]
                        if name == "sz" and j == 0:
                            act.wait_ge(sem("kk_ready"), 4)
                        act.activation(A(to + j), ps, ACT.Copy, scale=0.5)
                        b = ths[0]
                        ths[0] += 1
                        if b == 0:
                            act.wait_ge(sem("silu_done"), 24)
                        if b >= 3:
                            act.wait_ge(sem("gated"), b - 2)
                        act.activation(th[:, b % 3, :], ps, ACT.Tanh, scale=0.5).then_inc(done, 1); note(done)
                    elif name == "rg_ig":
                        h = j // 2
                        if j % 2 == 0:
                            link(act.activation(A(U2 + h), ps, ACT.Tanh, bias=half[:, 16 + h:17 + h], scale=0.5))
                            act.activation(A(U2 + h), A(U2 + h), ACT.Tanh, bias=half[:, 40 + h:41 + h],
                                           scale=half[:, 40 + h:41 + h]).then_inc(done, 1); note(done)
                        else:
                            act.activation(A(TI + h), ps, ACT.Tanh, bias=half[:, 28 + h:29 + h], scale=0.5)\
                                .then_inc(done, 1); note(done)

        @block.vector
        def _(dve):
            counts, last = {}, []

            def note(semaphore):
                n = str(semaphore.name)
                counts[n] = counts.get(n, 0) + 1
                last[:] = [semaphore, counts[n]]

            def settle():
                if last:
                    dve.wait_ge(*last)

            def link(ins):
                ins.then_inc(sem("dve_chain"), 1)
                note(sem("dve_chain"))
                settle()

            def take(key):
                dve.wait_ge(filled[where[key][0]], turn(key) + 1)
                return slot(key)


            zeros = [0]

            def fill(ap, value):
                dve.memset(ap, value).then_inc(sem("zeros"), 1)
                note(sem("zeros"))
                zeros[0] += 1

            fill(mean_d[:, :], 1.0 / D)
            fill(small[:, 0:1], 1e-6)
            fill(small[:, 1:2], 1e-5)
            fill(ones[:, :], 1.0)
            fill(ident[:, :], 0.0)
            fill(caus[:, :, :], 0.0)
            fill(jneg[:, :], 0.0)
            fill(cneg[:, :, :], 0.0)
            fill(cvis[:, :, :], 1.0)
            fill(mean_i[:, :], 1.0 / (2 * D))
            fill(mean_h[:, 0:64], 0.0)
            fill(mean_h[:, 64:128], 0.0)
            dve.wait_ge(sem("zeros"), zeros[0])
            fill(mean_h[0:64, 0:64], 1.0 / HD)
            fill(mean_h[64:128, 64:128], 1.0 / HD)
            for tile in (kk_d, kk_s, kk_w, kk_c, vcl, sbuf_t, raw):
                fill(tile[:], 0.0)
            fill(ikz, 0.0)
            fill(wcmp[0:64, :, :, 64:128], 0.0)
            fill(wcmp[64:128, :, :, 0:64], 0.0)
            assert zeros[0] == ZEROS
            dve.wait_ge(sem("zeros"), ZEROS)
            dve.wait_ge(sem("consts"), CONSTS)
            dve.wait_ge(sem("par_in"), 16)
            link(dve.tensor_scalar(half[:, 0:16], par[:, AT["ln_g"]:AT["ln_g"] + 16], 0.5, None, ALU.mult))
            link(dve.tensor_scalar(half[:, 16:40], par[:, AT["b_rg"]:AT["b_rg"] + 24], 0.5, None, ALU.mult))
            link(dve.tensor_scalar(half[:, 64:160], par[:, AT["ssd_cw"]:AT["ssd_cw"] + 96], 0.5, None, ALU.mult))
            link(dve.tensor_scalar(par[:, AT["ssd_cb"]:AT["ssd_cb"] + 24], par[:, AT["ssd_cb"]:AT["ssd_cb"] + 24],
                                   0.5, None, ALU.mult))
            sq = sem("sq_ready")
            ths = [0]
            for s in steps:
                k = s[0]
                settle()
                if k == "norm":
                    q = s[1]
                    if q == 0:
                        dve.wait_ge(sem("x_in"), 16)
                    for c in range(8):
                        dve.tensor_tensor(A(HT + c), A(XT + c), A(XT + c), ALU.mult).then_inc(sq, 1); note(sq)
                    was_read(dve, s)
                    link(dve.reciprocal(rinv[:, :], root[:, 0, :]))
                    g = ("norm1", "norm2", "even_g", "odd_g", "final_g")[q]
                    for c in range(8):
                        dve.scalar_tensor_tensor(out=A(HT + c), in0=A(XT + c), scalar=col(g, c), in1=rinv[:, :],
                                                 op0=ALU.mult, op1=ALU.mult).then_inc(sem("h_ready"), 1); note(sem("h_ready"))
                elif k == "softplus":
                    was_read(dve, ("tok", 1))
                    dve.wait_ge(sem("row_in"), 16)
                    for t in range(NT):
                        dve.tensor_tensor(sp[:, 0, 32 * t:32 * t + 32], tok[:, t, TOK_DT:TOK_DT + 32], row[:, 0:32],
                                          ALU.add)
                    link(dve.tensor_scalar(sp[:, 0, 64:76], par[:, AT["lam"]:AT["lam"] + 12], -1.0, None, ALU.mult))
                    dve.scalar_tensor_tensor(out=sp[:, 1, :], in0=sp[:, 0, :], scalar=-1.0, in1=sp[:, 0, :],
                                             op0=ALU.mult, op1=ALU.max)\
                        .then_inc(sem("abs_ready"), 1); note(sem("abs_ready"))
                    dve.wait_ge(sem("gate_tanh"), 1)
                    dve.tensor_scalar(gates[:, :, :], gates[:, :, :], 0.5, 0.5, ALU.mult, ALU.add)\
                        .then_inc(sem("gates_ready"), 1); note(sem("gates_ready"))
                    z, y, y2, acc = sp[:, 1, :], sp[:, 2, :], sp[:, 3, :], sp[:, 4, :]
                    dve.wait_ge(sem("expabs_ready"), 1)
                    link(dve.tensor_scalar(y2, z, 2.0, None, ALU.add))
                    link(dve.reciprocal(y, y2))
                    link(dve.tensor_tensor(y, y, z, ALU.mult))
                    link(dve.tensor_tensor(y2, y, y, ALU.mult))
                    link(dve.tensor_scalar(acc, y2, 1.0 / 17, None, ALU.mult))
                    for m in (15, 13, 11, 9, 7, 5, 3):
                        link(dve.scalar_tensor_tensor(out=acc, in0=acc, scalar=1.0 / m, in1=y2,
                                                      op0=ALU.add, op1=ALU.mult))
                    link(dve.scalar_tensor_tensor(out=acc, in0=acc, scalar=1.0, in1=y, op0=ALU.add, op1=ALU.mult))
                    link(dve.tensor_scalar(y, sp[:, 0, :], 0.0, None, ALU.max))
                    link(dve.scalar_tensor_tensor(out=sp[:, 5, :], in0=acc, scalar=2.0, in1=y,
                                                  op0=ALU.mult, op1=ALU.add))
                    link(dve.tensor_scalar(half[:, 40:52], sp[:, 5, 64:76], 2.0, None, ALU.mult))
                    dve.wait_ge(sem("ea_ready"), 1)
                    for t in range(NT):
                        dve.scalar_tensor_tensor(out=dta[:, 32 * t:32 * t + 32], in0=sp[:, 5, 32 * t:32 * t + 32],
                                                 scalar=-1.0, in1=ea[:, :], op0=ALU.mult, op1=ALU.mult)\
                            .then_inc(sem("dta_ready"), 1); note(sem("dta_ready"))
                elif k == "acum":
                    was_read(dve, s)
                    dve.tensor_tensor(dec[:, :], ac[:, 64:96], ac[:, 0:32], ALU.subtract)\
                        .then_inc(sem("decarg_ready"), 1); note(sem("decarg_ready"))
                elif k == "cmp_in":
                    for v, src in ((0, KC), (1, VC)):
                        was_read(dve, ("job", ("kc", "vc")[v], 0))
                        view = A(src).rearrange("p (m b) -> p b m", b=16)
                        for a in range(2):
                            pos = par[:, AT["cmp_pos"] + 32 * v + 16 * a:AT["cmp_pos"] + 32 * v + 16 * a + 16]
                            dve.tensor_tensor(kcp[:, v, 16 * a:16 * a + 16, :], view[:, :, a:a + N_CMP],
                                              pos.unsqueeze(2).to_broadcast([P, 16, N_CMP]), ALU.add)\
                                .then_inc(sem("kcp_ready"), 1); note(sem("kcp_ready"))
                elif k == "qsq":
                    i = s[1]
                    src, w, _, _ = qn[i]
                    job = {0: "dk", 1: "ks", 2: "kw"}.get(i)
                    if i == 3:
                        was_read(dve, ("cmp_mm",))
                    else:
                        was_read(dve, ("job", job, 0) if job else ("job", "dq" if i < 12 else "nq", (i - 4) % 8))
                    dve.tensor_tensor(sqb[:, i % 2, 0:w], src, src, ALU.mult).then_inc(sem("qsq_ready"), 1); note(sem("qsq_ready"))
                elif k == "qap":
                    i = s[1]
                    src, w, gain, gi = qn[i]
                    was_read(dve, ("qsq", i))
                    link(dve.reciprocal(rinv[:, 0:w], root[:, i % 2, 0:w]))
                    if i >= 4:
                        dve.scalar_tensor_tensor(out=src, in0=src, scalar=col(gain), in1=rinv[:, 0:w],
                                                 op0=ALU.mult, op1=ALU.mult).then_inc(sem("q_ready"), 1); note(sem("q_ready"))
                    else:
                        kk = (kk_d, kk_s, kk_w, kk_c)[i]
                        for half_in in range(2):
                            a = 64 * half_in
                            for half_out in ((half_in,) if i == 0 else (0, 1)):
                                b = 64 * half_out
                                dst = kk[b:b + 64, half_out, :] if i == 0 else kk[b:b + 64, half_in, half_out, :]
                                ins = dve.scalar_tensor_tensor(
                                    out=dst, in0=src[a:a + 64], scalar=col(gain, gi)[a:a + 64],
                                    in1=rinv[a:a + 64, 0:w], op0=ALU.mult, op1=ALU.mult)
                        ins.then_inc(sem("kk_ready"), 1); note(sem("kk_ready"))
                elif k == "idx":
                    i = s[1]
                    t = i // 4
                    kl = P * (t + 1)
                    was_read(dve, s)
                    for h in range(2):
                        head = 2 * (i % 4) + h
                        rl = arena[:, RL + 2 * (i % 2) + h, 0:kl]
                        iw = tok[:, t, TOK_IW + head:TOK_IW + head + 1]
                        acc = A(IDX + t)[:, 0:kl]
                        if head == 0:
                            ins = dve.tensor_scalar(acc, rl, iw, None, ALU.mult)
                        else:
                            ins = dve.scalar_tensor_tensor(out=acc, in0=rl, scalar=iw, in1=acc,
                                                           op0=ALU.mult, op1=ALU.add)
                        if h == 0:
                            link(ins)
                    ins.then_inc(sem("rl_used"), 1); note(sem("rl_used"))
                    dve.wait_ge(sem("rl_used"), i + 1)
                elif k == "select":
                    t = s[1]
                    kl = P * (t + 1)
                    acc = A(IDX + t)[:, 0:kl]
                    link(dve.tensor_tensor(acc, acc, caus[:, t, 0:kl], ALU.add))
                    for _ in range(TOPK // 8):
                        link(dve.max(m8[:, :], acc))
                        link(dve.match_replace(acc, m8[:, :], acc, MARK))
                    link(dve.tensor_scalar(acc, acc, MARK, 1.0, ALU.is_equal, ALU.subtract))
                    dve.scalar_tensor_tensor(out=dmask[:, t, 0:kl], in0=acc, scalar=-NEG, in1=caus[:, t, 0:kl],
                                             op0=ALU.mult, op1=ALU.add).then_inc(sem("select_done"), 1); note(sem("select_done"))
                    dve.wait_ge(sem("select_done"), t + 1)
                elif k == "pcmp":
                    t = s[1]
                    ps = take(s)[:, 0:16 * N_CMP].rearrange("p (h n) -> p h n", h=16)
                    e = ec[:, :, 0:N_CMP]
                    dve.tensor_tensor(e, ps, cneg[:, t, 0:N_CMP].unsqueeze(1).to_broadcast([P, 16, N_CMP]),
                                      ALU.add).then_inc(read["score", "D"], 1); note(read["score", "D"])
                    dve.wait_ge(read["score", "D"], sum("D" in r for r in turns["score"][:turn(s) + 1]))
                    link(dve.tensor_reduce(crow[:, 0, :], e, AX.X, ALU.max))
                    dve.tensor_tensor(e, e, crow[:, 0, :].unsqueeze(2).to_broadcast([P, 16, N_CMP]),
                                      ALU.subtract).then_inc(sem("carg_ready"), 1); note(sem("carg_ready"))
                    dve.wait_ge(sem("ce_ready"), t + 1)
                    link(dve.tensor_reduce(crow[:, 1, :], e, AX.X, ALU.add))
                    link(dve.reciprocal(crow[:, 2, :], crow[:, 1, :]))
                    link(dve.tensor_tensor(crow[:, 2, :], crow[:, 2, :],
                                           gates[:, t, :].rearrange("p (h j) -> p h j", j=3)[:, :, 0], ALU.mult))
                    link(dve.tensor_tensor(e, e, cvis[:, t, 0:N_CMP].unsqueeze(1).to_broadcast([P, 16, N_CMP]),
                                           ALU.mult))
                    if t == 1:
                        dve.wait_ge(filled["turn"], turn(("pcmpT", 0)) + 1)
                    dve.tensor_tensor(pc[:, :, 0:N_CMP], e, crow[:, 2, :].unsqueeze(2).to_broadcast([P, 16, N_CMP]),
                                      ALU.mult).then_inc(sem("pc_ready"), 1); note(sem("pc_ready"))
                elif k == "sA":
                    i = s[1]
                    t, c, kk, q, mask, v, gate = soft(i)
                    kl = P * (t + 1)
                    ps = take(s).rearrange("p (h k) -> p h k", h=2)[:, :, 0:kl]
                    x = sbuf_s[:, i % 4, :].rearrange("p (h k) -> p h k", h=2)[:, :, 0:kl]
                    if i >= 4:
                        dve.wait_ge(filled["turn"], turn(("sB", i - 4)) + 1)
                    dve.tensor_tensor(x, ps, mask[:, t, 0:kl].unsqueeze(1).to_broadcast([P, 2, kl]), ALU.add)\
                        .then_inc(read["score", "D"], 1); note(read["score", "D"])
                    dve.wait_ge(read["score", "D"], sum("D" in r for r in turns["score"][:turn(s) + 1]))
                    link(dve.tensor_reduce(srow[:, i % 4, 0:2], x, AX.X, ALU.max))
                    dve.tensor_scalar(srow[:, i % 4, 2:4], srow[:, i % 4, 0:2], -SCALE, None, ALU.mult)\
                        .then_inc(sem("nmax_ready"), 1); note(sem("nmax_ready"))
                elif k == "sR":
                    i = s[1]
                    t, c, _, _, _, _, gate = soft(i)
                    dve.wait_ge(sem("e_ready"), i + 1)
                    ins = dve.reciprocal(srow[:, i % 4, 6:8], srow[:, i % 4, 4:6])
                    if gate is not None:
                        link(ins)
                        gt = gates[:, t, :].rearrange("p (h j) -> p h j", j=3)[:, 2 * c:2 * c + 2, gate]
                        ins = dve.tensor_tensor(srow[:, i % 4, 6:8], srow[:, i % 4, 6:8], gt, ALU.mult)
                    ins.then_inc(sem("scale_ready"), 1); note(sem("scale_ready"))
                elif k in ("xconv", "oconv"):
                    j = s[1]
                    n = j if k == "xconv" else 24 + j
                    was_read(dve, ("job", "xbc" if k == "xconv" else "xr", j))
                    dst = A((XB if k == "xconv" else XC) + j)
                    for tap in range(4):
                        w = half[:, 64 + 4 * j + tap:65 + 4 * j + tap] if k == "xconv" else col("odd_cw", 4 * j + tap)
                        src = raw[:, n % 3, tap:tap + S]
                        if tap == 0:
                            link(dve.tensor_scalar(dst, src, w, col("ssd_cb" if k == "xconv" else "odd_cb", j),
                                                   ALU.mult, ALU.add))
                        else:
                            ins = dve.scalar_tensor_tensor(out=dst, in0=src, scalar=w, in1=dst,
                                                           op0=ALU.mult, op1=ALU.add)
                            if tap < 3:
                                link(ins)
                    ins.then_inc(sem("conv_done"), 1); note(sem("conv_done"))
                elif k == "xsilu":
                    j = s[1]
                    dve.wait_ge(sem("xtanh"), j + 1)
                    dve.scalar_tensor_tensor(out=A(XB + j), in0=th[:, j % 3, :], scalar=1.0, in1=A(XB + j),
                                             op0=ALU.add, op1=ALU.mult).then_inc(sem("silu_done"), 1); note(sem("silu_done"))
                elif k == "xtr":
                    i = s[1]
                    t, q = i // 4, i % 4
                    ps = take(s)
                    dve.tensor_tensor(
                        xd[t][:, 512 * q:512 * q + 512].rearrange("p (h e) -> p h e", h=8),
                        ps[:, :].rearrange("p (h e) -> p h e", h=8),
                        sp[:, 5, 32 * t + 8 * q:32 * t + 8 * q + 8].unsqueeze(2).to_broadcast([P, 8, 64]),
                        ALU.mult).then_inc(read["turn", "D"], 1); note(read["turn", "D"])
                elif k == "uA":
                    i = s[1]
                    t, hq = i // 8, i % 8
                    ps = take(s).rearrange("p (h i) -> p h i", h=4)
                    x = sbuf_s[:, i % 4, :].rearrange("p (h i) -> p h i", h=4)
                    if i >= 4:
                        dve.wait_ge(sem("pv_done"), 48 + i - 3)
                    else:
                        dve.wait_ge(sem("pv_done"), 48)
                    dve.tensor_tensor(x, ps, ac[:, 32 * t + 4 * hq:32 * t + 4 * hq + 4].unsqueeze(2)
                                      .to_broadcast([P, 4, P]), ALU.subtract).then_inc(read["score", "D"], 1); note(read["score", "D"])
                    dve.wait_ge(read["score", "D"], sum("D" in r for r in turns["score"][:turn(s) + 1]))
                    dve.tensor_tensor(x, x, jneg[:, :].unsqueeze(1).to_broadcast([P, 4, P]), ALU.add)\
                        .then_inc(sem("seg_ready"), 1); note(sem("seg_ready"))
                elif k == "uB":
                    i = s[1]
                    t, hq = i // 8, i % 8
                    dve.wait_ge(sem("pv_done"), 48 + i + 1)
                    ps = slot(s)
                    if i == 0:
                        dve.wait_ge(sem("gated"), 16)
                    for cc in range(2):
                        c = 2 * hq + cc
                        xs = A(XB + c)[:, P * t:P * t + P]
                        ins = dve.scalar_tensor_tensor(out=ytmp[:, cc, :], in0=xs, scalar=col("ssd_d", c),
                                                       in1=ps[:, P * cc:P * cc + P], op0=ALU.mult, op1=ALU.add)
                    ins.then_inc(read["pv", "D"], 1); note(read["pv", "D"])
                    dve.wait_ge(read["pv", "D"], i + 1)
                    for cc in range(2):
                        c = 2 * hq + cc
                        ins = dve.tensor_tensor(A(XB + c)[:, P * t:P * t + P], ytmp[:, cc, :],
                                                A(SZ + c)[:, P * t:P * t + P], ALU.mult)
                    link(ins)
                elif k == "ynorm":
                    for c in range(16):
                        dve.tensor_tensor(A(XD + c), A(XB + c), A(XB + c), ALU.mult).then_inc(sem("ysq_ready"), 1); note(sem("ysq_ready"))
                    was_read(dve, s)
                    link(dve.reciprocal(rinv[:, :], root[:, 0, :]))
                    for c in range(16):
                        dve.scalar_tensor_tensor(out=A(XB + c), in0=A(XB + c), scalar=col("ssd_g", c),
                                                 in1=rinv[:, :], op0=ALU.mult, op1=ALU.mult)\
                            .then_inc(sem("y_ready"), 1); note(sem("y_ready"))
                elif k == "econv":
                    c = s[1]
                    was_read(dve, ("job", "val_glu", 2 * c + 1))
                    if c == 0:
                        dve.wait_ge(sem("pads_ready"), 2)
                    link(dve.scalar_tensor_tensor(out=ub[:, c, 30:30 + S], in0=A(TA + c), scalar=1.0, in1=A(VA + c),
                                                  op0=ALU.add, op1=ALU.mult))
                    dst = A(AC + c)
                    link(dve.tensor_scalar(dst, ub[:, c, 0:S], col("even_cw", CONV_K * c), col("even_cb", c),
                                           ALU.mult, ALU.add))
                    for tap in range(1, CONV_K):
                        ins = dve.scalar_tensor_tensor(out=dst, in0=ub[:, c, tap:tap + S],
                                                       scalar=col("even_cw", CONV_K * c + tap), in1=dst,
                                                       op0=ALU.mult, op1=ALU.add)
                        if tap < CONV_K - 1:
                            link(ins)
                    ins.then_inc(sem("econv_done"), 1); note(sem("econv_done"))
                elif k == "ln":
                    was_read(dve, ("ln", 0))
                    dve.wait_ge(sem("econv_done"), 8)
                    for c in range(8):
                        ins = dve.tensor_tensor(A(AC + c), A(AC + c), root[:, 1, :], ALU.subtract)
                    link(ins)
                    for c in range(8):
                        dve.tensor_tensor(A(SQ + c), A(AC + c), A(AC + c), ALU.mult).then_inc(sem("lsq_ready"), 1); note(sem("lsq_ready"))
                    was_read(dve, ("ln", 1))
                    link(dve.reciprocal(rinv[:, :], root[:, 0, :]))
                    for c in range(8):
                        dve.tensor_tensor(A(AC + c), A(AC + c), rinv[:, :], ALU.mult).then_inc(sem("ln_z"), 1); note(sem("ln_z"))
                    for c in range(8):
                        dve.wait_ge(sem("ln_tanh"), c + 1)
                        link(dve.scalar_tensor_tensor(out=A(YA + c), in0=A(SQ + c), scalar=1.0, in1=A(AC + c),
                                                      op0=ALU.add, op1=ALU.mult))
                        dve.tensor_tensor(A(YA + c), A(YA + c), A(GA + c), ALU.mult).then_inc(sem("ya_ready"), 1); note(sem("ya_ready"))
                elif k == "lru":
                    h = s[1]
                    was_read(dve, ("job", "rg_ig", 2 * h + 1))
                    link(dve.tensor_scalar(A(LA + h), A(U2 + h), 1.0, None, ALU.add))
                    dve.reciprocal(A(R2 + h), A(LA + h)).then_inc(sem("r2_ready"), 1); note(sem("r2_ready"))
                    dve.wait_ge(sem("r2_ready"), h + 1)
                    dve.tensor_scalar(A(LA + h), A(R2 + h), 2.0, -1.0, ALU.mult, ALU.add)
                    link(dve.scalar_tensor_tensor(out=A(W1 + h), in0=A(TI + h), scalar=1.0, in1=A(XC + h),
                                                  op0=ALU.add, op1=ALU.mult))
                elif k == "scan":
                    for h in range(LRU_H):
                        dve.wait_ge(sem("usqrt"), h + 1)
                        link(dve.tensor_tensor(A(R2 + h), A(R2 + h), A(U2 + h), ALU.mult))
                        link(dve.tensor_tensor(A(W1 + h), A(W1 + h), A(R2 + h), ALU.mult))
                        link(dve.tensor_tensor_scan(A(TI + h), A(LA + h), A(W1 + h), 0.0, ALU.mult, ALU.add))
                        dve.tensor_tensor(A(LY + h), A(TI + h), A(GG + h), ALU.mult).then_inc(sem("ly_ready"), 1); note(sem("ly_ready"))
                elif k == "job" and s[1] in ("sz", "a_gate", "b_gate", "gate"):
                    to = {"sz": SZ, "a_gate": GA, "b_gate": GB, "gate": GG}[s[1]] + s[2]
                    b = ths[0]
                    ths[0] += 1
                    was_read(dve, s)
                    dve.scalar_tensor_tensor(out=A(to), in0=th[:, b % 3, :], scalar=1.0, in1=A(to),
                                             op0=ALU.add, op1=ALU.mult).then_inc(sem("gated"), 1); note(sem("gated"))
                elif k == "job" and s[1] in ON_VECTOR:
                    _, name, j = s
                    dve.wait_ge(filled["proj"], filled_at[s])
                    ps = slot(s)[:, 0:S]
                    done = read["proj", "D"]
                    mine = sum("D" in r for r in turns["proj"][:turn(s) + 1])
                    if name == "br_dsa":
                        if j == 0:
                            dve.wait_ge(sem("mg_ready"), 24)
                        dve.tensor_tensor(A(HT + j), ps, A(MG + j), ALU.mult).then_inc(done, 1); note(done)
                    elif name in ("br_nsa", "br_ssd"):
                        g = MG + (8 if name == "br_nsa" else 16) + j
                        dve.tensor_tensor(sqb[:, 0, :], ps, A(g), ALU.mult).then_inc(done, 1); note(done)
                        dve.wait_ge(done, mine)
                        ins = dve.tensor_tensor(A(HT + j), A(HT + j), sqb[:, 0, :], ALU.add)
                        if name == "br_nsa":
                            link(ins)
                        else:
                            ins.then_inc(sem("mix_ready"), 1); note(sem("mix_ready"))
                            dve.wait_ge(sem("mix_ready"), j + 1)
                    elif name == "pool":
                        dve.tensor_scalar(A(YB + j), ps, col("pool_b", j), col("pool_s", j), ALU.add, ALU.mult)\
                            .then_inc(done, 1); note(done)
                        dve.wait_ge(done, mine)
                        if j == 0:
                            dve.wait_ge(sem("gated"), 32)
                        dve.tensor_tensor(A(YB + j), A(YB + j), A(GB + j), ALU.mult).then_inc(sem("yb_ready"), 1); note(sem("yb_ready"))
                    else:
                        dve.tensor_tensor(A(XT + j), A(XT + j), ps, ALU.add).then_inc(done, 1); note(done)
                        dve.wait_ge(done, mine)

        @block.tensor
        def _(pe):
            pe.wait_ge(sem("zeros"), ZEROS)
            pe.wait_ge(sem("consts"), CONSTS)


            for s in steps:
                k = s[0]
                if k == "norm":
                    q = s[1]
                    readers_done(pe, s)
                    for c in range(8):
                        pe.wait_ge(sem("sq_ready"), 8 * q + c + 1)
                        mm = pe.matmul(slot(s), mean_d[:, :], A(HT + c), start=(c == 0), stop=(c == 7))
                    mm.then_inc(filled["mean"], 1)
                elif k == "tok":
                    t = s[1]
                    readers_done(pe, s)
                    if t == 0:
                        pe.wait_ge(sem("wtok_in"), 16)
                    for c in range(8):
                        pe.wait_ge(sem("h_ready"), c + 1)
                        mm = pe.matmul(slot(s)[:, 0:TOK], A(HT + c)[:, P * t:P * t + P], wtok[:, c, :],
                                       start=(c == 0), stop=(c == 7))
                    mm.then_inc(filled["score"], 1)
                elif k == "acum":
                    readers_done(pe, s)
                    pe.wait_ge(sem("dta_ready"), 2)
                    ps = slot(s)
                    pe.matmul(ps[:, 0:64], upper[:, :], dta[:, :], start=True, stop=True)
                    pe.matmul(ps[:, 64:96], ones[:, :], dta[:, 0:32], start=True, stop=True)\
                        .then_inc(filled["mean"], 1)
                elif k == "cmp_mm":
                    readers_done(pe, s)
                    pe.wait_ge(sem("wcmp_in"), 32)
                    pe.wait_ge(sem("kcp_ready"), 4)
                    for v in range(2):
                        for l in range(32):
                            mm = pe.matmul(slot(s)[:, 256 * v:256 * v + N_CMP], wcmp[:, v, l, :], kcp[:, v, l, :],
                                           start=(l == 0), stop=(l == 31))
                    mm.then_inc(filled["score"], 1)
                elif k == "qsq":
                    i = s[1]
                    w = qn[i][1]
                    readers_done(pe, s)
                    pe.wait_ge(sem("qsq_ready"), i + 1)
                    pe.matmul(slot(s)[:, 0:w], mean_h[:, :], sqb[:, i % 2, 0:w], start=True, stop=True)\
                        .then_inc(filled["mean"], 1)
                elif k == "idx":
                    i = s[1]
                    t, m, pair = i // 4, (i % 4) // 2, i % 2
                    kl = P * (t + 1)
                    readers_done(pe, s)
                    was_read(pe, ("job", "ik", 0))
                    ps = slot(s).rearrange("p (h k) -> p h k", h=2)[:, :, 0:kl]
                    pe.matmul(ps, A(IQ + m)[:, P * t:P * t + P], ikz[:, 2 * pair:2 * pair + 2, 0:kl],
                              start=True, stop=True).then_inc(filled["score"], 1)
                elif k == "vcmp":
                    readers_done(pe, s)
                    was_read(pe, ("cmp_mm",))
                    pe.transpose(slot(s)[0:N_CMP, 0:P], kcr[:, 1, 0:N_CMP], ident[:, :]).then_inc(filled["turn"], 1)
                elif k == "pcmp":
                    t = s[1]
                    readers_done(pe, s)
                    pe.wait_ge(sem("kk_ready"), 4)
                    pe.wait_ge(sem("q_ready"), 16)
                    for c in range(8):
                        mm = pe.matmul(slot(s)[:, 30 * c:30 * c + 30], A(NQ + c)[:, P * t:P * t + P],
                                       kk_c[:, c // 4, :, :].rearrange("p h n -> p (h n)"), start=True, stop=True)
                    mm.then_inc(filled["score"], 1)
                    key = ("pcmpT", t)
                    readers_done(pe, key)
                    pe.wait_ge(sem("pc_ready"), t + 1)
                    for m in range(4):
                        mm = pe.transpose(slot(key)[:, P * m:P * m + P],
                                          pc[:, 4 * m:4 * m + 4, :].rearrange("p h n -> p (h n)"), ident[:, :])
                    mm.then_inc(filled["turn"], 1)
                elif k == "sA":
                    i = s[1]
                    t, c, kk, q, mask, v, gate = soft(i)
                    kl = P * (t + 1)
                    readers_done(pe, s)
                    if i < 16 and i % 8 == 0:
                        pe.wait_ge(sem("select_done"), t + 1)
                    ps = slot(s).rearrange("p (h k) -> p h k", h=2)[:, :, 0:kl]
                    pe.matmul(ps, A(q + c)[:, P * t:P * t + P], kk[:, :, 0:kl], start=True, stop=True)\
                        .then_inc(filled["score"], 1)
                elif k == "sB":
                    i = s[1]
                    t = soft(i)[0]
                    readers_done(pe, s)
                    pe.wait_ge(sem("p_ready"), i + 1)
                    for kt in range(t + 1):
                        for h in range(2):
                            n = 2 * kt + h
                            mm = pe.transpose(slot(s)[:, P * n:P * n + P],
                                              sbuf_s[:, i % 4, 256 * h + P * kt:256 * h + P * kt + P], ident[:, :])
                    mm.then_inc(filled["turn"], 1)
                elif k == "sC":
                    i = s[1]
                    t, c, _, _, _, v, gate = soft(i)
                    closes = ("sC", i if i < 16 or i % 2 else i + 1)
                    ps = slot(closes)
                    if gate in (None, 1):
                        readers_done(pe, closes)
                    if gate == 1:
                        was_read(pe, ("pcmpT", t))
                        pe.matmul(ps[:, 0:P], vcl[:, 2 * (c % 2) + c // 4, :], pct[:, t, P * (c // 2):P * (c // 2) + P],
                                  start=True, stop=False, skip_group_check=True)
                    was_read(pe, ("sB", i))
                    for h in range(2):
                        for kt in range(t + 1):
                            n = 2 * kt + h
                            mm = pe.matmul(ps[64 * h:64 * h + 64, 0:P], tok[:, kt, v:v + 64],
                                           sbuf_t[:, i % 2, P * n:P * n + P], start=(gate is None and kt == 0),
                                           stop=(kt == t and gate in (None, 2)), skip_group_check=True)
                    mm.then_inc(sem("pv_done"), 1)
                elif k == "xtr":
                    i = s[1]
                    t, q = i // 4, i % 4
                    readers_done(pe, s)
                    if i == 0:
                        pe.wait_ge(sem("silu_done"), 24)
                    for m in range(4):
                        mm = pe.transpose(slot(s)[:, P * m:P * m + P], A(XB + 4 * q + m)[:, P * t:P * t + P],
                                          ident[:, :])
                    mm.then_inc(filled["turn"], 1)
                elif k == "btr":
                    readers_done(pe, s)
                    for g in range(4):
                        mm = pe.transpose(slot(s)[:, P * g:P * g + P], A(XB + 16 + g)[:, 0:P], ident[:, :])
                    mm.then_inc(filled["turn"], 1)
                elif k == "cbt":
                    t = s[1]
                    readers_done(pe, s)
                    for g in range(4):
                        mm = pe.matmul(slot(s)[:, P * g:P * g + P], A(XB + 16 + g)[:, P * t:P * t + P],
                                       A(XB + 20 + g)[:, P * t:P * t + P], start=True, stop=True)
                    mm.then_inc(filled["score"], 1)
                elif k == "st":
                    g = s[1]
                    readers_done(pe, s)
                    was_read(pe, ("btr",))
                    pe.wait_ge(sem("xw_ready"), 4)
                    pe.matmul(slot(s)[:, :], bmt[:, g, :], xw[:, 512 * g:512 * g + 512], start=True, stop=True)\
                        .then_inc(filled["score"], 1)
                elif k == "uA":
                    i = s[1]
                    t, hq = i // 8, i % 8
                    readers_done(pe, s)
                    for h in range(4):
                        n = 32 * t + 4 * hq + h
                        mm = pe.matmul(slot(s)[:, P * h:P * h + P], dta[:, n:n + 1].to_broadcast([P, P]),
                                       upper[:, :], start=True, stop=True)
                    mm.then_inc(filled["score"], 1)
                elif k == "uB":
                    i = s[1]
                    t, hq = i // 8, i % 8
                    readers_done(pe, s)
                    pe.wait_ge(sem("m_ready"), i + 1)
                    if i == 0:
                        was_read(pe, ("st", 3))
                        was_read(pe, ("xtr", 7), "D")
                    for h in range(4):
                        head = 4 * hq + h
                        o = slot(s)[64 * (h % 2):64 * (h % 2) + 64, P * (h // 2):P * (h // 2) + P]
                        mm = pe.matmul(o, xd[t][:, 64 * head:64 * head + 64], sbuf_s[:, i % 4, P * h:P * h + P],
                                       start=True, stop=(t == 0), skip_group_check=True)
                        if t == 1:
                            mm = pe.matmul(o, hst[:, 64 * head:64 * head + 64], sbuf_t[:, i % 2, P * h:P * h + P],
                                           start=False, stop=True, skip_group_check=True)
                    mm.then_inc(sem("pv_done"), 1)
                elif k == "ynorm":
                    readers_done(pe, s)
                    for c in range(16):
                        pe.wait_ge(sem("ysq_ready"), c + 1)
                        mm = pe.matmul(slot(s), mean_i[:, :], A(XD + c), start=(c == 0), stop=(c == 15))
                    mm.then_inc(filled["mean"], 1)
                elif k == "ln":
                    for n, (src, ready) in enumerate(((AC, "econv_done"), (SQ, "lsq_ready"))):
                        key = ("ln", n)
                        readers_done(pe, key)
                        for c in range(8):
                            pe.wait_ge(sem(ready), c + 1)
                            mm = pe.matmul(slot(key), mean_d[:, :], A(src + c), start=(c == 0), stop=(c == 7))
                        mm.then_inc(filled["mean"], 1)
                elif k == "job":
                    _, name, j = s
                    n, b0 = blocks[s], first[s]
                    readers_done(pe, s)
                    rhs = [A(HT + c) for c in range(8)]
                    h_at = 0
                    if name == "br_dsa":
                        rhs = [A(DQ + c) for c in range(8)]
                        if j == 0:
                            was_read(pe, ("sC", 15))
                    elif name == "br_nsa":
                        rhs = [A(NQ + c) for c in range(8)]
                        if j == 0:
                            was_read(pe, ("sC", 47))
                    elif name == "br_ssd":
                        rhs = [A(XB + c) for c in range(16)]
                        if j == 0:
                            pe.wait_ge(sem("y_ready"), 16)
                    elif name == "w_out":
                        if j == 0:
                            pe.wait_ge(sem("mix_ready"), 8)
                    elif name == "ff1":
                        h_at = 8
                    elif name == "ff2":
                        rhs = [A(FF + c) for c in range(FFC)]
                        if j == 0:
                            pe.wait_ge(sem("ff_ready"), 32)
                    elif name in ("val_glu", "b_val", "b_gate", "a_gate"):
                        h_at = 16
                    elif name == "pool":
                        pe.wait_ge(sem("dp_ready"), 2 * (j // 2) + 2)
                        rhs = [A(DP + 2 * (j // 2)), A(DP + 2 * (j // 2) + 1)]
                    elif name == "even_out":
                        rhs = [A(YA + c) for c in range(8)] + [A(YB + c) for c in range(8)]
                        if j == 0:
                            pe.wait_ge(sem("yb_ready"), 8)
                            pe.wait_ge(sem("ya_ready"), 8)
                    elif name in ("xr", "gate"):
                        h_at = 24
                    elif name == "rg_ig":
                        if j % 2 == 0:
                            pe.wait_ge(sem("conv_done"), 24 + j // 2 + 1)
                        rhs = [A(XC + j // 2)]
                    elif name == "odd_out":
                        rhs = [A(LY + c) for c in range(12)]
                        if j == 0:
                            pe.wait_ge(sem("ly_ready"), 12)
                    for c in range(n):
                        if h_at and j == 0:
                            pe.wait_ge(sem("h_ready"), h_at + c + 1)
                        b = b0 + c
                        u = b // 8
                        if b % 8 == 0:
                            pe.wait_ge(w_in[u % RING], 16 * (u // RING + 1))
                        mm = pe.matmul(slot(s)[:, 0:S], ring[:, u % RING, b % 8, :], rhs[c],
                                       start=(c == 0), stop=(c == n - 1))
                        if b % 8 == 7 or c == n - 1:
                            mm.then_inc(filled["proj"], 1)


def kernel(**inputs):
    import numpy as np
    import concourse.bacc as bacc
    from concourse.bass_utils import run_bass_kernel_spmd

    a = {k: np.asarray(v) for k, v in inputs.items()}
    w = a["w_in"][0]
    cuts = np.cumsum([0, 1024, 64, 64, 256, 32, 8, 1024, 768, 48, 2048, 3072, 32, 3072])
    (dq, dk, dv, iq, ik, iw, nq, nkv, ng, sz, xbc, dt, mg) = [w[:, cuts[i]:cuts[i + 1]] for i in range(13)]
    kc, vc, ks, vs, kw, vw = [nkv[:, 128 * i:128 * i + 128] for i in range(6)]

    def tiles(m):
        K, N = m.shape
        return m.reshape(K // 128, 128, N // 128, 128).transpose(2, 0, 1, 3)

    even = a["w_in_even_2"][0]
    val, glu, a_gate, b_val, b_gate = [even[:, 1024 * i:1024 * i + 1024] for i in range(5)]
    odd = a["w_in_odd_2"][0]
    weights = {
        "iq": tiles(iq), "ik": tiles(np.concatenate([ik] * 4, axis=1)), "dk": tiles(np.concatenate([dk, dk], axis=1)),
        "kc": tiles(kc), "vc": tiles(vc), "ks": tiles(ks), "kw": tiles(kw), "dq": tiles(dq), "nq": tiles(nq),
        "xbc": tiles(xbc), "sz": tiles(sz), "mg": tiles(mg),
        "br_dsa": tiles(a["w_br_dsa"][0]), "br_nsa": tiles(a["w_br_nsa"][0]), "br_ssd": tiles(a["w_br_ssd"][0]),
        "w_out": tiles(a["w_out"][0]), "ff1": tiles(a["w_ff1"][0]), "ff2": tiles(a["w_ff2"][0]),
        "val_glu": np.stack([tiles(val), tiles(glu)], axis=1).reshape(16, 8, 128, 128),
        "b_val": tiles(b_val), "b_gate": tiles(b_gate), "a_gate": tiles(a_gate),
        "pool": a["pool_w_2"][0].reshape(4, 2, 128, 2, 128).transpose(0, 3, 1, 2, 4).reshape(8, 2, 128, 128),
        "even_out": tiles(a["w_out_even_2"][0]), "xr": tiles(odd[:, :1536]), "gate": tiles(odd[:, 1536:]),
        "rg_ig": np.stack([a["w_rg_2"][0], a["w_ig_2"][0]], axis=1).reshape(24, 1, 128, 128),
        "odd_out": tiles(a["w_out_odd_2"][0]),
    }
    parts = []
    for s in schedule():
        if s[0] == "job":
            parts.append(weights[s[1]][s[2]])
    stream = np.concatenate(parts, axis=0)
    stream = np.ascontiguousarray(stream.reshape(-1, 8, 128, 128).transpose(0, 2, 1, 3)).reshape(-1, 128, 1024)

    w_tok = np.concatenate([iw, ng, dt, dv, vs, vw], axis=1).reshape(8, 128, TOK).transpose(1, 0, 2)
    w_cmp = a["nsa_cmp_w"][0].transpose(2, 0, 1, 3)

    def chunks(v):
        return v.reshape(-1, 128).T

    def twice(v):
        return np.concatenate([v, v]).reshape(128, 1)

    pos = a["nsa_cmp_pos"][0].reshape(64, 64).T
    columns = {
        "norm1": chunks(a["norm1_g"]), "dq_g": twice(a["dsa_q_norm"][0]), "dk_g": twice(a["dsa_k_norm"][0]),
        "nq_g": twice(a["nsa_q_norm"][0]),
        "nk_g": np.concatenate([twice(a["nsa_k_norm"][0, i]) for i in range(3)], axis=1),
        "cmp_pos": np.concatenate([pos, pos], axis=0),
        "ssd_cw": a["ssd_conv_w"][0].reshape(4, 24, 128).transpose(2, 1, 0).reshape(128, 96),
        "ssd_cb": chunks(a["ssd_conv_b"]), "ssd_d": chunks(np.repeat(a["ssd_d"][0], 64)),
        "ssd_g": chunks(a["ssd_norm_g"]), "norm2": chunks(a["norm2_g"]), "even_g": chunks(a["norm_even_2"]),
        "even_cw": a["conv_a_w_2"][0].reshape(31, 8, 128).transpose(2, 1, 0).reshape(128, 248),
        "even_cb": chunks(a["conv_a_b_2"]), "ln_g": chunks(a["ln_a_g_2"]), "ln_b": chunks(a["ln_a_b_2"]),
        "pool_b": chunks(a["pool_b_2"]), "pool_s": chunks(a["pool_scale_2"]), "odd_g": chunks(a["norm_odd_2"]),
        "odd_cw": a["conv_c_w_2"][0].reshape(4, 12, 128).transpose(2, 1, 0).reshape(128, 48),
        "odd_cb": chunks(a["conv_c_b_2"]), "b_rg": chunks(a["b_rg_2"]), "b_ig": chunks(a["b_ig_2"]),
        "lam": chunks(a["lru_lambda_2"]), "final_g": chunks(a["final_norm_2"]),
    }
    cols = np.concatenate([columns[name] for name, _ in COLUMNS], axis=1)
    rows = np.broadcast_to(np.concatenate([a["ssd_dt_bias"], a["ssd_a_log"]], axis=1), (128, 64))
    x_t = a["x"][0].T.reshape(8, 128, 256).transpose(1, 0, 2)
    arrays = {"x_t": x_t, "w_stream": stream, "w_tok": w_tok, "w_cmp": w_cmp, "cols": cols, "rows": rows}
    arrays = {k: np.ascontiguousarray(v) for k, v in arrays.items()}

    nc = bacc.Bacc("TRN2", target_bir_lowering=False, num_devices=1)
    aps = [nc.dram_tensor(k, v.shape, mybir.dt.from_np(v.dtype), kind="ExternalInput").ap() for k, v in arrays.items()]
    out = nc.dram_tensor("out_t", (128, 8, 256), F32, kind="ExternalOutput").ap()
    program(nc, *aps, out)
    r = run_bass_kernel_spmd(nc, [arrays], core_ids=[0])
    got = r.results[0]["out_t"]
    return np.ascontiguousarray(got.transpose(1, 0, 2).reshape(1024, 256).T)[None]
```

```python
from contextlib import ExitStack

import concourse.bass as bass
from concourse import mybir

F32 = mybir.dt.float32
F32R = mybir.dt.float32r
ALU = mybir.AluOpType
ACT = mybir.ActivationFunctionType
AX = mybir.AxisListType

P = 128
S = 256
NT = S // P
D = 1024
KD = D // P
HD = 64
NEG = -1e30
MARK = -3e38
TOPK = 64
SCALE = HD ** -0.5
N_CMP = 15
SSD_H = 32
FFC = 4 * D // P
LRU_H = 12
CONV_K = 31
WINDOWS = (2, 4, 8, 16)
RING = 5
HIS = 3
AHEAD = 2
TOK = 408
TOK_IW, TOK_NG, TOK_DT, TOK_DV, TOK_VS, TOK_VW = 0, 8, 56, 88, 152, 280

COLUMNS = [("norm1", 8), ("dq_g", 1), ("dk_g", 1), ("nq_g", 1), ("nk_g", 3), ("cmp_pos", 64),
           ("ssd_cw", 96), ("ssd_cb", 24), ("ssd_d", 16), ("ssd_g", 16), ("norm2", 8),
           ("even_g", 8), ("even_cw", 248), ("even_cb", 8), ("ln_g", 8), ("ln_b", 8), ("pool_b", 8),
           ("pool_s", 8), ("odd_g", 8), ("odd_cw", 48), ("odd_cb", 12), ("b_rg", 12), ("b_ig", 12),
           ("lam", 12), ("final_g", 8)]
AT, _n = {}, 0
for _name, _w in COLUMNS:
    AT[_name] = _n
    _n += _w
NCOLS = _n

PHASES = [("iq", 2, 8), ("ik", 1, 8), ("dk", 1, 8), ("kc", 1, 8), ("vc", 1, 8), ("ks", 1, 8), ("kw", 1, 8),
          ("dq", 8, 8), ("nq", 8, 8), ("xbc", 24, 8), ("sz", 16, 8), ("mg", 24, 8),
          ("br_dsa", 8, 8), ("br_nsa", 8, 8), ("br_ssd", 8, 16), ("w_out", 8, 8),
          ("ff1", 32, 8), ("ff2", 8, 32), ("val_glu", 16, 8), ("b_val", 8, 8), ("b_gate", 8, 8),
          ("a_gate", 8, 8), ("pool", 8, 2), ("even_out", 8, 16), ("xr", 12, 8), ("gate", 12, 8),
          ("rg_ig", 24, 1), ("odd_out", 8, 12)]
ON_VECTOR = {"br_dsa", "br_nsa", "br_ssd", "w_out", "ff2", "pool", "even_out", "odd_out"}

PLAIN = {"br_dsa", "br_nsa", "pool", "rg_ig"}

XT, HH, HL, DQ, NQ, SZ, XB, MGA, MGB, XD = 0, 8, 16, 24, 32, 40, 56, 80, 88, 96
KCP, DK, KC, VC, KS, KW = 40, 44, 45, 46, 47, 48
WTOK, HF0 = 56, 69
WCMP = 80
RL, IDX = 96, 100
IQ, IKZ = 112, 114
XW, HST = 112, 116
HF = 116
FFH, FFL, FFR, FFS = 24, 56, 88, 92
UB, VA, TA, AC, GA, GB, BV, DP, YA, YB, YAL, YBL, SQ = 24, 33, 41, 49, 57, 65, 73, 82, 90, 98, 106, 33, 114
XC, U2, TI, GG, LA, R2, W1, LYH, LYL = 24, 36, 48, 60, 72, 84, 96, 36, 72
ARENA = 124


def schedule():
    out = []
    jobs = {name: [("job", name, i) for i in range(n)] for name, n, _ in PHASES}
    out += [("norm", 0)] + [("split", "h0", c) for c in range(8)] + [("tok", 0), ("tok", 1), ("softplus",)]
    for name in ("iq", "ik", "dk", "kc", "vc", "ks", "kw"):
        out += jobs[name]
    out += [("acum",), ("cmp_in",), ("cmp_mm",)]
    norms = list(range(20))
    out += [("qsq", 0), ("qsq", 1), ("qap", 0), ("qsq", 2), ("qap", 1), ("qsq", 3), ("qap", 2)]
    idx = [("idx", i) for i in range(8)]
    big = jobs["dq"] + jobs["nq"]
    for n, job in enumerate(big):
        out.append(job)
        if n % 2 == 1:
            out.append(idx[n // 2])
        if n % 8 == 0 and n:
            out.append(("select", n // 8 - 1))
        if n >= 1:
            out.append(("qsq", n + 3))
            out.append(("qap", n + 2))
    out += [("qsq", 19), ("qap", 18), ("qap", 19), ("select", 1)]
    out += [("vcmp",), ("pcmp", 0), ("pcmp", 1)]
    soft = []
    for i in range(48 + 3):
        s = []
        if i < 48:
            s.append(("sA", i))
        if 1 <= i < 49:
            s.append(("sR", i - 1))
        if 2 <= i < 50:
            s.append(("sB", i - 2))
        if 3 <= i:
            s.append(("sC", i - 3))
        soft.append(s)
    prep = [[("btr",)], [("xtr", 0)], [("xtr", 1)], [("st", 0)], [("xtr", 2)], [("st", 1)], [("xtr", 3)],
            [("st", 2)], [("xtr", 4)], [("st", 3)], [("xtr", 5)], [("xtr", 6)], [("xtr", 7)],
            [("cbt", 0)], [("cbt", 1)]]
    quads = []
    for i in range(16 + 2):
        s = []
        if i < 16:
            s.append(("uA", i))
        if i >= 2:
            s.append(("uB", i - 2))
        quads.append(s)
    filler = soft + prep + quads
    mg = jobs["mg"]
    wide = jobs["xbc"] + jobs["sz"] + mg[0:8] + jobs["br_dsa"] + mg[8:16] + jobs["br_nsa"] + mg[16:24]
    at = 0
    for n, job in enumerate(wide):
        if n == 24:
            out.append(("xsilu", 23))
        out.append(job)
        if job[1] == "xbc":
            out.append(("xconv", job[2]))
            if job[2] >= 1:
                out.append(("xsilu", job[2] - 1))
        want = (n + 1) * len(filler) // (len(wide) - 2)
        while at < min(want, len(filler)):
            out += filler[at]
            at += 1
    while at < len(filler):
        out += filler[at]
        at += 1
    out += [("ynorm",)] + [("split", "y", c) for c in range(16)]
    for c in range(8):
        out += [jobs["br_ssd"][c], ("split", "mix", c)]
    out += jobs["w_out"] + [("norm", 1)] + [("split", "h1", c) for c in range(8)]
    for j in range(34):
        if j < 32:
            out.append(jobs["ff1"][j])
        if 1 <= j < 33:
            out.append(("ffsq", j - 1))
        if j >= 2:
            out.append(("split", "ff", j - 2))
    out += jobs["ff2"]
    out += [("norm", 2)] + [("split", "h2", c) for c in range(8)] + [("pads",)]
    vg = jobs["val_glu"]
    conv = 0
    for c in range(8):
        out += [vg[2 * c], vg[2 * c + 1]]
        if c % 2 == 1:
            out.append(("econv", conv))
            conv += 1
    for c in range(8):
        out += [jobs["b_val"][c], ("winsum", c)]
        if c % 2 == 1:
            out.append(("econv", conv))
            conv += 1
    out += jobs["b_gate"] + jobs["a_gate"]
    for j in range(8):
        out += [jobs["pool"][j], ("split", "yb", j)]
    out += [("ln",)] + [("lnout", c) for c in range(8)]
    out += [("split", "ya", c) for c in range(8)] + jobs["even_out"]
    out += [("norm", 3)] + [("split", "h3", c) for c in range(8)]
    for j in range(12):
        out += [jobs["xr"][j], ("oconv", j)]
    for b in range(3):
        out += jobs["rg_ig"][8 * b:8 * b + 8]
        for j in range(4 * b, 4 * b + 4):
            out += [jobs["gate"][j], ("lru", j)]
    out += [("scan", h) for h in range(12)] + [("split", "ly", c) for c in range(12)]
    out += jobs["odd_out"] + [("norm", 4), ("store",)]
    at, splits = 0, {}
    order = [s for s in out if s[0] == "job"]
    starts = []
    for s in order:
        starts += [s] * {name: k for name, _, k in PHASES}[s[1]]
    units = len(starts) // 8
    for u in range(units):
        if starts[8 * u][1] not in PLAIN:
            splits.setdefault(starts[8 * max(u - AHEAD, 0)], []).append(("wsplit", u))
    final = []
    for s in out:
        final += splits.get(s, []) + [s]
    out = final
    assert len(set(out)) == len(out)
    return out


def psum_tenants(steps):
    turns = {"proj": [], "score": [], "turn": [], "pv": [], "mean": []}
    where = {}

    def add(group, key, readers):
        where[key] = (group, len(turns[group]))
        turns[group].append(readers)

    for s in steps:
        k = s[0]
        if k == "job":
            add("proj", s, "D" if s[1] in ON_VECTOR else "A")
        elif k in ("tok", "cmp_mm", "idx", "cbt", "st"):
            add("score", s, "A")
        elif k in ("sA", "pcmp"):
            add("score", s, "D")
            if k == "pcmp":
                add("turn", ("pcmpT", s[1]), "A")
        elif k == "uA":
            add("score", s, "AD" if s[1] >= 8 else "D")
        elif k in ("vcmp", "sB", "btr"):
            add("turn", s, "A")
        elif k == "xtr":
            add("turn", s, "D")
        elif k == "sC" and (s[1] < 16 or s[1] % 2 == 1):
            add("pv", s, "A")
        elif k == "uB":
            add("pv", s, "D")
        elif k in ("norm", "qsq", "acum", "ynorm"):
            add("mean", s, "A")
        elif k == "ln":
            add("mean", ("ln", 0), "A")
            add("mean", ("ln", 1), "A")
    return where, turns


def program(nc, x_t, w_stream, w_tok, w_cmp, cols, rows, out):
    steps = schedule()
    where, turns = psum_tenants(steps)
    slots = {"proj": 3, "score": 2, "turn": 1, "pv": 1, "mean": 1}

    blocks, first = {}, {}
    at = 0
    order = [s for s in steps if s[0] == "job"]
    for s in order:
        n = next(k for name, _, k in PHASES if name == s[1])
        first[s], blocks[s] = at, n
        at += n
    n_units = at // 8
    assert at % 8 == 0 and w_stream.shape[0] == n_units
    milestone, used, filled_at = 0, {}, {}
    for s in order:
        for b in range(first[s], first[s] + blocks[s]):
            if b % 8 == 7 or b == first[s] + blocks[s] - 1:
                milestone += 1
            if b % 8 == 7:
                used[b // 8] = milestone
        filled_at[s] = milestone

    with ExitStack() as ctx:
        def sb(name, shape):
            return ctx.enter_context(nc.sbuf_tensor(name, shape, F32))

        def psum(name, shape):
            return ctx.enter_context(nc.psum_tensor(name, shape, F32))

        sems = {}

        def sem(name):
            if name not in sems:
                sems[name] = ctx.enter_context(nc.semaphore(name))
            return sems[name]

        def under(name, shape, back):
            return nc.alloc_sbuf_tensor_at(name, shape, F32R, offset=nc.sbuf_base - back)

        arena = sb("arena", [P, ARENA, S])
        arena_r = [under(f"arena_r{c}", [P, 4, S], (ARENA - c) * S * 4) for c in range(0, ARENA, 4)]
        ring = sb("ring", [P, RING, 8, P])
        ring_lo = under("ring_lo", [P, RING, 8, P], RING * 8 * P * 4)
        ring_hi = ctx.enter_context(nc.sbuf_tensor("ring_hi", [P, HIS, 8, P], F32R))
        par = sb("par", [P, NCOLS])
        row = sb("row", [P, 2 * SSD_H])
        tok = sb("tok", [P, NT, TOK])
        sbuf_s = sb("sbuf_s", [P, 4, 512])
        sbuf_t = sb("sbuf_t", [P, 2, 512])
        raw = sb("raw", [P, 3, 3 + S])
        th = sb("th", [P, 3, S])
        sqb = sb("sqb", [P, 2, S])
        root = sb("root", [P, 2, S])
        rinv = sb("rinv", [P, S])
        kk_d = sb("kk_d", [P, 2, S])
        kk_s = sb("kk_s", [P, 2, 2, S])
        kk_w = sb("kk_w", [P, 2, 2, S])
        kk_c = sb("kk_c", [P, 2, 2, N_CMP])
        kcr = sb("kcr", [P, 2, 16])
        vcl = sb("vcl", [P, 4, P])
        pc = sbuf_t[:, 1, :].rearrange("p (h n) -> p h n", n=32)
        ec = sbuf_t[:, 0, 0:256].rearrange("p (h n) -> p h n", n=16)
        pct = arena[:, IQ:IQ + 4, :].rearrange("p (t c) s -> p t (c s)", t=NT)
        bmt = kk_d[:, :, :].rearrange("p a s -> p (a s)").rearrange("p (g n) -> p g n", g=4)
        cbt = kk_s[:, :, :, :].rearrange("p t a s -> p t (a s)")
        caus = sb("caus", [P, NT, S])
        jneg = sb("jneg", [P, P])
        dmask = arena[:, IDX + 2:IDX + 4, :]
        ident = sb("ident", [P, P])
        ones = sb("ones", [P, P])
        mean_d = sb("mean_d", [P, P])
        mean_h = sb("mean_h", [P, P])
        upper = sb("upper", [P, P])
        cneg = sb("cneg", [P, NT, 16])
        cvis = sb("cvis", [P, NT, 16])
        icnt = sb("icnt", [P, 4, 16])
        small = sb("small", [P, 64])
        gates = sb("gates", [P, NT, 48])
        sp = sb("sp", [P, 6, 76])
        dta = sb("dta", [P, 64])
        ea = sb("ea", [P, 32])
        ac = sb("ac", [P, 96])
        dec = sb("dec", [P, 32])
        half = sb("half", [P, 160])
        m8 = sb("m8", [P, 8])
        srow = sb("srow", [P, 4, 8])
        crow = sb("crow", [P, 3, 16])
        ytmp = pct[:, 0, 0:2 * P].rearrange("p (c i) -> p c i", c=2)
        wtmp = kk_w[:, :, :, :].rearrange("p a b s -> p a (b s)")[:, :, 0:272]

        bank = {"proj": [psum(f"p_proj{i}", [P, 512]) for i in range(3)],
                "score": [psum(f"p_score{i}", [P, 512]) for i in range(2)],
                "turn": [psum("p_turn", [P, 512])]}
        bank["pv"] = [psum("p_pv", [P, 512])]
        bank["mean"] = [psum("p_mean", [P, 512])]

        filled = {g: sem(f"{g}_filled") for g in turns}
        read = {(g, e): sem(f"{g}_read_{'act' if e == 'A' else 'dve'}") for g in turns for e in "AD"}
        w_in = [sem(f"w_in{i}") for i in range(RING)]

        def A(c, n=1):
            return arena[:, c, :] if n == 1 else arena[:, c:c + n, :]

        def R(c):
            return arena_r[c // 4][:, c % 4, :]

        def flat(c, n):
            return arena[:, c:c + n, :].rearrange("p c s -> p (c s)")

        wtok = flat(WTOK, 13)[:, 0:8 * TOK].rearrange("p (k n) -> p k n", k=8)
        wcmp = flat(WCMP, 32).rearrange("p (v l e) -> p v l e", v=2, l=32)
        kcp = flat(KCP, 4)[:, 0:2 * 32 * N_CMP].rearrange("p (v l n) -> p v l n", v=2, l=32)
        ikz = arena[:, IKZ:IKZ + 4, :]
        xd = [flat(XD + 8 * t, 8) for t in range(NT)]
        xw, hst = flat(XW, 4), flat(HST, 8)
        ub = flat(UB, 9)[:, 0:8 * (S + 30)].rearrange("p (c s) -> p c s", c=8)
        bv = flat(BV, 9)[:, 0:8 * (S + 16)].rearrange("p (c s) -> p c s", c=8)

        def col(name, i=0):
            return par[:, AT[name] + i:AT[name] + i + 1]

        def slot(key):
            g, n = where[key]
            return bank[g][n % slots[g]][:, 0:256 if g == "mean" else 512]

        def turn(key):
            return where[key][1]

        def readers_done(eng, key):
            g, n = where[key]
            prev = n - slots[g]
            if prev >= 0:
                for e in turns[g][prev]:
                    eng.wait_ge(read[g, e], sum(e in r for r in turns[g][:prev + 1]))

        def was_read(eng, key, reader="A"):
            g, n = where[key]
            eng.wait_ge(read[g, reader], sum(reader in r for r in turns[g][:n + 1]))

        parts = {"y": (lambda c: A(SZ + c), lambda c: R(XB + c), lambda c: R(XD + c), "yf_ready", "P"),
                 "mix": (lambda c: A(MGA + c), lambda c: R(HH + c), lambda c: R(HL + c), "mixf_ready", "P"),
                 "ff": (lambda c: A(FFS + c % 4), lambda c: R(FFH + c), lambda c: R(FFL + c), "ffs_ready", "D"),
                 "ya": (lambda c: A(SQ + c), lambda c: R(YA + c), lambda c: R(YAL + c), "yaf_ready", "P"),
                 "yb": (lambda c: A(GB + c), lambda c: R(YB + c), lambda c: R(YBL + c), "ybf_ready", "P"),
                 "ly": (lambda c: A(GG + c), lambda c: R(LYH + c), lambda c: R(LYL + c), "lyf_ready", "P")}
        for q in range(4):
            src = HF0 if q == 0 else HF
            parts[f"h{q}"] = (lambda c, src=src: A(src + c), lambda c: R(HH + c), lambda c: R(HL + c),
                              "hf_ready", "P")

        def source_count(tag, c):
            return c + 1 + (8 * int(tag[1]) if tag[0] == "h" else 0)

        split_units = [s[1] for s in steps if s[0] == "wsplit"]
        hi_slot = {u: n % HIS for n, u in enumerate(split_units)}
        hi_before = {u: split_units[n - HIS] if n >= HIS else None for n, u in enumerate(split_units)}
        hi_turn = {u: n + 1 for n, u in enumerate(split_units)}
        unit_of = {}
        for s in order:
            for b in range(first[s], first[s] + blocks[s]):
                unit_of.setdefault(b // 8, s[1])

        def on_gpsimd(u):
            n = hi_turn[u]
            return n % 2 == 0

        lo_turn = {}
        for side in (True, False):
            for n, u in enumerate([u for u in split_units if on_gpsimd(u) == side]):
                lo_turn[u] = n + 1

        def remainder(eng, u):
            eng.wait_ge(sem("w_hi_ready"), hi_turn[u])
            return eng.tensor_tensor(ring_lo[:, u % RING, :, :].rearrange("p k n -> p (k n)"),
                                     ring[:, u % RING, :, :].rearrange("p k n -> p (k n)"),
                                     ring_hi[:, hi_slot[u], :, :].rearrange("p k n -> p (k n)").bitcast(F32),
                                     ALU.subtract)

        def part_remainder(eng, tag, c):
            src, hi, lo, _, _ = parts[tag]
            eng.wait_ge(sem(f"hi_{tag}"), c + 1)
            return eng.tensor_tensor(lo(c), src(c), hi(c).bitcast(F32), ALU.subtract)

        qn = [(A(DK), S, "dk_g", 0), (A(KS), S, "nk_g", 1), (A(KW), S, "nk_g", 2),
              (kcr[:, 0, 0:N_CMP], N_CMP, "nk_g", 0)]
        qn += [(A(DQ + c), S, "dq_g", 0) for c in range(8)] + [(A(NQ + c), S, "nq_g", 0) for c in range(8)]

        def soft(i):
            if i < 16:
                return i // 8, i % 8, kk_d[:, :, :], DQ, dmask, TOK_DV, None
            u, kind = (i - 16) // 2, (i - 16) % 2
            t, c = u // 8, u % 8
            g = c // 4
            kk = (kk_w if kind else kk_s)[:, g, :, :]
            return t, c, kk, NQ, caus, (TOK_VW if kind else TOK_VS) + 64 * g, kind + 1

        CONSTS, ZEROS = 6 + 4 * 16, 23

        block = ctx.enter_context(nc.Block())

        @block.sync
        def _(sp_eng):
            sp_eng.dma_start(arena[:, XT:XT + 8, :], x_t).then_inc(sem("x_in"), 16)
            sp_eng.dma_start(par[:, :], cols).then_inc(sem("par_in"), 16)
            sp_eng.dma_start(wtok, w_tok).then_inc(sem("wtok_in"), 16)
            for u in range(n_units):
                if u >= RING:
                    sp_eng.wait_ge(filled["proj"], used[u - RING])
                sp_eng.dma_start(ring[:, u % RING, :, :].rearrange("p k n -> p (k n)"),
                                 w_stream[u]).then_inc(w_in[u % RING], 16)
            sp_eng.wait_ge(sem("hf_ready"), 40)
            sp_eng.dma_start(out, arena[:, HF:HF + 8, :]).then_inc(sem("stored"), 16)
            sp_eng.wait_ge(sem("stored"), 16)

        @block.gpsimd
        def _(pool):
            consts = sem("consts")
            counts, last = {}, []

            def note(semaphore):
                n = str(semaphore.name)
                counts[n] = counts.get(n, 0) + 1
                last[:] = [semaphore, counts[n]]

            def settle():
                if last:
                    pool.wait_ge(*last)

            def link(ins):
                ins.then_inc(sem("pool_chain"), 1)
                note(sem("pool_chain"))
                settle()

            n = [0]

            def const(ins):
                ins.then_inc(consts, 1)
                note(consts)
                n[0] += 1

            pool.wait_ge(sem("zeros"), ZEROS)
            const(pool.affine_select(out=upper[:, :], in_=ones[:, :], compare_op=ALU.is_ge, fill=0.0,
                                     base=0, pattern=[[1, P]], channel_multiplier=-1))
            const(pool.affine_select(out=ident[:, :], in_=ident[:, :], compare_op=ALU.not_equal, fill=1.0,
                                     base=0, pattern=[[-1, P]], channel_multiplier=1))
            const(pool.affine_select(out=caus[:, :, :], in_=caus[:, :, :], compare_op=ALU.is_ge, fill=NEG,
                                     base=0, pattern=[[P, NT], [-1, S]], channel_multiplier=1))
            const(pool.affine_select(out=jneg[:, :], in_=jneg[:, :], compare_op=ALU.is_ge, fill=NEG,
                                     base=0, pattern=[[1, P]], channel_multiplier=-1))
            const(pool.affine_select(out=cneg[:, :, :], in_=cneg[:, :, :], compare_op=ALU.is_ge, fill=NEG,
                                     base=-31, pattern=[[P, NT], [-16, 16]], channel_multiplier=1))
            const(pool.affine_select(out=cvis[:, :, :], in_=cvis[:, :, :], compare_op=ALU.is_ge, fill=0.0,
                                     base=-31, pattern=[[P, NT], [-16, 16]], channel_multiplier=1))
            for g, w in enumerate(WINDOWS):
                for k in range(16):
                    ins = pool.memset(icnt[:, g, k:k + 1], 1.0 / min(k + 1, w))
                    const(ins)
            assert n[0] == CONSTS, n[0]

            for s in steps:
                k = s[0]
                settle()
                if k == "sR":
                    i = s[1]
                    t, c, kk, q, mask, v, gate = soft(i)
                    kl = P * (t + 1)
                    p = sbuf_s[:, i % 4, :].rearrange("p (h k) -> p h k", h=2)[:, :, 0:kl]
                    pool.wait_ge(sem("scale_ready"), i + 1)
                    r = srow[:, i % 4, 6:8]
                    pool.tensor_tensor(p, p, r.unsqueeze(2).to_broadcast([P, 2, kl]), ALU.mult)\
                        .then_inc(sem("p_ready"), 1); note(sem("p_ready"))
                elif k == "xtr" and s[1] < 4:
                    i = s[1]
                    was_read(pool, s, "D")
                    pool.wait_ge(sem("dec_ready"), 1)
                    if i >= 2:
                        was_read(pool, ("st", i - 2))
                    pool.tensor_tensor(
                        xw[:, 512 * (i % 2):512 * (i % 2) + 512].rearrange("p (h e) -> p h e", h=8),
                        xd[0][:, 512 * i:512 * i + 512].rearrange("p (h e) -> p h e", h=8),
                        dec[:, 8 * i:8 * i + 8].unsqueeze(2).to_broadcast([P, 8, 64]), ALU.mult)\
                        .then_inc(sem("xw_ready"), 1); note(sem("xw_ready"))
                elif k == "uA":
                    i = s[1]
                    t, hq = i // 8, i % 8
                    g = hq // 2
                    l = sbuf_s[:, i % 4, :].rearrange("p (h i) -> p h i", h=4)
                    pool.wait_ge(sem("l_ready"), i + 1)
                    if t == 1:
                        e = sbuf_t[:, i % 2, :].rearrange("p (h i) -> p h i", h=4)
                        link(pool.tensor_tensor(e, e, A(XB + 20 + g)[:, P:S].unsqueeze(1).to_broadcast([P, 4, P]),
                                                ALU.mult))
                    if i == 0:
                        was_read(pool, ("cbt", 1))
                    pool.tensor_tensor(
                        l, l, cbt[:, t, P * g:P * g + P].unsqueeze(1).to_broadcast([P, 4, P]),
                        ALU.mult).then_inc(sem("m_ready"), 1); note(sem("m_ready"))
                elif k == "job" and s[1] == "mg":
                    j = s[2]
                    was_read(pool, s)
                    gate = A((MGA if j < 8 else MGB) + j % 8)
                    pool.tensor_scalar(gate, gate, 0.5, 0.5, ALU.mult, ALU.add)\
                        .then_inc(sem("mg_ready"), 1); note(sem("mg_ready"))
                elif k == "wsplit" and on_gpsimd(s[1]):
                    remainder(pool, s[1]).then_inc(sem("w_lo_pool"), 1); note(sem("w_lo_pool"))
                elif k == "split" and parts[s[1]][4] == "P":
                    part_remainder(pool, s[1], s[2]).then_inc(sem(f"lo_{s[1]}"), 1)
                    note(sem(f"lo_{s[1]}"))
                elif k == "pads":
                    was_read(pool, ("job", "ff2", 7), "D")
                    pool.memset(ub[:, :, 0:30], 0.0).then_inc(sem("pads_ready"), 1); note(sem("pads_ready"))
                    pool.memset(bv[:, :, 0:16], 0.0).then_inc(sem("pads_ready"), 1); note(sem("pads_ready"))
                elif k == "winsum":
                    c = s[1]
                    g, w = c // 2, WINDOWS[c // 2]
                    was_read(pool, ("job", "b_val", c))
                    if c == 0:
                        pool.wait_ge(sem("pads_ready"), 2)
                    src, reach, flip = bv[:, c, :], 1, 0
                    while reach < w:
                        dst = wtmp[:, flip, :]
                        lo = 2 * reach - 1
                        link(pool.tensor_tensor(dst[:, lo:272], src[:, lo:272], src[:, lo - reach:272 - reach],
                                                ALU.add))
                        src, reach, flip = dst, 2 * reach, 1 - flip
                    link(pool.tensor_tensor(wtmp[:, flip, 16:32], src[:, 16:32], icnt[:, g, :], ALU.mult))
                    link(pool.tensor_scalar(wtmp[:, flip, 32:272], src[:, 32:272], 1.0 / w, 1.0, ALU.mult, ALU.mult))
                    pool.tensor_tensor(A(DP + c), wtmp[:, flip, 16:272], bv[:, c, 16:272], ALU.subtract)\
                        .then_inc(sem("dp_ready"), 1); note(sem("dp_ready"))
                    pool.wait_ge(sem("dp_ready"), c + 1)

        @block.scalar
        def _(act):
            act.dma_start(row[:, :], rows).then_inc(sem("row_in"), 16)
            act.dma_start(wcmp[0:64, :, :, 0:64], w_cmp).then_inc(sem("wcmp_in"), 16)
            act.dma_start(wcmp[64:128, :, :, 64:128], w_cmp).then_inc(sem("wcmp_in"), 16)
            counts, last = {}, []

            def note(semaphore):
                n = str(semaphore.name)
                counts[n] = counts.get(n, 0) + 1
                last[:] = [semaphore, counts[n]]

            def settle():
                if last:
                    act.wait_ge(*last)

            def link(ins):
                ins.then_inc(sem("act_chain"), 1)
                note(sem("act_chain"))
                settle()

            def take(key):
                act.wait_ge(filled[where[key][0]], turn(key) + 1)
                return slot(key)

            act.wait_ge(sem("zeros"), ZEROS)
            ths = [0]
            for s in steps:
                k = s[0]
                settle()
                if k == "norm":
                    ps = take(s)
                    act.activation(root[:, 0, :], ps, ACT.Sqrt, bias=small[:, 0:1]).then_inc(read["mean", "A"], 1); note(read["mean", "A"])
                elif k == "tok":
                    ps = take(s)
                    act.activation(tok[:, s[1], :], ps[:, 0:TOK], ACT.Copy).then_inc(read["score", "A"], 1); note(read["score", "A"])
                elif k == "softplus":
                    act.wait_ge(read["score", "A"], 2)
                    act.activation(gates[:, :, :], tok[:, :, TOK_NG:TOK_NG + 48], ACT.Tanh, scale=0.5)\
                        .then_inc(sem("gate_tanh"), 1); note(sem("gate_tanh"))
                    act.wait_ge(sem("row_in"), 16)
                    act.activation(ea[:, :], row[:, 32:64], ACT.Exp).then_inc(sem("ea_ready"), 1); note(sem("ea_ready"))
                    act.wait_ge(sem("abs_ready"), 1)
                    act.activation(sp[:, 1, :], sp[:, 1, :], ACT.Exp, scale=-1.0).then_inc(sem("expabs_ready"), 1); note(sem("expabs_ready"))
                elif k == "acum":
                    ps = take(s)
                    act.activation(ac[:, :], ps[:, 0:96], ACT.Copy).then_inc(read["mean", "A"], 1); note(read["mean", "A"])
                    act.wait_ge(sem("decarg_ready"), 1)
                    act.activation(dec[:, :], dec[:, :], ACT.Exp).then_inc(sem("dec_ready"), 1); note(sem("dec_ready"))
                elif k == "cmp_mm":
                    ps = take(s)
                    act.activation(kcr[:, 0, 0:N_CMP], ps[:, 0:N_CMP], ACT.Copy)
                    act.activation(kcr[:, 1, 0:N_CMP], ps[:, 256:256 + N_CMP], ACT.Copy)\
                        .then_inc(read["score", "A"], 1); note(read["score", "A"])
                elif k == "qsq":
                    i = s[1]
                    ps = take(s)
                    act.activation(root[:, i % 2, 0:qn[i][1]], ps[:, 0:qn[i][1]], ACT.Sqrt, bias=small[:, 0:1])\
                        .then_inc(read["mean", "A"], 1); note(read["mean", "A"])
                elif k == "idx":
                    i = s[1]
                    kl = P * (i // 4 + 1)
                    ps = take(s).rearrange("p (h k) -> p h k", h=2)[:, :, 0:kl]
                    if i >= 2:
                        act.wait_ge(sem("rl_used"), i - 1)
                    act.activation(arena[:, RL + 2 * (i % 2):RL + 2 * (i % 2) + 2, 0:kl], ps, ACT.Relu)\
                        .then_inc(read["score", "A"], 1); note(read["score", "A"])
                elif k == "vcmp":
                    ps = take(s)
                    for b in range(2):
                        for g in range(2):
                            for h in range(2):
                                r = 32 * (2 * b + h)
                                ins = act.activation(vcl[r:r + N_CMP, 2 * b + g, 64 * h:64 * h + 64],
                                                     ps[0:N_CMP, 64 * g:64 * g + 64], ACT.Copy)
                    ins.then_inc(read["turn", "A"], 1); note(read["turn", "A"])
                elif k == "pcmp":
                    t = s[1]
                    act.wait_ge(sem("carg_ready"), t + 1)
                    act.activation(ec[:, :, 0:N_CMP], ec[:, :, 0:N_CMP], ACT.Exp, scale=SCALE)\
                        .then_inc(sem("ce_ready"), 1); note(sem("ce_ready"))
                    ps = take(("pcmpT", t))
                    act.activation(pct[:, t, :], ps, ACT.Copy).then_inc(read["turn", "A"], 1); note(read["turn", "A"])
                elif k == "sA":
                    i = s[1]
                    t = soft(i)[0]
                    kl = P * (t + 1)
                    act.wait_ge(sem("nmax_ready"), i + 1)
                    for h in range(2):
                        p = sbuf_s[:, i % 4, 256 * h:256 * h + kl]
                        ins = act.activation(p, p, ACT.Exp, bias=srow[:, i % 4, 2 + h:3 + h], scale=SCALE,
                                             accum_out=srow[:, i % 4, 4 + h:5 + h])
                    ins.then_inc(sem("e_ready"), 1); note(sem("e_ready"))
                elif k == "sB":
                    i = s[1]
                    t = soft(i)[0]
                    ps = take(s)
                    if i >= 2:
                        act.wait_ge(sem("pv_done"), i - 1)
                    act.activation(sbuf_t[:, i % 2, 0:256 * (t + 1)], ps[:, 0:256 * (t + 1)], ACT.Copy)\
                        .then_inc(read["turn", "A"], 1); note(read["turn", "A"])
                elif k == "sC" and s in where:
                    i = s[1]
                    t, c, _, q, _, _, _ = soft(i)
                    act.wait_ge(sem("pv_done"), i + 1)
                    act.activation(A(q + c)[:, P * t:P * t + P], slot(s)[:, 0:P], ACT.Copy)\
                        .then_inc(read["pv", "A"], 1); note(read["pv", "A"])
                elif k == "xsilu":
                    j = s[1]
                    act.wait_ge(sem("conv_done"), j + 1)
                    if j >= 3:
                        act.wait_ge(sem("silu_done"), j - 2)
                    act.activation(th[:, j % 3, :], A(XB + j), ACT.Tanh).then_inc(sem("xtanh"), 1); note(sem("xtanh"))
                elif k == "btr":
                    ps = take(s)
                    act.activation(bmt[:, :, :].rearrange("p g n -> p (g n)"), ps, ACT.Copy)\
                        .then_inc(read["turn", "A"], 1); note(read["turn", "A"])
                elif k == "cbt":
                    ps = take(s)
                    act.activation(cbt[:, s[1], :], ps, ACT.Copy).then_inc(read["score", "A"], 1); note(read["score", "A"])
                elif k == "st":
                    g = s[1]
                    ps = take(s)
                    act.activation(hst[:, 512 * g:512 * g + 512], ps, ACT.Copy).then_inc(read["score", "A"], 1); note(read["score", "A"])
                elif k == "uA":
                    i = s[1]
                    if i >= 8:
                        ps = take(s)
                        was_read(act, s, "D")
                        if i == 8:
                            act.wait_ge(sem("pv_done"), 48)
                        elif i >= 10:
                            act.wait_ge(sem("pv_done"), 48 + i - 1)
                        act.activation(sbuf_t[:, i % 2, :], ps, ACT.Exp).then_inc(read["score", "A"], 1); note(read["score", "A"])
                    act.wait_ge(sem("seg_ready"), i + 1)
                    l = sbuf_s[:, i % 4, :]
                    act.activation(l, l, ACT.Exp).then_inc(sem("l_ready"), 1); note(sem("l_ready"))
                elif k == "wsplit":
                    u = s[1]
                    act.wait_ge(w_in[u % RING], 16 * (u // RING + 1))
                    if hi_before[u] is not None:
                        act.wait_ge(filled["proj"], used[hi_before[u]])
                    act.activation(ring_hi[:, hi_slot[u], :, :].rearrange("p k n -> p (k n)"),
                                   ring[:, u % RING, :, :].rearrange("p k n -> p (k n)"), ACT.Copy)\
                        .then_inc(sem("w_hi_ready"), 1); note(sem("w_hi_ready"))
                elif k == "split":
                    _, tag, c = s
                    src, hi, lo, ready, _ = parts[tag]
                    act.wait_ge(sem(ready), source_count(tag, c))
                    act.activation(hi(c), src(c), ACT.Copy).then_inc(sem(f"hi_{tag}"), 1)
                    note(sem(f"hi_{tag}"))
                elif k == "ynorm":
                    ps = take(s)
                    act.activation(root[:, 0, :], ps, ACT.Sqrt, bias=small[:, 0:1], scale=0.5).then_inc(read["mean", "A"], 1); note(read["mean", "A"])
                elif k == "ln":
                    ps = take(("ln", 0))
                    act.activation(root[:, 1, :], ps, ACT.Copy).then_inc(read["mean", "A"], 1); note(read["mean", "A"])
                    ps = take(("ln", 1))
                    act.activation(root[:, 0, :], ps, ACT.Sqrt, bias=small[:, 1:2]).then_inc(read["mean", "A"], 1); note(read["mean", "A"])
                elif k == "lnout":
                    c = s[1]
                    act.wait_ge(sem("ln_z"), c + 1)
                    link(act.activation(A(AC + c), A(AC + c), ACT.Identity, bias=half[:, 8 + c:9 + c],
                                        scale=half[:, c:c + 1]))
                    act.activation(A(SQ + c), A(AC + c), ACT.Tanh).then_inc(sem("ln_tanh"), 1); note(sem("ln_tanh"))
                elif k == "scan":
                    h = s[1]
                    act.wait_ge(sem("r2_ready"), h + 1)
                    act.activation(A(U2 + h), A(U2 + h), ACT.Sqrt).then_inc(sem("usqrt"), 1); note(sem("usqrt"))
                elif k == "job" and s[1] not in ON_VECTOR:
                    _, name, j = s
                    act.wait_ge(filled["proj"], filled_at[s])
                    ps = slot(s)[:, 0:S]
                    done = read["proj", "A"]
                    if name == "iq":
                        act.activation(A(IQ + j), ps, ACT.Copy).then_inc(done, 1); note(done)
                    elif name == "ik":
                        for a in range(4):
                            ins = act.activation(ikz[32 * a:32 * a + 32, a, :], ps[32 * a:32 * a + 32, :], ACT.Copy)
                        ins.then_inc(done, 1); note(done)
                    elif name in ("dk", "kc", "vc", "ks", "kw"):
                        to = {"dk": DK, "kc": KC, "vc": VC, "ks": KS, "kw": KW}[name]
                        act.activation(A(to), ps, ACT.Copy).then_inc(done, 1); note(done)
                    elif name in ("dq", "nq"):
                        act.activation(A((DQ if name == "dq" else NQ) + j), ps, ACT.Copy).then_inc(done, 1); note(done)
                    elif name in ("xbc", "xr"):
                        n = j if name == "xbc" else 24 + j
                        if n >= 3:
                            act.wait_ge(sem("conv_done"), n - 2)
                        act.activation(raw[:, n % 3, 3:3 + S], ps, ACT.Copy).then_inc(done, 1); note(done)
                    elif name == "mg":
                        if j >= 16:
                            was_read(act, ("job", "br_nsa", j - 16), "D")
                        act.activation(A((MGA if j < 8 else MGB) + j % 8), ps, ACT.Tanh, scale=0.5).then_inc(done, 1); note(done)
                    elif name == "ff1":
                        if j >= 4:
                            act.wait_ge(sem("ffs_ready"), j - 3)
                        act.activation(A(FFR + j % 4), ps, ACT.Relu).then_inc(done, 1); note(done)
                    elif name == "val_glu":
                        c = j // 2
                        if j % 2 == 0:
                            act.activation(A(VA + c), ps, ACT.Copy, scale=0.5).then_inc(done, 1); note(done)
                        else:
                            act.activation(A(TA + c), ps, ACT.Tanh, scale=0.5).then_inc(done, 1); note(done)
                    elif name == "b_val":
                        if j == 0:
                            act.wait_ge(sem("pads_ready"), 2)
                        act.activation(bv[:, j, 16:16 + S], ps, ACT.Copy).then_inc(done, 1); note(done)
                    elif name in ("sz", "a_gate", "b_gate", "gate"):
                        to = {"sz": SZ, "a_gate": GA, "b_gate": GB, "gate": GG}[name]
                        if name == "sz" and j == 0:
                            act.wait_ge(sem("kk_ready"), 4)
                        act.activation(A(to + j), ps, ACT.Copy, scale=0.5)
                        b = ths[0]
                        ths[0] += 1
                        if b == 0:
                            act.wait_ge(sem("silu_done"), 24)
                        if b >= 3:
                            act.wait_ge(sem("gated"), b - 2)
                        act.activation(th[:, b % 3, :], ps, ACT.Tanh, scale=0.5).then_inc(done, 1); note(done)
                    elif name == "rg_ig":
                        h = j // 2
                        if j % 2 == 0:
                            link(act.activation(A(U2 + h), ps, ACT.Tanh, bias=half[:, 16 + h:17 + h], scale=0.5))
                            act.activation(A(U2 + h), A(U2 + h), ACT.Tanh, bias=half[:, 40 + h:41 + h],
                                           scale=half[:, 40 + h:41 + h]).then_inc(done, 1); note(done)
                        else:
                            act.activation(A(TI + h), ps, ACT.Tanh, bias=half[:, 28 + h:29 + h], scale=0.5)\
                                .then_inc(done, 1); note(done)

        @block.vector
        def _(dve):
            counts, last = {}, []

            def note(semaphore):
                n = str(semaphore.name)
                counts[n] = counts.get(n, 0) + 1
                last[:] = [semaphore, counts[n]]

            def settle():
                if last:
                    dve.wait_ge(*last)

            def link(ins):
                ins.then_inc(sem("dve_chain"), 1)
                note(sem("dve_chain"))
                settle()

            def take(key):
                dve.wait_ge(filled[where[key][0]], turn(key) + 1)
                return slot(key)


            zeros = [0]

            def fill(ap, value):
                dve.memset(ap, value).then_inc(sem("zeros"), 1)
                note(sem("zeros"))
                zeros[0] += 1

            fill(mean_d[:, :], 1.0 / D)
            fill(small[:, 0:1], 1e-6)
            fill(small[:, 1:2], 1e-5)
            fill(ones[:, :], 1.0)
            fill(ident[:, :], 0.0)
            fill(caus[:, :, :], 0.0)
            fill(jneg[:, :], 0.0)
            fill(cneg[:, :, :], 0.0)
            fill(cvis[:, :, :], 1.0)
            fill(mean_h[:, 0:64], 0.0)
            fill(mean_h[:, 64:128], 0.0)
            dve.wait_ge(sem("zeros"), zeros[0])
            fill(mean_h[0:64, 0:64], 1.0 / HD)
            fill(mean_h[64:128, 64:128], 1.0 / HD)
            for tile in (kk_d, kk_s, kk_w, kk_c, vcl, sbuf_t, raw):
                fill(tile[:], 0.0)
            fill(ikz, 0.0)
            fill(wcmp[0:64, :, :, 64:128], 0.0)
            fill(wcmp[64:128, :, :, 0:64], 0.0)
            assert zeros[0] == ZEROS
            dve.wait_ge(sem("zeros"), ZEROS)
            dve.wait_ge(sem("consts"), CONSTS)
            dve.wait_ge(sem("par_in"), 16)
            link(dve.tensor_scalar(half[:, 0:16], par[:, AT["ln_g"]:AT["ln_g"] + 16], 0.5, None, ALU.mult))
            link(dve.tensor_scalar(half[:, 16:40], par[:, AT["b_rg"]:AT["b_rg"] + 24], 0.5, None, ALU.mult))
            link(dve.tensor_scalar(half[:, 64:160], par[:, AT["ssd_cw"]:AT["ssd_cw"] + 96], 0.5, None, ALU.mult))
            link(dve.tensor_scalar(par[:, AT["ssd_cb"]:AT["ssd_cb"] + 24], par[:, AT["ssd_cb"]:AT["ssd_cb"] + 24],
                                   0.5, None, ALU.mult))
            sq = sem("sq_ready")
            ths = [0]
            for s in steps:
                k = s[0]
                settle()
                if k == "norm":
                    q = s[1]
                    h = HF0 if q == 0 else HF
                    if q == 0:
                        dve.wait_ge(sem("x_in"), 16)
                    for c in range(8):
                        dve.tensor_tensor(A(h + c), A(XT + c), A(XT + c), ALU.mult).then_inc(sq, 1); note(sq)
                    was_read(dve, s)
                    link(dve.reciprocal(rinv[:, :], root[:, 0, :]))
                    g = ("norm1", "norm2", "even_g", "odd_g", "final_g")[q]
                    for c in range(8):
                        dve.scalar_tensor_tensor(out=A(h + c), in0=A(XT + c), scalar=col(g, c), in1=rinv[:, :],
                                                 op0=ALU.mult, op1=ALU.mult).then_inc(sem("hf_ready"), 1)
                        note(sem("hf_ready"))
                elif k == "wsplit" and not on_gpsimd(s[1]):
                    remainder(dve, s[1]).then_inc(sem("w_lo_dve"), 1); note(sem("w_lo_dve"))
                elif k == "split" and parts[s[1]][4] == "D":
                    part_remainder(dve, s[1], s[2]).then_inc(sem(f"lo_{s[1]}"), 1)
                    note(sem(f"lo_{s[1]}"))
                elif k == "ffsq":
                    j = s[1]
                    was_read(dve, ("job", "ff1", j))
                    if j >= 4:
                        dve.wait_ge(sem("hi_ff"), j - 3)
                    dve.tensor_tensor(A(FFS + j % 4), A(FFR + j % 4), A(FFR + j % 4), ALU.mult)\
                        .then_inc(sem("ffs_ready"), 1); note(sem("ffs_ready"))
                elif k == "softplus":
                    was_read(dve, ("tok", 1))
                    dve.wait_ge(sem("row_in"), 16)
                    for t in range(NT):
                        dve.tensor_tensor(sp[:, 0, 32 * t:32 * t + 32], tok[:, t, TOK_DT:TOK_DT + 32], row[:, 0:32],
                                          ALU.add)
                    link(dve.tensor_scalar(sp[:, 0, 64:76], par[:, AT["lam"]:AT["lam"] + 12], -1.0, None, ALU.mult))
                    dve.scalar_tensor_tensor(out=sp[:, 1, :], in0=sp[:, 0, :], scalar=-1.0, in1=sp[:, 0, :],
                                             op0=ALU.mult, op1=ALU.max)\
                        .then_inc(sem("abs_ready"), 1); note(sem("abs_ready"))
                    dve.wait_ge(sem("gate_tanh"), 1)
                    dve.tensor_scalar(gates[:, :, :], gates[:, :, :], 0.5, 0.5, ALU.mult, ALU.add)\
                        .then_inc(sem("gates_ready"), 1); note(sem("gates_ready"))
                    z, y, y2, acc = sp[:, 1, :], sp[:, 2, :], sp[:, 3, :], sp[:, 4, :]
                    dve.wait_ge(sem("expabs_ready"), 1)
                    link(dve.tensor_scalar(y2, z, 2.0, None, ALU.add))
                    link(dve.reciprocal(y, y2))
                    link(dve.tensor_tensor(y, y, z, ALU.mult))
                    link(dve.tensor_tensor(y2, y, y, ALU.mult))
                    link(dve.tensor_scalar(acc, y2, 1.0 / 17, None, ALU.mult))
                    for m in (15, 13, 11, 9, 7, 5, 3):
                        link(dve.scalar_tensor_tensor(out=acc, in0=acc, scalar=1.0 / m, in1=y2,
                                                      op0=ALU.add, op1=ALU.mult))
                    link(dve.scalar_tensor_tensor(out=acc, in0=acc, scalar=1.0, in1=y, op0=ALU.add, op1=ALU.mult))
                    link(dve.tensor_scalar(y, sp[:, 0, :], 0.0, None, ALU.max))
                    link(dve.scalar_tensor_tensor(out=sp[:, 5, :], in0=acc, scalar=2.0, in1=y,
                                                  op0=ALU.mult, op1=ALU.add))
                    link(dve.tensor_scalar(half[:, 40:52], sp[:, 5, 64:76], 2.0, None, ALU.mult))
                    dve.wait_ge(sem("ea_ready"), 1)
                    for t in range(NT):
                        dve.scalar_tensor_tensor(out=dta[:, 32 * t:32 * t + 32], in0=sp[:, 5, 32 * t:32 * t + 32],
                                                 scalar=-1.0, in1=ea[:, :], op0=ALU.mult, op1=ALU.mult)\
                            .then_inc(sem("dta_ready"), 1); note(sem("dta_ready"))
                elif k == "acum":
                    was_read(dve, s)
                    dve.tensor_tensor(dec[:, :], ac[:, 64:96], ac[:, 0:32], ALU.subtract)\
                        .then_inc(sem("decarg_ready"), 1); note(sem("decarg_ready"))
                elif k == "cmp_in":
                    for v, src in ((0, KC), (1, VC)):
                        was_read(dve, ("job", ("kc", "vc")[v], 0))
                        view = A(src).rearrange("p (m b) -> p b m", b=16)
                        for a in range(2):
                            pos = par[:, AT["cmp_pos"] + 32 * v + 16 * a:AT["cmp_pos"] + 32 * v + 16 * a + 16]
                            dve.tensor_tensor(kcp[:, v, 16 * a:16 * a + 16, :], view[:, :, a:a + N_CMP],
                                              pos.unsqueeze(2).to_broadcast([P, 16, N_CMP]), ALU.add)\
                                .then_inc(sem("kcp_ready"), 1); note(sem("kcp_ready"))
                elif k == "qsq":
                    i = s[1]
                    src, w, _, _ = qn[i]
                    job = {0: "dk", 1: "ks", 2: "kw"}.get(i)
                    if i == 3:
                        was_read(dve, ("cmp_mm",))
                    else:
                        was_read(dve, ("job", job, 0) if job else ("job", "dq" if i < 12 else "nq", (i - 4) % 8))
                    dve.tensor_tensor(sqb[:, i % 2, 0:w], src, src, ALU.mult).then_inc(sem("qsq_ready"), 1); note(sem("qsq_ready"))
                elif k == "qap":
                    i = s[1]
                    src, w, gain, gi = qn[i]
                    was_read(dve, ("qsq", i))
                    link(dve.reciprocal(rinv[:, 0:w], root[:, i % 2, 0:w]))
                    if i >= 4:
                        dve.scalar_tensor_tensor(out=src, in0=src, scalar=col(gain), in1=rinv[:, 0:w],
                                                 op0=ALU.mult, op1=ALU.mult).then_inc(sem("q_ready"), 1); note(sem("q_ready"))
                    else:
                        kk = (kk_d, kk_s, kk_w, kk_c)[i]
                        for half_in in range(2):
                            a = 64 * half_in
                            for half_out in ((half_in,) if i == 0 else (0, 1)):
                                b = 64 * half_out
                                dst = kk[b:b + 64, half_out, :] if i == 0 else kk[b:b + 64, half_in, half_out, :]
                                ins = dve.scalar_tensor_tensor(
                                    out=dst, in0=src[a:a + 64], scalar=col(gain, gi)[a:a + 64],
                                    in1=rinv[a:a + 64, 0:w], op0=ALU.mult, op1=ALU.mult)
                        ins.then_inc(sem("kk_ready"), 1); note(sem("kk_ready"))
                elif k == "idx":
                    i = s[1]
                    t = i // 4
                    kl = P * (t + 1)
                    was_read(dve, s)
                    for h in range(2):
                        head = 2 * (i % 4) + h
                        rl = arena[:, RL + 2 * (i % 2) + h, 0:kl]
                        iw = tok[:, t, TOK_IW + head:TOK_IW + head + 1]
                        acc = A(IDX + t)[:, 0:kl]
                        if head == 0:
                            ins = dve.tensor_scalar(acc, rl, iw, None, ALU.mult)
                        else:
                            ins = dve.scalar_tensor_tensor(out=acc, in0=rl, scalar=iw, in1=acc,
                                                           op0=ALU.mult, op1=ALU.add)
                        if h == 0:
                            link(ins)
                    ins.then_inc(sem("rl_used"), 1); note(sem("rl_used"))
                    dve.wait_ge(sem("rl_used"), i + 1)
                elif k == "select":
                    t = s[1]
                    kl = P * (t + 1)
                    acc = A(IDX + t)[:, 0:kl]
                    link(dve.tensor_tensor(acc, acc, caus[:, t, 0:kl], ALU.add))
                    for _ in range(TOPK // 8):
                        link(dve.max(m8[:, :], acc))
                        link(dve.match_replace(acc, m8[:, :], acc, MARK))
                    link(dve.tensor_scalar(acc, acc, MARK, 1.0, ALU.is_equal, ALU.subtract))
                    dve.scalar_tensor_tensor(out=dmask[:, t, 0:kl], in0=acc, scalar=-NEG, in1=caus[:, t, 0:kl],
                                             op0=ALU.mult, op1=ALU.add).then_inc(sem("select_done"), 1); note(sem("select_done"))
                    dve.wait_ge(sem("select_done"), t + 1)
                elif k == "pcmp":
                    t = s[1]
                    ps = take(s)[:, 0:16 * N_CMP].rearrange("p (h n) -> p h n", h=16)
                    e = ec[:, :, 0:N_CMP]
                    dve.tensor_tensor(e, ps, cneg[:, t, 0:N_CMP].unsqueeze(1).to_broadcast([P, 16, N_CMP]),
                                      ALU.add).then_inc(read["score", "D"], 1); note(read["score", "D"])
                    dve.wait_ge(read["score", "D"], sum("D" in r for r in turns["score"][:turn(s) + 1]))
                    link(dve.tensor_reduce(crow[:, 0, :], e, AX.X, ALU.max))
                    dve.tensor_tensor(e, e, crow[:, 0, :].unsqueeze(2).to_broadcast([P, 16, N_CMP]),
                                      ALU.subtract).then_inc(sem("carg_ready"), 1); note(sem("carg_ready"))
                    dve.wait_ge(sem("ce_ready"), t + 1)
                    link(dve.tensor_reduce(crow[:, 1, :], e, AX.X, ALU.add))
                    link(dve.reciprocal(crow[:, 2, :], crow[:, 1, :]))
                    link(dve.tensor_tensor(crow[:, 2, :], crow[:, 2, :],
                                           gates[:, t, :].rearrange("p (h j) -> p h j", j=3)[:, :, 0], ALU.mult))
                    link(dve.tensor_tensor(e, e, cvis[:, t, 0:N_CMP].unsqueeze(1).to_broadcast([P, 16, N_CMP]),
                                           ALU.mult))
                    if t == 1:
                        dve.wait_ge(filled["turn"], turn(("pcmpT", 0)) + 1)
                    dve.tensor_tensor(pc[:, :, 0:N_CMP], e, crow[:, 2, :].unsqueeze(2).to_broadcast([P, 16, N_CMP]),
                                      ALU.mult).then_inc(sem("pc_ready"), 1); note(sem("pc_ready"))
                elif k == "sA":
                    i = s[1]
                    t, c, kk, q, mask, v, gate = soft(i)
                    kl = P * (t + 1)
                    ps = take(s).rearrange("p (h k) -> p h k", h=2)[:, :, 0:kl]
                    x = sbuf_s[:, i % 4, :].rearrange("p (h k) -> p h k", h=2)[:, :, 0:kl]
                    if i >= 4:
                        dve.wait_ge(filled["turn"], turn(("sB", i - 4)) + 1)
                    dve.tensor_tensor(x, ps, mask[:, t, 0:kl].unsqueeze(1).to_broadcast([P, 2, kl]), ALU.add)\
                        .then_inc(read["score", "D"], 1); note(read["score", "D"])
                    dve.wait_ge(read["score", "D"], sum("D" in r for r in turns["score"][:turn(s) + 1]))
                    link(dve.tensor_reduce(srow[:, i % 4, 0:2], x, AX.X, ALU.max))
                    dve.tensor_scalar(srow[:, i % 4, 2:4], srow[:, i % 4, 0:2], -SCALE, None, ALU.mult)\
                        .then_inc(sem("nmax_ready"), 1); note(sem("nmax_ready"))
                elif k == "sR":
                    i = s[1]
                    t, c, _, _, _, _, gate = soft(i)
                    dve.wait_ge(sem("e_ready"), i + 1)
                    ins = dve.reciprocal(srow[:, i % 4, 6:8], srow[:, i % 4, 4:6])
                    if gate is not None:
                        link(ins)
                        gt = gates[:, t, :].rearrange("p (h j) -> p h j", j=3)[:, 2 * c:2 * c + 2, gate]
                        ins = dve.tensor_tensor(srow[:, i % 4, 6:8], srow[:, i % 4, 6:8], gt, ALU.mult)
                    ins.then_inc(sem("scale_ready"), 1); note(sem("scale_ready"))
                elif k in ("xconv", "oconv"):
                    j = s[1]
                    n = j if k == "xconv" else 24 + j
                    was_read(dve, ("job", "xbc" if k == "xconv" else "xr", j))
                    dst = A((XB if k == "xconv" else XC) + j)
                    for tap in range(4):
                        w = half[:, 64 + 4 * j + tap:65 + 4 * j + tap] if k == "xconv" else col("odd_cw", 4 * j + tap)
                        src = raw[:, n % 3, tap:tap + S]
                        if tap == 0:
                            link(dve.tensor_scalar(dst, src, w, col("ssd_cb" if k == "xconv" else "odd_cb", j),
                                                   ALU.mult, ALU.add))
                        else:
                            ins = dve.scalar_tensor_tensor(out=dst, in0=src, scalar=w, in1=dst,
                                                           op0=ALU.mult, op1=ALU.add)
                            if tap < 3:
                                link(ins)
                    ins.then_inc(sem("conv_done"), 1); note(sem("conv_done"))
                elif k == "xsilu":
                    j = s[1]
                    dve.wait_ge(sem("xtanh"), j + 1)
                    dve.scalar_tensor_tensor(out=A(XB + j), in0=th[:, j % 3, :], scalar=1.0, in1=A(XB + j),
                                             op0=ALU.add, op1=ALU.mult).then_inc(sem("silu_done"), 1); note(sem("silu_done"))
                elif k == "xtr":
                    i = s[1]
                    t, q = i // 4, i % 4
                    ps = take(s)
                    dve.tensor_tensor(
                        xd[t][:, 512 * q:512 * q + 512].rearrange("p (h e) -> p h e", h=8),
                        ps[:, :].rearrange("p (h e) -> p h e", h=8),
                        sp[:, 5, 32 * t + 8 * q:32 * t + 8 * q + 8].unsqueeze(2).to_broadcast([P, 8, 64]),
                        ALU.mult).then_inc(read["turn", "D"], 1); note(read["turn", "D"])
                elif k == "uA":
                    i = s[1]
                    t, hq = i // 8, i % 8
                    ps = take(s).rearrange("p (h i) -> p h i", h=4)
                    x = sbuf_s[:, i % 4, :].rearrange("p (h i) -> p h i", h=4)
                    if i >= 4:
                        dve.wait_ge(sem("pv_done"), 48 + i - 3)
                    else:
                        dve.wait_ge(sem("pv_done"), 48)
                    dve.tensor_tensor(x, ps, ac[:, 32 * t + 4 * hq:32 * t + 4 * hq + 4].unsqueeze(2)
                                      .to_broadcast([P, 4, P]), ALU.subtract).then_inc(read["score", "D"], 1); note(read["score", "D"])
                    dve.wait_ge(read["score", "D"], sum("D" in r for r in turns["score"][:turn(s) + 1]))
                    dve.tensor_tensor(x, x, jneg[:, :].unsqueeze(1).to_broadcast([P, 4, P]), ALU.add)\
                        .then_inc(sem("seg_ready"), 1); note(sem("seg_ready"))
                elif k == "uB":
                    i = s[1]
                    t, hq = i // 8, i % 8
                    dve.wait_ge(sem("pv_done"), 48 + i + 1)
                    ps = slot(s)
                    if i == 0:
                        dve.wait_ge(sem("gated"), 16)
                    for cc in range(2):
                        c = 2 * hq + cc
                        xs = A(XB + c)[:, P * t:P * t + P]
                        ins = dve.scalar_tensor_tensor(out=ytmp[:, cc, :], in0=xs, scalar=col("ssd_d", c),
                                                       in1=ps[:, P * cc:P * cc + P], op0=ALU.mult, op1=ALU.add)
                    ins.then_inc(read["pv", "D"], 1); note(read["pv", "D"])
                    dve.wait_ge(read["pv", "D"], i + 1)
                    for cc in range(2):
                        c = 2 * hq + cc
                        ins = dve.tensor_tensor(A(XB + c)[:, P * t:P * t + P], ytmp[:, cc, :],
                                                A(SZ + c)[:, P * t:P * t + P], ALU.mult)
                    link(ins)
                elif k == "ynorm":
                    for c in range(16):
                        dve.tensor_tensor(A(XD + c), A(XB + c), A(XB + c), ALU.mult).then_inc(sem("ysq_ready"), 1); note(sem("ysq_ready"))
                    was_read(dve, s)
                    link(dve.reciprocal(rinv[:, :], root[:, 0, :]))
                    for c in range(16):
                        dve.scalar_tensor_tensor(out=A(SZ + c), in0=A(XB + c), scalar=col("ssd_g", c),
                                                 in1=rinv[:, :], op0=ALU.mult, op1=ALU.mult)\
                            .then_inc(sem("yf_ready"), 1); note(sem("yf_ready"))
                elif k == "econv":
                    c = s[1]
                    was_read(dve, ("job", "val_glu", 2 * c + 1))
                    if c == 0:
                        dve.wait_ge(sem("pads_ready"), 2)
                    link(dve.scalar_tensor_tensor(out=ub[:, c, 30:30 + S], in0=A(TA + c), scalar=1.0, in1=A(VA + c),
                                                  op0=ALU.add, op1=ALU.mult))
                    dst = A(AC + c)
                    link(dve.tensor_scalar(dst, ub[:, c, 0:S], col("even_cw", CONV_K * c), col("even_cb", c),
                                           ALU.mult, ALU.add))
                    for tap in range(1, CONV_K):
                        ins = dve.scalar_tensor_tensor(out=dst, in0=ub[:, c, tap:tap + S],
                                                       scalar=col("even_cw", CONV_K * c + tap), in1=dst,
                                                       op0=ALU.mult, op1=ALU.add)
                        if tap < CONV_K - 1:
                            link(ins)
                    ins.then_inc(sem("econv_done"), 1); note(sem("econv_done"))
                elif k == "ln":
                    was_read(dve, ("ln", 0))
                    dve.wait_ge(sem("econv_done"), 8)
                    for c in range(8):
                        ins = dve.tensor_tensor(A(AC + c), A(AC + c), root[:, 1, :], ALU.subtract)
                    link(ins)
                    for c in range(8):
                        dve.tensor_tensor(A(SQ + c), A(AC + c), A(AC + c), ALU.mult).then_inc(sem("lsq_ready"), 1); note(sem("lsq_ready"))
                    was_read(dve, ("ln", 1))
                    link(dve.reciprocal(rinv[:, :], root[:, 0, :]))
                    for c in range(8):
                        dve.tensor_tensor(A(AC + c), A(AC + c), rinv[:, :], ALU.mult).then_inc(sem("ln_z"), 1); note(sem("ln_z"))
                elif k == "lnout":
                    c = s[1]
                    dve.wait_ge(sem("ln_tanh"), c + 1)
                    link(dve.scalar_tensor_tensor(out=A(SQ + c), in0=A(SQ + c), scalar=1.0, in1=A(AC + c),
                                                  op0=ALU.add, op1=ALU.mult))
                    dve.tensor_tensor(A(SQ + c), A(SQ + c), A(GA + c), ALU.mult)\
                        .then_inc(sem("yaf_ready"), 1); note(sem("yaf_ready"))
                elif k == "lru":
                    h = s[1]
                    was_read(dve, ("job", "rg_ig", 2 * h + 1))
                    link(dve.tensor_scalar(A(LA + h), A(U2 + h), 1.0, None, ALU.add))
                    dve.reciprocal(A(R2 + h), A(LA + h)).then_inc(sem("r2_ready"), 1); note(sem("r2_ready"))
                    dve.wait_ge(sem("r2_ready"), h + 1)
                    dve.tensor_scalar(A(LA + h), A(R2 + h), 2.0, -1.0, ALU.mult, ALU.add)
                    link(dve.scalar_tensor_tensor(out=A(W1 + h), in0=A(TI + h), scalar=1.0, in1=A(XC + h),
                                                  op0=ALU.add, op1=ALU.mult))
                elif k == "scan":
                    h = s[1]
                    dve.wait_ge(sem("usqrt"), h + 1)
                    link(dve.tensor_tensor(A(R2 + h), A(R2 + h), A(U2 + h), ALU.mult))
                    link(dve.tensor_tensor(A(W1 + h), A(W1 + h), A(R2 + h), ALU.mult))
                    link(dve.tensor_tensor_scan(A(TI + h), A(LA + h), A(W1 + h), 0.0, ALU.mult, ALU.add))
                    dve.tensor_tensor(A(GG + h), A(TI + h), A(GG + h), ALU.mult)\
                        .then_inc(sem("lyf_ready"), 1); note(sem("lyf_ready"))
                elif k == "job" and s[1] in ("sz", "a_gate", "b_gate", "gate"):
                    to = {"sz": SZ, "a_gate": GA, "b_gate": GB, "gate": GG}[s[1]] + s[2]
                    b = ths[0]
                    ths[0] += 1
                    was_read(dve, s)
                    dve.scalar_tensor_tensor(out=A(to), in0=th[:, b % 3, :], scalar=1.0, in1=A(to),
                                             op0=ALU.add, op1=ALU.mult).then_inc(sem("gated"), 1); note(sem("gated"))
                elif k == "job" and s[1] in ON_VECTOR:
                    _, name, j = s
                    dve.wait_ge(filled["proj"], filled_at[s])
                    ps = slot(s)[:, 0:S]
                    done = read["proj", "D"]
                    mine = sum("D" in r for r in turns["proj"][:turn(s) + 1])
                    if name == "br_dsa":
                        dve.wait_ge(sem("mg_ready"), j + 1)
                        dve.tensor_tensor(A(MGA + j), ps, A(MGA + j), ALU.mult).then_inc(done, 1); note(done)
                    elif name in ("br_nsa", "br_ssd"):
                        dve.wait_ge(sem("mg_ready"), (9 if name == "br_nsa" else 17) + j)
                        dve.tensor_tensor(sqb[:, 0, :], ps, A(MGB + j), ALU.mult).then_inc(done, 1); note(done)
                        dve.wait_ge(done, mine)
                        ins = dve.tensor_tensor(A(MGA + j), A(MGA + j), sqb[:, 0, :], ALU.add)
                        if name == "br_nsa":
                            link(ins)
                        else:
                            ins.then_inc(sem("mixf_ready"), 1); note(sem("mixf_ready"))
                    elif name == "pool":
                        dve.tensor_scalar(sqb[:, 0, :], ps, col("pool_b", j), col("pool_s", j), ALU.add, ALU.mult)\
                            .then_inc(done, 1); note(done)
                        dve.wait_ge(done, mine)
                        if j == 0:
                            dve.wait_ge(sem("gated"), 32)
                        dve.tensor_tensor(A(GB + j), sqb[:, 0, :], A(GB + j), ALU.mult)\
                            .then_inc(sem("ybf_ready"), 1); note(sem("ybf_ready"))
                    else:
                        dve.tensor_tensor(A(XT + j), A(XT + j), ps, ALU.add).then_inc(done, 1); note(done)
                        dve.wait_ge(done, mine)

        @block.tensor
        def _(pe):
            pe.wait_ge(sem("zeros"), ZEROS)
            pe.wait_ge(sem("consts"), CONSTS)


            for s in steps:
                k = s[0]
                if k == "norm":
                    q = s[1]
                    readers_done(pe, s)
                    for c in range(8):
                        pe.wait_ge(sem("sq_ready"), 8 * q + c + 1)
                        mm = pe.matmul(slot(s), mean_d[:, :], A((HF0 if q == 0 else HF) + c),
                                       start=(c == 0), stop=(c == 7))
                    mm.then_inc(filled["mean"], 1)
                elif k == "tok":
                    t = s[1]
                    readers_done(pe, s)
                    if t == 0:
                        pe.wait_ge(sem("wtok_in"), 16)
                    for c in range(8):
                        pe.wait_ge(sem("hf_ready"), c + 1)
                        mm = pe.matmul(slot(s)[:, 0:TOK], A(HF0 + c)[:, P * t:P * t + P], wtok[:, c, :],
                                       start=(c == 0), stop=(c == 7))
                    mm.then_inc(filled["score"], 1)
                elif k == "acum":
                    readers_done(pe, s)
                    pe.wait_ge(sem("dta_ready"), 2)
                    ps = slot(s)
                    pe.matmul(ps[:, 0:64], upper[:, :], dta[:, :], start=True, stop=True)
                    pe.matmul(ps[:, 64:96], ones[:, :], dta[:, 0:32], start=True, stop=True)\
                        .then_inc(filled["mean"], 1)
                elif k == "cmp_mm":
                    readers_done(pe, s)
                    pe.wait_ge(sem("wcmp_in"), 32)
                    pe.wait_ge(sem("kcp_ready"), 4)
                    for v in range(2):
                        for l in range(32):
                            mm = pe.matmul(slot(s)[:, 256 * v:256 * v + N_CMP], wcmp[:, v, l, :], kcp[:, v, l, :],
                                           start=(l == 0), stop=(l == 31))
                    mm.then_inc(filled["score"], 1)
                elif k == "qsq":
                    i = s[1]
                    w = qn[i][1]
                    readers_done(pe, s)
                    pe.wait_ge(sem("qsq_ready"), i + 1)
                    pe.matmul(slot(s)[:, 0:w], mean_h[:, :], sqb[:, i % 2, 0:w], start=True, stop=True)\
                        .then_inc(filled["mean"], 1)
                elif k == "idx":
                    i = s[1]
                    t, m, pair = i // 4, (i % 4) // 2, i % 2
                    kl = P * (t + 1)
                    readers_done(pe, s)
                    was_read(pe, ("job", "ik", 0))
                    ps = slot(s).rearrange("p (h k) -> p h k", h=2)[:, :, 0:kl]
                    pe.matmul(ps, A(IQ + m)[:, P * t:P * t + P], ikz[:, 2 * pair:2 * pair + 2, 0:kl],
                              start=True, stop=True).then_inc(filled["score"], 1)
                elif k == "vcmp":
                    readers_done(pe, s)
                    was_read(pe, ("cmp_mm",))
                    pe.transpose(slot(s)[0:N_CMP, 0:P], kcr[:, 1, 0:N_CMP], ident[:, :]).then_inc(filled["turn"], 1)
                elif k == "pcmp":
                    t = s[1]
                    readers_done(pe, s)
                    pe.wait_ge(sem("kk_ready"), 4)
                    pe.wait_ge(sem("q_ready"), 16)
                    for c in range(8):
                        mm = pe.matmul(slot(s)[:, 30 * c:30 * c + 30], A(NQ + c)[:, P * t:P * t + P],
                                       kk_c[:, c // 4, :, :].rearrange("p h n -> p (h n)"), start=True, stop=True)
                    mm.then_inc(filled["score"], 1)
                    key = ("pcmpT", t)
                    readers_done(pe, key)
                    pe.wait_ge(sem("pc_ready"), t + 1)
                    for m in range(4):
                        mm = pe.transpose(slot(key)[:, P * m:P * m + P],
                                          pc[:, 4 * m:4 * m + 4, :].rearrange("p h n -> p (h n)"), ident[:, :])
                    mm.then_inc(filled["turn"], 1)
                elif k == "sA":
                    i = s[1]
                    t, c, kk, q, mask, v, gate = soft(i)
                    kl = P * (t + 1)
                    readers_done(pe, s)
                    if i < 16 and i % 8 == 0:
                        pe.wait_ge(sem("select_done"), t + 1)
                    ps = slot(s).rearrange("p (h k) -> p h k", h=2)[:, :, 0:kl]
                    pe.matmul(ps, A(q + c)[:, P * t:P * t + P], kk[:, :, 0:kl], start=True, stop=True)\
                        .then_inc(filled["score"], 1)
                elif k == "sB":
                    i = s[1]
                    t = soft(i)[0]
                    readers_done(pe, s)
                    pe.wait_ge(sem("p_ready"), i + 1)
                    for kt in range(t + 1):
                        for h in range(2):
                            n = 2 * kt + h
                            mm = pe.transpose(slot(s)[:, P * n:P * n + P],
                                              sbuf_s[:, i % 4, 256 * h + P * kt:256 * h + P * kt + P], ident[:, :])
                    mm.then_inc(filled["turn"], 1)
                elif k == "sC":
                    i = s[1]
                    t, c, _, _, _, v, gate = soft(i)
                    closes = ("sC", i if i < 16 or i % 2 else i + 1)
                    ps = slot(closes)
                    if gate in (None, 1):
                        readers_done(pe, closes)
                    if gate == 1:
                        was_read(pe, ("pcmpT", t))
                        pe.matmul(ps[:, 0:P], vcl[:, 2 * (c % 2) + c // 4, :], pct[:, t, P * (c // 2):P * (c // 2) + P],
                                  start=True, stop=False, skip_group_check=True)
                    was_read(pe, ("sB", i))
                    for h in range(2):
                        for kt in range(t + 1):
                            n = 2 * kt + h
                            mm = pe.matmul(ps[64 * h:64 * h + 64, 0:P], tok[:, kt, v:v + 64],
                                           sbuf_t[:, i % 2, P * n:P * n + P], start=(gate is None and kt == 0),
                                           stop=(kt == t and gate in (None, 2)), skip_group_check=True)
                    mm.then_inc(sem("pv_done"), 1)
                elif k == "xtr":
                    i = s[1]
                    t, q = i // 4, i % 4
                    readers_done(pe, s)
                    if i == 0:
                        pe.wait_ge(sem("silu_done"), 24)
                    for m in range(4):
                        mm = pe.transpose(slot(s)[:, P * m:P * m + P], A(XB + 4 * q + m)[:, P * t:P * t + P],
                                          ident[:, :])
                    mm.then_inc(filled["turn"], 1)
                elif k == "btr":
                    readers_done(pe, s)
                    for g in range(4):
                        mm = pe.transpose(slot(s)[:, P * g:P * g + P], A(XB + 16 + g)[:, 0:P], ident[:, :])
                    mm.then_inc(filled["turn"], 1)
                elif k == "cbt":
                    t = s[1]
                    readers_done(pe, s)
                    for g in range(4):
                        mm = pe.matmul(slot(s)[:, P * g:P * g + P], A(XB + 16 + g)[:, P * t:P * t + P],
                                       A(XB + 20 + g)[:, P * t:P * t + P], start=True, stop=True)
                    mm.then_inc(filled["score"], 1)
                elif k == "st":
                    g = s[1]
                    readers_done(pe, s)
                    was_read(pe, ("btr",))
                    pe.wait_ge(sem("xw_ready"), g + 1)
                    pe.matmul(slot(s)[:, :], bmt[:, g, :], xw[:, 512 * (g % 2):512 * (g % 2) + 512], start=True, stop=True)\
                        .then_inc(filled["score"], 1)
                elif k == "uA":
                    i = s[1]
                    t, hq = i // 8, i % 8
                    readers_done(pe, s)
                    for h in range(4):
                        n = 32 * t + 4 * hq + h
                        mm = pe.matmul(slot(s)[:, P * h:P * h + P], dta[:, n:n + 1].to_broadcast([P, P]),
                                       upper[:, :], start=True, stop=True)
                    mm.then_inc(filled["score"], 1)
                elif k == "uB":
                    i = s[1]
                    t, hq = i // 8, i % 8
                    readers_done(pe, s)
                    pe.wait_ge(sem("m_ready"), i + 1)
                    if i == 0:
                        was_read(pe, ("st", 3))
                        was_read(pe, ("xtr", 7), "D")
                    for h in range(4):
                        head = 4 * hq + h
                        o = slot(s)[64 * (h % 2):64 * (h % 2) + 64, P * (h // 2):P * (h // 2) + P]
                        mm = pe.matmul(o, xd[t][:, 64 * head:64 * head + 64], sbuf_s[:, i % 4, P * h:P * h + P],
                                       start=True, stop=(t == 0), skip_group_check=True)
                        if t == 1:
                            mm = pe.matmul(o, hst[:, 64 * head:64 * head + 64], sbuf_t[:, i % 2, P * h:P * h + P],
                                           start=False, stop=True, skip_group_check=True)
                    mm.then_inc(sem("pv_done"), 1)
                elif k == "ynorm":
                    readers_done(pe, s)
                    for c in range(16):
                        pe.wait_ge(sem("ysq_ready"), c + 1)
                        mm = pe.matmul(slot(s), mean_d[:, :], A(XD + c), start=(c == 0), stop=(c == 15))
                    mm.then_inc(filled["mean"], 1)
                elif k == "ln":
                    for n, (src, ready) in enumerate(((AC, "econv_done"), (SQ, "lsq_ready"))):
                        key = ("ln", n)
                        readers_done(pe, key)
                        for c in range(8):
                            pe.wait_ge(sem(ready), c + 1)
                            mm = pe.matmul(slot(key), mean_d[:, :], A(src + c), start=(c == 0), stop=(c == 7))
                        mm.then_inc(filled["mean"], 1)
                elif k == "job":
                    _, name, j = s
                    n, b0 = blocks[s], first[s]
                    readers_done(pe, s)
                    tag = {"br_ssd": "y", "w_out": "mix", "ff1": "h1", "ff2": "ff", "val_glu": "h2", "b_val": "h2",
                           "b_gate": "h2", "a_gate": "h2", "even_out": "ya", "xr": "h3", "gate": "h3",
                           "odd_out": "ly"}.get(name, "h0")
                    if name == "br_dsa":
                        rhs = [A(DQ + c) for c in range(8)]
                        if j == 0:
                            was_read(pe, ("sC", 15))
                    elif name == "br_nsa":
                        rhs = [A(NQ + c) for c in range(8)]
                        if j == 0:
                            was_read(pe, ("sC", 47))
                    elif name == "pool":
                        pe.wait_ge(sem("dp_ready"), 2 * (j // 2) + 2)
                        rhs = [A(DP + 2 * (j // 2)), A(DP + 2 * (j // 2) + 1)]
                    elif name == "rg_ig":
                        if j % 2 == 0:
                            pe.wait_ge(sem("conv_done"), 24 + j // 2 + 1)
                        rhs = [A(XC + j // 2)]
                    elif name == "even_out":
                        rhs = [(R(YA + c), R(YAL + c)) for c in range(8)]
                        rhs += [(R(YB + c), R(YBL + c)) for c in range(8)]
                        if j == 0:
                            pe.wait_ge(sem("lo_yb"), 8)
                    else:
                        rhs = [(parts[tag][1](c), parts[tag][2](c)) for c in range(n)]
                    for c in range(n):
                        b = b0 + c
                        u = b // 8
                        if name in PLAIN:
                            if b % 8 == 0:
                                pe.wait_ge(w_in[u % RING], 16 * (u // RING + 1))
                            mm = pe.matmul(slot(s)[:, 0:S], ring[:, u % RING, b % 8, :], rhs[c],
                                           start=(c == 0), stop=(c == n - 1))
                        else:
                            if j == 0 and (name != "even_out" or c < 8):
                                pe.wait_ge(sem(f"lo_{tag}"), c + 1)
                            if b % 8 == 0:
                                pe.wait_ge(sem("w_lo_pool" if on_gpsimd(u) else "w_lo_dve"), lo_turn[u])
                            w_hi, w_lo = ring_hi[:, hi_slot[u], b % 8, :], ring_lo[:, u % RING, b % 8, :]
                            hi, lo = rhs[c]
                            pe.matmul(slot(s)[:, 0:S], w_hi, hi, start=(c == 0), stop=False)
                            pe.matmul(slot(s)[:, 0:S], w_hi, lo, start=False, stop=False)
                            mm = pe.matmul(slot(s)[:, 0:S], w_lo, hi, start=False, stop=(c == n - 1))
                        if b % 8 == 7 or c == n - 1:
                            mm.then_inc(filled["proj"], 1)


def kernel(**inputs):
    import numpy as np
    import concourse.bacc as bacc
    from concourse.bass_utils import run_bass_kernel_spmd

    a = {k: np.asarray(v) for k, v in inputs.items()}
    w = a["w_in"][0]
    cuts = np.cumsum([0, 1024, 64, 64, 256, 32, 8, 1024, 768, 48, 2048, 3072, 32, 3072])
    (dq, dk, dv, iq, ik, iw, nq, nkv, ng, sz, xbc, dt, mg) = [w[:, cuts[i]:cuts[i + 1]] for i in range(13)]
    kc, vc, ks, vs, kw, vw = [nkv[:, 128 * i:128 * i + 128] for i in range(6)]

    def tiles(m):
        K, N = m.shape
        return m.reshape(K // 128, 128, N // 128, 128).transpose(2, 0, 1, 3)

    even = a["w_in_even_2"][0]
    val, glu, a_gate, b_val, b_gate = [even[:, 1024 * i:1024 * i + 1024] for i in range(5)]
    odd = a["w_in_odd_2"][0]
    weights = {
        "iq": tiles(iq), "ik": tiles(np.concatenate([ik] * 4, axis=1)), "dk": tiles(np.concatenate([dk, dk], axis=1)),
        "kc": tiles(kc), "vc": tiles(vc), "ks": tiles(ks), "kw": tiles(kw), "dq": tiles(dq), "nq": tiles(nq),
        "xbc": tiles(xbc), "sz": tiles(sz), "mg": tiles(mg),
        "br_dsa": tiles(a["w_br_dsa"][0]), "br_nsa": tiles(a["w_br_nsa"][0]), "br_ssd": tiles(a["w_br_ssd"][0]),
        "w_out": tiles(a["w_out"][0]), "ff1": tiles(a["w_ff1"][0]), "ff2": tiles(a["w_ff2"][0]),
        "val_glu": np.stack([tiles(val), tiles(glu)], axis=1).reshape(16, 8, 128, 128),
        "b_val": tiles(b_val), "b_gate": tiles(b_gate), "a_gate": tiles(a_gate),
        "pool": a["pool_w_2"][0].reshape(4, 2, 128, 2, 128).transpose(0, 3, 1, 2, 4).reshape(8, 2, 128, 128),
        "even_out": tiles(a["w_out_even_2"][0]), "xr": tiles(odd[:, :1536]), "gate": tiles(odd[:, 1536:]),
        "rg_ig": np.stack([a["w_rg_2"][0], a["w_ig_2"][0]], axis=1).reshape(24, 1, 128, 128),
        "odd_out": tiles(a["w_out_odd_2"][0]),
    }
    parts = []
    for s in schedule():
        if s[0] == "job":
            parts.append(weights[s[1]][s[2]])
    stream = np.concatenate(parts, axis=0)
    stream = np.ascontiguousarray(stream.reshape(-1, 8, 128, 128).transpose(0, 2, 1, 3)).reshape(-1, 128, 1024)

    w_tok = np.concatenate([iw, ng, dt, dv, vs, vw], axis=1).reshape(8, 128, TOK).transpose(1, 0, 2)
    w_cmp = a["nsa_cmp_w"][0].transpose(2, 0, 1, 3)

    def chunks(v):
        return v.reshape(-1, 128).T

    def twice(v):
        return np.concatenate([v, v]).reshape(128, 1)

    pos = a["nsa_cmp_pos"][0].reshape(64, 64).T
    columns = {
        "norm1": chunks(a["norm1_g"]), "dq_g": twice(a["dsa_q_norm"][0]), "dk_g": twice(a["dsa_k_norm"][0]),
        "nq_g": twice(a["nsa_q_norm"][0]),
        "nk_g": np.concatenate([twice(a["nsa_k_norm"][0, i]) for i in range(3)], axis=1),
        "cmp_pos": np.concatenate([pos, pos], axis=0),
        "ssd_cw": a["ssd_conv_w"][0].reshape(4, 24, 128).transpose(2, 1, 0).reshape(128, 96),
        "ssd_cb": chunks(a["ssd_conv_b"]), "ssd_d": chunks(np.repeat(a["ssd_d"][0], 64)),
        "ssd_g": chunks(a["ssd_norm_g"]), "norm2": chunks(a["norm2_g"]), "even_g": chunks(a["norm_even_2"]),
        "even_cw": a["conv_a_w_2"][0].reshape(31, 8, 128).transpose(2, 1, 0).reshape(128, 248),
        "even_cb": chunks(a["conv_a_b_2"]), "ln_g": chunks(a["ln_a_g_2"]), "ln_b": chunks(a["ln_a_b_2"]),
        "pool_b": chunks(a["pool_b_2"]), "pool_s": chunks(a["pool_scale_2"]), "odd_g": chunks(a["norm_odd_2"]),
        "odd_cw": a["conv_c_w_2"][0].reshape(4, 12, 128).transpose(2, 1, 0).reshape(128, 48),
        "odd_cb": chunks(a["conv_c_b_2"]), "b_rg": chunks(a["b_rg_2"]), "b_ig": chunks(a["b_ig_2"]),
        "lam": chunks(a["lru_lambda_2"]), "final_g": chunks(a["final_norm_2"]),
    }
    cols = np.concatenate([columns[name] for name, _ in COLUMNS], axis=1)
    rows = np.broadcast_to(np.concatenate([a["ssd_dt_bias"], a["ssd_a_log"]], axis=1), (128, 64))
    x_t = a["x"][0].T.reshape(8, 128, 256).transpose(1, 0, 2)
    arrays = {"x_t": x_t, "w_stream": stream, "w_tok": w_tok, "w_cmp": w_cmp, "cols": cols, "rows": rows}
    arrays = {k: np.ascontiguousarray(v) for k, v in arrays.items()}

    nc = bacc.Bacc("TRN2", target_bir_lowering=False, num_devices=1)
    aps = [nc.dram_tensor(k, v.shape, mybir.dt.from_np(v.dtype), kind="ExternalInput").ap() for k, v in arrays.items()]
    out = nc.dram_tensor("out_t", (128, 8, 256), F32, kind="ExternalOutput").ap()
    program(nc, *aps, out)
    r = run_bass_kernel_spmd(nc, [arrays], core_ids=[0])
    got = r.results[0]["out_t"]
    return np.ascontiguousarray(got.transpose(1, 0, 2).reshape(1024, 256).T)[None]
```

```python
from contextlib import ExitStack

import concourse.bass as bass
from concourse import mybir

F32 = mybir.dt.float32
F32R = mybir.dt.float32r
ALU = mybir.AluOpType
ACT = mybir.ActivationFunctionType
AX = mybir.AxisListType

P = 128
S = 256
NT = S // P
D = 1024
KD = D // P
HD = 64
NEG = -1e30
MARK = -3e38
TOPK = 64
SCALE = HD ** -0.5
N_CMP = 15
SSD_H = 32
FFC = 4 * D // P
LRU_H = 12
CONV_K = 31
WINDOWS = (2, 4, 8, 16)
RING = 5
HIS = 3
AHEAD = 2
TOK = 408
TOK_IW, TOK_NG, TOK_DT, TOK_DV, TOK_VS, TOK_VW = 0, 8, 56, 88, 152, 280

COLUMNS = [("norm1", 8), ("dq_g", 1), ("dk_g", 1), ("nq_g", 1), ("nk_g", 3), ("cmp_pos", 64),
           ("ssd_cw", 96), ("ssd_cb", 24), ("ssd_d", 16), ("ssd_g", 16), ("norm2", 8),
           ("even_g", 8), ("even_cw", 248), ("even_cb", 8), ("ln_g", 8), ("ln_b", 8), ("pool_b", 8),
           ("pool_s", 8), ("odd_g", 8), ("odd_cw", 48), ("odd_cb", 12), ("b_rg", 12), ("b_ig", 12),
           ("lam", 12), ("final_g", 8)]
AT, _n = {}, 0
for _name, _w in COLUMNS:
    AT[_name] = _n
    _n += _w
NCOLS = _n

PHASES = [("iq", 2, 8), ("ik", 1, 8), ("dk", 1, 8), ("kc", 1, 8), ("vc", 1, 8), ("ks", 1, 8), ("kw", 1, 8),
          ("dq", 8, 8), ("nq", 8, 8), ("xbc", 24, 8), ("sz", 16, 8), ("mg", 24, 8),
          ("br_dsa", 8, 8), ("br_nsa", 8, 8), ("br_ssd", 8, 16), ("w_out", 8, 8),
          ("ff1", 32, 8), ("ff2", 8, 32), ("val_glu", 16, 8), ("b_val", 8, 8), ("b_gate", 8, 8),
          ("a_gate", 8, 8), ("pool", 8, 2), ("even_yb", 8, 8), ("even_ya", 8, 8), ("xr", 12, 8), ("gate", 12, 8),
          ("rg_ig", 24, 1), ("odd_out", 8, 12)]
ON_VECTOR = {"br_dsa", "br_nsa", "br_ssd", "w_out", "ff2", "even_yb", "even_ya", "odd_out"}

PLAIN = {"br_dsa", "br_nsa", "b_val", "pool", "rg_ig"}

XT, HH, HL, DQ, NQ, SZ, XB, MGA, MGB, XD = 0, 8, 16, 24, 32, 40, 56, 80, 88, 96
KCP, DK, KC, VC, KS, KW = 40, 44, 45, 46, 47, 48
WTOK, HF0 = 56, 69
WCMP = 80
RL, IDX = 96, 100
IQ, IKZ = 112, 114
XW, HST = 112, 116
HF = 116
FFH, FFL, FFR, FFS = 24, 56, 88, 92
UB, VA, TA, AC, GA, GB, BV, DP, YA, YB, YAL, YBL, SQ = 24, 33, 41, 49, 57, 65, 73, 82, 90, 98, 106, 33, 114
XC, U2, TI, GG, LA, R2, W1, LYH, LYL = 24, 36, 48, 60, 72, 84, 96, 36, 72
ARENA = 124


def schedule():
    out = []
    jobs = {name: [("job", name, i) for i in range(n)] for name, n, _ in PHASES}
    out += [("norm", 0)] + [("split", "h0", c) for c in range(8)] + [("fills",), ("tok", 0), ("tok", 1)]
    for name in ("iq", "ik", "dk", "kc", "vc", "ks", "kw"):
        out += jobs[name]
    out += [("cmp_in",), ("cmp_mm",)]
    out += [("qsq", 0), ("qsq", 1), ("qap", 0), ("qsq", 2), ("qap", 1), ("qsq", 3), ("qap", 2), ("qap", 3)]
    for n, job in enumerate(jobs["dq"] + jobs["nq"]):
        out.append(job)
        if n >= 1:
            out.append(("qm", n - 1))
        if n % 2 == 1:
            out.append(("idx", n // 2))
        if n == 1:
            out.append(("softplus",))
        if n in (9, 15):
            out.append(("select", n // 15))
    out += [("qm", 15), ("qroot",), ("vcmp",), ("acum",)]
    soft = []
    for i in range(48 + 4):
        group = []
        for stage, lag in (("sA", 0), ("sE", 1), ("sR", 2), ("sB", 3), ("sC", 4)):
            if 0 <= i - lag < 48:
                group.append((stage, i - lag))
        group += {2: [("pA", 0)], 5: [("pB", 0)], 8: [("pA", 1)], 11: [("pB", 1)]}.get(i, [])
        soft.append(group)
    prep = [[("btr",)], [("xtr", 0)], [("xtr", 1)], [("st", 0)], [("xtr", 2)], [("st", 1)], [("xtr", 3)],
            [("st", 2)], [("xtr", 4)], [("st", 3)], [("xtr", 5)], [("xtr", 6)], [("xtr", 7)],
            [("cbt", 0)], [("cbt", 1)]]
    quads = []
    for i in range(16 + 3):
        group = []
        for stage, lag in (("uA", 0), ("uE", 1), ("uB", 3)):
            if 0 <= i - lag < 16:
                group.append((stage, i - lag))
        quads.append(group)
    filler = soft + prep + quads
    mg = jobs["mg"]
    wide = jobs["xbc"] + jobs["sz"] + mg[0:8] + jobs["br_dsa"] + mg[8:16] + jobs["br_nsa"] + mg[16:24]
    at = 0
    for n, job in enumerate(wide):
        if n == 24:
            out += [("xconv", 23), ("xsilu", 22), ("xsilu", 23)]
        out.append(job)
        want = (n + 1) * len(filler) // (len(wide) - 2)
        while at < min(want, len(filler)):
            out += filler[at]
            at += 1
        if job[1] == "xbc":
            if job[2] >= 1:
                out.append(("xconv", job[2] - 1))
            if job[2] >= 2:
                out.append(("xsilu", job[2] - 2))
    out += sum(filler[at:], [])
    out += [("ynorm",)] + [("split", "y", c) for c in range(16)]
    for c in range(8):
        out += [jobs["br_ssd"][c], ("split", "mix", c)]
    out += jobs["w_out"] + [("norm", 1)] + [("split", "h1", c) for c in range(8)]
    for j in range(34):
        if j < 32:
            out.append(jobs["ff1"][j])
        if 1 <= j < 33:
            out.append(("ffsq", j - 1))
        if j >= 2:
            out.append(("split", "ff", j - 2))
    out += jobs["ff2"]
    out += [("norm", 2)] + [("split", "h2", c) for c in range(8)] + [("pads",)]
    pool, a_gate, even_yb = jobs["pool"], jobs["a_gate"], jobs["even_yb"]
    val_glu, b_val = jobs["val_glu"], jobs["b_val"]
    first = val_glu[0:4]
    for i in range(8):
        first += [b_val[i]] + val_glu[4 + 12 * i // 8:4 + 12 * (i + 1) // 8]
    conv, columns = 0, 0
    for job in first + jobs["b_gate"] + pool[0:4] + a_gate[0:4] + pool[4:8] + a_gate[4:8]:
        out.append(job)
        columns += {"pool": 2, "b_val": 10}.get(job[1], 8)
        while conv < min(32, (columns - 24) // 10):
            out.append(("econv", conv))
            conv += 1
        if job[1] == "b_val":
            out.append(("winsum", job[2]))
        elif job[1] == "pool":
            out.append(("split", "yb", job[2]))
    out += [("econv", n) for n in range(conv, 32)]
    out += [("ln",)] + even_yb[0:3] + [("lnv",)] + even_yb[3:5]
    for c in range(8):
        out += ([even_yb[5 + c // 2]] if c in (0, 2, 4) else []) + [("lnout", c)]
        if c >= 3:
            out.append(("split", "ya", c - 3))
    out += [("split", "ya", c) for c in range(5, 8)]
    out += jobs["even_ya"]
    out += [("norm", 3)] + [("split", "h3", c) for c in range(8)]
    xr, rg_ig = jobs["xr"], jobs["rg_ig"]
    for j in range(12):
        out.append(xr[j])
        if j >= 1:
            out.append(("oconv", j - 1))
        if j in (6, 10):
            out += rg_ig[8 * (j // 4 - 1):8 * (j // 4)]
            out += [("lru", h) for h in range(j // 4 * 4 - 4, j // 4 * 4 - 2)]
        if j in (8,):
            out += [("lru", 2), ("lru", 3)]
    out += [("oconv", 11)] + rg_ig[16:24] + [("lru", h) for h in range(6, 12)]
    for j in range(12):
        out.append(jobs["gate"][j])
        if j == 3:
            out += [("uroot", h) for h in range(12)]
        if j >= 4:
            out.append(("scan", j - 4))
        if j >= 5:
            out.append(("scanout", j - 5))
    for h in range(8, 12):
        out += [("scan", h), ("scanout", h - 1)]
    out += [("scanout", 11)] + [("split", "ly", c) for c in range(12)]
    out += jobs["odd_out"] + [("norm", 4), ("store",)]
    at, splits = 0, {}
    order = [s for s in out if s[0] == "job"]
    starts = []
    for s in order:
        starts += [s] * {name: k for name, _, k in PHASES}[s[1]]
    units = len(starts) // 8
    for u in range(units):
        if starts[8 * u][1] not in PLAIN:
            splits.setdefault(("tok", 0) if u < AHEAD else starts[8 * (u - AHEAD)], []).append(("wsplit", u))
    final = []
    for s in out:
        final += splits.get(s, []) + [s]
    out = final
    assert len(set(out)) == len(out)
    return out


def psum_tenants(steps):
    turns = {"proj": [], "score": [], "turn": [], "pv": [], "mean": []}
    where = {}

    def add(group, key, readers):
        where[key] = (group, len(turns[group]))
        turns[group].append(readers)

    for s in steps:
        k = s[0]
        if k == "job":
            add("proj", s, "D" if s[1] in ON_VECTOR else "A")
        elif k in ("tok", "cmp_mm", "idx", "cbt", "st"):
            add("score", s, "A")
        elif k in ("sA", "pA"):
            add("score", s, "D")
        elif k == "qm":
            if s[1] == 0:
                add("mean", ("qroot",), "A")
        elif k == "uA":
            add("score", s, "AD" if s[1] >= 8 else "D")
        elif k in ("vcmp", "pB", "sB", "btr"):
            add("turn", s, "A")
        elif k == "xtr":
            add("turn", s, "D")
        elif k == "sC" and (s[1] < 16 or s[1] % 2 == 1):
            add("pv", s, "A")
        elif k == "uB":
            add("pv", s, "D")
        elif k in ("norm", "qsq", "acum", "ynorm"):
            add("mean", s, "A")
        elif k == "ln":
            add("mean", s, "A")
        elif k == "lnv":
            add("mean", s, "A")
    return where, turns


def program(nc, x_t, w_stream, w_tok, w_cmp, cols, rows, out):
    steps = schedule()
    where, turns = psum_tenants(steps)
    slots = {"proj": 3, "score": 2, "turn": 1, "pv": 1, "mean": 1}

    blocks, first = {}, {}
    at = 0
    order = [s for s in steps if s[0] == "job"]
    for s in order:
        n = next(k for name, _, k in PHASES if name == s[1])
        first[s], blocks[s] = at, n
        at += n
    n_units = at // 8
    assert at % 8 == 0 and w_stream.shape[0] == n_units
    milestone, used, filled_at = 0, {}, {}
    for s in order:
        for b in range(first[s], first[s] + blocks[s]):
            if b % 8 == 7 or b == first[s] + blocks[s] - 1:
                milestone += 1
            if b % 8 == 7:
                used[b // 8] = milestone
        filled_at[s] = milestone

    with ExitStack() as ctx:
        def sb(name, shape):
            return ctx.enter_context(nc.sbuf_tensor(name, shape, F32))

        def psum(name, shape):
            return ctx.enter_context(nc.psum_tensor(name, shape, F32))

        sems = {}

        def sem(name):
            if name not in sems:
                sems[name] = ctx.enter_context(nc.semaphore(name))
            return sems[name]

        def under(name, shape, back):
            return nc.alloc_sbuf_tensor_at(name, shape, F32R, offset=nc.sbuf_base - back)

        arena = sb("arena", [P, ARENA, S])
        arena_r = [under(f"arena_r{c}", [P, 4, S], (ARENA - c) * S * 4) for c in range(0, ARENA, 4)]
        ring = sb("ring", [P, RING, 8, P])
        ring_lo = under("ring_lo", [P, RING, 8, P], RING * 8 * P * 4)
        ring_hi = ctx.enter_context(nc.sbuf_tensor("ring_hi", [P, HIS, 8, P], F32R))
        par = sb("par", [P, NCOLS])
        row = sb("row", [P, 2 * SSD_H])
        tok = sb("tok", [P, NT, TOK])
        sbuf_s = sb("sbuf_s", [P, 4, 512])
        sbuf_t = sb("sbuf_t", [P, 2, 512])
        raw = sb("raw", [P, 3, 3 + S])
        th = sb("th", [P, 3, S])
        sqb = sb("sqb", [P, 2, S])
        root = sb("root", [P, 2, S])
        rinv = sb("rinv", [P, S])
        kk_d = sb("kk_d", [P, 2, S])
        kk_s = sb("kk_s", [P, 2, 2, S])
        kk_w = sb("kk_w", [P, 2, 2, S])
        kk_c = sb("kk_c", [P, 2, 2, 32])
        kcr = sb("kcr", [P, 2, 2, 32])
        vcl = sb("vcl", [P, 4, P])
        pc = arena[:, RL:RL + 2, :].rearrange("p c s -> p (c s)").rearrange("p (h n) -> p h n", n=32)
        ec = arena[:, RL + 2, :].rearrange("p (h n) -> p h n", n=16)
        rq = sb("rq", [P, 64])
        pct = arena[:, IQ:IQ + 4, :].rearrange("p (t c) s -> p t (c s)", t=NT)
        bmt = kk_d[:, :, :].rearrange("p a s -> p (a s)").rearrange("p (g n) -> p g n", g=4)
        cbt = kk_s[:, :, :, :].rearrange("p t a s -> p t (a s)")
        caus = sb("caus", [P, NT, S])
        jneg = sb("jneg", [P, P])
        dmask = arena[:, IDX + 2:IDX + 4, :]
        ident = sb("ident", [P, P])
        ones = sb("ones", [P, P])
        mean_d = sb("mean_d", [P, P])
        mean_h = sb("mean_h", [P, P])
        upper = sb("upper", [P, P])
        cneg = sb("cneg", [P, NT, 16])
        cvis = sb("cvis", [P, NT, 16])
        icnt = sb("icnt", [P, 4, 16])
        small = sb("small", [P, 64])
        gates = sb("gates", [P, NT, 48])
        sp = sb("sp", [P, 6, 76])
        dta = sb("dta", [P, 64])
        ea = sb("ea", [P, 32])
        ac = sb("ac", [P, 96])
        dec = sb("dec", [P, 32])
        half = sb("half", [P, 160])
        m8 = sb("m8", [P, 8])
        srow = sb("srow", [P, 4, 8])
        crow = row[:, 0:48].rearrange("p (r h) -> p r h", r=3)
        ytmp = pct[:, 0, 0:2 * P].rearrange("p (c i) -> p c i", c=2)
        wtmp = kk_w[:, :, :, :].rearrange("p a b s -> p a (b s)")[:, :, 0:272]

        bank = {"proj": [psum(f"p_proj{i}", [P, 512]) for i in range(3)],
                "score": [psum(f"p_score{i}", [P, 512]) for i in range(2)],
                "turn": [psum("p_turn", [P, 512])]}
        bank["pv"] = [psum("p_pv", [P, 512])]
        bank["mean"] = [psum("p_mean", [P, 512])]

        filled = {g: sem(f"{g}_filled") for g in turns}
        read = {(g, e): sem(f"{g}_read_{'act' if e == 'A' else 'dve'}") for g in turns for e in "AD"}
        w_in = [sem(f"w_in{i}") for i in range(RING)]

        def A(c, n=1):
            return arena[:, c, :] if n == 1 else arena[:, c:c + n, :]

        def R(c):
            return arena_r[c // 4][:, c % 4, :]

        def flat(c, n):
            return arena[:, c:c + n, :].rearrange("p c s -> p (c s)")

        wtok = flat(WTOK, 13)[:, 0:8 * TOK].rearrange("p (k n) -> p k n", k=8)
        wcmp = flat(WCMP, 8).rearrange("p (v m e) -> p v m e", v=2, m=16)
        kcp = flat(KCP, 4)[:, 0:2 * 32 * N_CMP].rearrange("p (v m g n) -> p v m g n", v=2, m=16, g=2)
        ikz = arena[:, IKZ:IKZ + 4, :]
        xd = [flat(XD + 8 * t, 8) for t in range(NT)]
        xw, hst = flat(XW, 4), flat(HST, 8)
        ub = flat(UB, 9)[:, 0:8 * (S + 30)].rearrange("p (c s) -> p c s", c=8)
        bv = flat(BV, 9)[:, 0:8 * (S + 16)].rearrange("p (c s) -> p c s", c=8)

        def col(name, i=0):
            return par[:, AT[name] + i:AT[name] + i + 1]

        def slot(key):
            g, n = where[key]
            return bank[g][n % slots[g]][:, 0:256 if g == "mean" else 512]

        def turn(key):
            return where[key][1]

        def readers_done(eng, key):
            g, n = where[key]
            prev = n - slots[g]
            if prev >= 0:
                for e in turns[g][prev]:
                    eng.wait_ge(read[g, e], sum(e in r for r in turns[g][:prev + 1]))

        def was_read(eng, key, reader="A"):
            g, n = where[key]
            eng.wait_ge(read[g, reader], sum(reader in r for r in turns[g][:n + 1]))

        parts = {"y": (lambda c: A(SZ + c), lambda c: R(XB + c), lambda c: R(XD + c), "yf_ready", "P"),
                 "mix": (lambda c: A(MGA + c), lambda c: R(HH + c), lambda c: R(HL + c), "mixf_ready", "P"),
                 "ff": (lambda c: A(FFS + c % 4), lambda c: R(FFH + c), lambda c: R(FFL + c), "ffs_ready", "D"),
                 "ya": (lambda c: A(SQ + c), lambda c: R(YA + c), lambda c: R(YAL + c), "yaf_ready", "P"),
                 "yb": (lambda c: A(GB + c), lambda c: R(YB + c), lambda c: R(YBL + c), "ybf_ready", "P"),
                 "ly": (lambda c: A(GG + c), lambda c: R(LYH + c), lambda c: R(LYL + c), "lyf_ready", "P")}
        for q in range(4):
            src = HF0 if q == 0 else HF
            parts[f"h{q}"] = (lambda c, src=src: A(src + c), lambda c: R(HH + c), lambda c: R(HL + c),
                              "hf_ready", "P")

        def source_count(tag, c):
            return c + 1 + (8 * int(tag[1]) if tag[0] == "h" else 0)

        split_units = [s[1] for s in steps if s[0] == "wsplit"]
        hi_slot = {u: n % HIS for n, u in enumerate(split_units)}
        hi_before = {u: split_units[n - HIS] if n >= HIS else None for n, u in enumerate(split_units)}
        hi_turn = {u: n + 1 for n, u in enumerate(split_units)}
        unit_of = {}
        for s in order:
            for b in range(first[s], first[s] + blocks[s]):
                unit_of.setdefault(b // 8, s[1])

        def on_gpsimd(u):
            if unit_of[u] in ("val_glu", "b_gate", "a_gate", "even_yb", "xr", "gate"):
                return True
            if unit_of[u] in ("xbc",):
                return hi_turn[u] % 3 > 0
            return hi_turn[u] % 2 == 0

        lo_turn = {}
        for side in (True, False):
            for n, u in enumerate([u for u in split_units if on_gpsimd(u) == side]):
                lo_turn[u] = n + 1

        def remainder(eng, u):
            eng.wait_ge(sem("w_hi_ready"), hi_turn[u])
            return eng.tensor_tensor(ring_lo[:, u % RING, :, :].rearrange("p k n -> p (k n)"),
                                     ring[:, u % RING, :, :].rearrange("p k n -> p (k n)"),
                                     ring_hi[:, hi_slot[u], :, :].rearrange("p k n -> p (k n)").bitcast(F32),
                                     ALU.subtract)

        def part_remainder(eng, tag, c):
            src, hi, lo, _, _ = parts[tag]
            eng.wait_ge(sem(f"hi_{tag}"), c + 1)
            return eng.tensor_tensor(lo(c), src(c), hi(c).bitcast(F32), ALU.subtract)

        qn = [(A(DK), S, 52), (A(KS), S, 54), (A(KW), S, 55),
              (kcr[:, 0, :, :].rearrange("p g n -> p (g n)"), 64, 53)]

        def soft(i):
            if i < 16:
                return i // 8, i % 8, kk_d[:, :, :], DQ, dmask, TOK_DV, None
            u, kind = (i - 16) // 2, (i - 16) % 2
            t, c = u // 8, u % 8
            g = c // 4
            kk = (kk_w if kind else kk_s)[:, g, :, :]
            return t, c, kk, NQ, caus, (TOK_VW if kind else TOK_VS) + 64 * g, kind + 1

        CONSTS, ZEROS = 6 + 4 * 16, 21
        SMALL_ZEROS = 13

        block = ctx.enter_context(nc.Block())

        @block.sync
        def _(sp_eng):
            sp_eng.dma_start(arena[:, XT:XT + 8, :], x_t).then_inc(sem("x_in"), 16)
            sp_eng.dma_start(par[:, :], cols).then_inc(sem("par_in"), 16)
            sp_eng.dma_start(wtok, w_tok).then_inc(sem("wtok_in"), 16)
            for u in range(n_units):
                if u >= RING:
                    sp_eng.wait_ge(filled["proj"], used[u - RING])
                sp_eng.dma_start(ring[:, u % RING, :, :].rearrange("p k n -> p (k n)"),
                                 w_stream[u]).then_inc(w_in[u % RING], 16)
            sp_eng.wait_ge(sem("hf_ready"), 40)
            sp_eng.dma_start(out, arena[:, HF:HF + 8, :]).then_inc(sem("stored"), 16)
            sp_eng.wait_ge(sem("stored"), 16)

        @block.gpsimd
        def _(pool):
            consts = sem("consts")
            counts, last = {}, []

            def note(semaphore):
                n = str(semaphore.name)
                counts[n] = counts.get(n, 0) + 1
                last[:] = [semaphore, counts[n]]

            def settle():
                if last:
                    pool.wait_ge(*last)

            def link(ins):
                ins.then_inc(sem("pool_chain"), 1)
                note(sem("pool_chain"))
                settle()

            n = [0]

            def const(ins):
                ins.then_inc(consts, 1)
                note(consts)
                n[0] += 1

            pool.wait_ge(sem("zeros"), SMALL_ZEROS)
            const(pool.affine_select(out=upper[:, :], in_=ones[:, :], compare_op=ALU.is_ge, fill=0.0,
                                     base=0, pattern=[[1, P]], channel_multiplier=-1))
            const(pool.affine_select(out=ident[:, :], in_=ident[:, :], compare_op=ALU.not_equal, fill=1.0,
                                     base=0, pattern=[[-1, P]], channel_multiplier=1))
            const(pool.affine_select(out=caus[:, :, :], in_=caus[:, :, :], compare_op=ALU.is_ge, fill=NEG,
                                     base=0, pattern=[[P, NT], [-1, S]], channel_multiplier=1))
            const(pool.affine_select(out=jneg[:, :], in_=jneg[:, :], compare_op=ALU.is_ge, fill=NEG,
                                     base=0, pattern=[[1, P]], channel_multiplier=-1))
            const(pool.affine_select(out=cneg[:, :, :], in_=cneg[:, :, :], compare_op=ALU.is_ge, fill=NEG,
                                     base=-31, pattern=[[P, NT], [-16, 16]], channel_multiplier=1))
            const(pool.affine_select(out=cvis[:, :, :], in_=cvis[:, :, :], compare_op=ALU.is_ge, fill=0.0,
                                     base=-31, pattern=[[P, NT], [-16, 16]], channel_multiplier=1))
            for g, w in enumerate(WINDOWS):
                for k in range(16):
                    ins = pool.memset(icnt[:, g, k:k + 1], w / min(k + 1, w))
                    const(ins)
            assert n[0] == CONSTS, n[0]

            for s in steps:
                k = s[0]
                if k == "sR":
                    i = s[1]
                    t, c, kk, q, mask, v, gate = soft(i)
                    kl = P * (t + 1)
                    p = sbuf_s[:, i % 4, :].rearrange("p (h k) -> p h k", h=2)[:, :, 0:kl]
                    pool.wait_ge(sem("scale_ready"), i + 1)
                    r = srow[:, i % 4, 6:8]
                    pool.tensor_tensor(p, p, r.unsqueeze(2).to_broadcast([P, 2, kl]), ALU.mult)\
                        .then_inc(sem("p_ready"), 1); note(sem("p_ready"))
                elif k == "xtr" and s[1] < 4:
                    i = s[1]
                    was_read(pool, s, "D")
                    pool.wait_ge(sem("dec_ready"), 1)
                    if i >= 2:
                        was_read(pool, ("st", i - 2))
                    pool.tensor_tensor(
                        xw[:, 512 * (i % 2):512 * (i % 2) + 512].rearrange("p (h e) -> p h e", h=8),
                        xd[0][:, 512 * i:512 * i + 512].rearrange("p (h e) -> p h e", h=8),
                        dec[:, 8 * i:8 * i + 8].unsqueeze(2).to_broadcast([P, 8, 64]), ALU.mult)\
                        .then_inc(sem("xw_ready"), 1); note(sem("xw_ready"))
                elif k == "uE":
                    i = s[1]
                    t, hq = i // 8, i % 8
                    g = hq // 2
                    l = sbuf_s[:, i % 4, :].rearrange("p (h i) -> p h i", h=4)
                    pool.wait_ge(sem("l_ready"), i + 1)
                    if t == 1:
                        e = sbuf_t[:, i % 2, :].rearrange("p (h i) -> p h i", h=4)
                        link(pool.tensor_tensor(e, e, A(XB + 20 + g)[:, P:S].unsqueeze(1).to_broadcast([P, 4, P]),
                                                ALU.mult))
                    if i == 0:
                        was_read(pool, ("cbt", 1))
                    pool.tensor_tensor(
                        l, l, cbt[:, t, P * g:P * g + P].unsqueeze(1).to_broadcast([P, 4, P]),
                        ALU.mult).then_inc(sem("m_ready"), 1); note(sem("m_ready"))
                elif k == "job" and s[1] == "mg":
                    j = s[2]
                    was_read(pool, s)
                    gate = A((MGA if j < 8 else MGB) + j % 8)
                    pool.tensor_scalar(gate, gate, 0.5, 0.5, ALU.mult, ALU.add)\
                        .then_inc(sem("mg_ready"), 1); note(sem("mg_ready"))
                elif k == "wsplit" and on_gpsimd(s[1]):
                    remainder(pool, s[1]).then_inc(sem("w_lo_pool"), 1); note(sem("w_lo_pool"))
                elif k == "split" and parts[s[1]][4] == "P":
                    part_remainder(pool, s[1], s[2]).then_inc(sem(f"lo_{s[1]}"), 1)
                    note(sem(f"lo_{s[1]}"))
                elif k == "pads":
                    was_read(pool, ("job", "ff2", 7), "D")
                    pool.memset(ub[:, :, 0:30], 0.0).then_inc(sem("pads_ready"), 1); note(sem("pads_ready"))
                    pool.memset(bv[:, :, 0:16], 0.0).then_inc(sem("pads_ready"), 1); note(sem("pads_ready"))
                elif k == "winsum":
                    c = s[1]
                    g, w = c // 2, WINDOWS[c // 2]
                    was_read(pool, ("job", "b_val", c))
                    if c == 0:
                        pool.wait_ge(sem("pads_ready"), 2)
                    src, reach, flip = bv[:, c, :], 1, 0
                    while reach < w:
                        dst = wtmp[:, flip, :]
                        lo = 2 * reach - 1
                        link(pool.tensor_tensor(dst[:, lo:272], src[:, lo:272], src[:, lo - reach:272 - reach],
                                                ALU.add))
                        src, reach, flip = dst, 2 * reach, 1 - flip
                    link(pool.tensor_tensor(src[:, 16:32], src[:, 16:32], icnt[:, g, :], ALU.mult))
                    pool.tensor_tensor(A(DP + c), src[:, 16:272], A(DP + c), ALU.subtract)\
                        .then_inc(sem("dp_ready"), 1); note(sem("dp_ready"))
                    pool.wait_ge(sem("dp_ready"), c + 1)

        @block.scalar
        def _(act):
            act.dma_start(row[:, :], rows).then_inc(sem("row_in"), 16)
            act.dma_start(wcmp, w_cmp).then_inc(sem("wcmp_in"), 16)
            counts, last = {}, []

            def note(semaphore):
                n = str(semaphore.name)
                counts[n] = counts.get(n, 0) + 1
                last[:] = [semaphore, counts[n]]

            def settle():
                if last:
                    act.wait_ge(*last)

            def link(ins):
                ins.then_inc(sem("act_chain"), 1)
                note(sem("act_chain"))
                settle()

            def take(key):
                act.wait_ge(filled[where[key][0]], turn(key) + 1)
                return slot(key)

            act.wait_ge(sem("zeros"), SMALL_ZEROS)
            ths = [0]
            for s in steps:
                k = s[0]
                if k == "norm":
                    ps = take(s)
                    act.activation(root[:, 0, :], ps, ACT.Sqrt, bias=small[:, 0:1]).then_inc(read["mean", "A"], 1); note(read["mean", "A"])
                elif k == "tok":
                    ps = take(s)
                    act.activation(tok[:, s[1], :], ps[:, 0:TOK], ACT.Copy).then_inc(read["score", "A"], 1); note(read["score", "A"])
                elif k == "softplus":
                    act.wait_ge(read["score", "A"], 2)
                    act.activation(gates[:, :, :], tok[:, :, TOK_NG:TOK_NG + 48], ACT.Tanh, scale=0.5)\
                        .then_inc(sem("gate_tanh"), 1); note(sem("gate_tanh"))
                    act.wait_ge(sem("row_in"), 16)
                    act.activation(ea[:, :], row[:, 32:64], ACT.Exp).then_inc(sem("ea_ready"), 1); note(sem("ea_ready"))
                    act.wait_ge(sem("abs_ready"), 1)
                    act.activation(sp[:, 1, :], sp[:, 1, :], ACT.Exp, scale=-1.0).then_inc(sem("expabs_ready"), 1); note(sem("expabs_ready"))
                elif k == "acum":
                    ps = take(s)
                    act.activation(ac[:, :], ps[:, 0:96], ACT.Copy).then_inc(read["mean", "A"], 1); note(read["mean", "A"])
                    act.wait_ge(sem("decarg_ready"), 1)
                    act.activation(dec[:, :], dec[:, :], ACT.Exp).then_inc(sem("dec_ready"), 1); note(sem("dec_ready"))
                elif k == "cmp_mm":
                    ps = take(s)
                    k_cmp, v_cmp = [ps[0:64, 256 * v:256 * v + 2 * N_CMP].rearrange("p (g n) -> p g n", g=2)
                                    for v in range(2)]
                    act.wait_ge(sem("zeros"), ZEROS)
                    act.activation(kcr[0:64, 0, :, 0:N_CMP], k_cmp, ACT.Copy)
                    act.activation(kcr[64:128, 0, :, 0:N_CMP], k_cmp, ACT.Copy)
                    act.activation(kcr[0:64, 1, :, 0:N_CMP], v_cmp, ACT.Copy)\
                        .then_inc(read["score", "A"], 1); note(read["score", "A"])
                elif k == "qsq":
                    i = s[1]
                    ps = take(s)
                    act.activation(root[:, i % 2, 0:qn[i][1]], ps[:, 0:qn[i][1]], ACT.Sqrt, bias=small[:, 0:1])\
                        .then_inc(read["mean", "A"], 1); note(read["mean", "A"])
                elif k == "idx":
                    i = s[1]
                    kl = P * (i // 4 + 1)
                    ps = take(s).rearrange("p (h k) -> p h k", h=2)[:, :, 0:kl]
                    if i >= 2:
                        act.wait_ge(sem("rl_used"), i - 1)
                    act.activation(arena[:, RL + 2 * (i % 2):RL + 2 * (i % 2) + 2, 0:kl], ps, ACT.Relu)\
                        .then_inc(read["score", "A"], 1); note(read["score", "A"])
                elif k == "vcmp":
                    ps = take(s)
                    for b in range(2):
                        for g in range(2):
                            for h in range(2):
                                r = 32 * (2 * b + h)
                                ins = act.activation(vcl[r:r + N_CMP, 2 * b + g, 64 * h:64 * h + 64],
                                                     ps[32 * g:32 * g + N_CMP, 0:64], ACT.Copy)
                    ins.then_inc(read["turn", "A"], 1); note(read["turn", "A"])
                elif k == "qroot":
                    ps = take(s)
                    act.activation(root[:, 0, 0:64], ps[:, 0:64], ACT.Sqrt, bias=small[:, 0:1])\
                        .then_inc(read["mean", "A"], 1); note(read["mean", "A"])
                elif k == "pA":
                    t = s[1]
                    act.wait_ge(sem("carg_ready"), t + 1)
                    act.activation(ec[:, :, 0:N_CMP], ec[:, :, 0:N_CMP], ACT.Exp, scale=SCALE)\
                        .then_inc(sem("ce_ready"), 1); note(sem("ce_ready"))
                elif k == "pB":
                    act.activation(pct[:, s[1], :], take(s), ACT.Copy).then_inc(read["turn", "A"], 1)
                elif k == "sE":
                    i = s[1]
                    t = soft(i)[0]
                    kl = P * (t + 1)
                    act.wait_ge(sem("nmax_ready"), i + 1)
                    for h in range(2):
                        p = sbuf_s[:, i % 4, 256 * h:256 * h + kl]
                        ins = act.activation(p, p, ACT.Exp, bias=srow[:, i % 4, 2 + h:3 + h], scale=SCALE,
                                             accum_out=srow[:, i % 4, 4 + h:5 + h])
                    ins.then_inc(sem("e_ready"), 1); note(sem("e_ready"))
                elif k == "sB":
                    i = s[1]
                    t = soft(i)[0]
                    ps = take(s)
                    if i >= 2:
                        act.wait_ge(sem("pv_done"), i - 1)
                    act.activation(sbuf_t[:, i % 2, 0:256 * (t + 1)], ps[:, 0:256 * (t + 1)], ACT.Copy)\
                        .then_inc(read["turn", "A"], 1); note(read["turn", "A"])
                elif k == "sC" and s in where:
                    i = s[1]
                    t, c, _, q, _, _, _ = soft(i)
                    act.wait_ge(sem("pv_done"), i + 1)
                    act.activation(A(q + c)[:, P * t:P * t + P], slot(s)[:, 0:P], ACT.Copy)\
                        .then_inc(read["pv", "A"], 1); note(read["pv", "A"])
                elif k == "xsilu":
                    j = s[1]
                    act.wait_ge(sem("conv_done"), j + 1)
                    if j >= 3:
                        act.wait_ge(sem("silu_done"), j - 2)
                    act.activation(th[:, j % 3, :], A(XB + j), ACT.Tanh).then_inc(sem("xtanh"), 1); note(sem("xtanh"))
                elif k == "btr":
                    ps = take(s)
                    act.activation(bmt[:, :, :].rearrange("p g n -> p (g n)"), ps, ACT.Copy)\
                        .then_inc(read["turn", "A"], 1); note(read["turn", "A"])
                elif k == "cbt":
                    ps = take(s)
                    act.activation(cbt[:, s[1], :], ps, ACT.Copy).then_inc(read["score", "A"], 1); note(read["score", "A"])
                elif k == "st":
                    g = s[1]
                    ps = take(s)
                    act.activation(hst[:, 512 * g:512 * g + 512], ps, ACT.Copy).then_inc(read["score", "A"], 1); note(read["score", "A"])
                elif k == "uE":
                    i = s[1]
                    if i >= 8:
                        key = ("uA", i)
                        ps = take(key)
                        was_read(act, key, "D")
                        if i == 8:
                            act.wait_ge(sem("pv_done"), 48)
                        elif i >= 10:
                            act.wait_ge(sem("pv_done"), 48 + i - 1)
                        act.activation(sbuf_t[:, i % 2, :], ps, ACT.Exp).then_inc(read["score", "A"], 1)
                        note(read["score", "A"])
                    act.wait_ge(sem("seg_ready"), i + 1)
                    l = sbuf_s[:, i % 4, :]
                    act.activation(l, l, ACT.Exp).then_inc(sem("l_ready"), 1); note(sem("l_ready"))
                elif k == "wsplit":
                    u = s[1]
                    act.wait_ge(w_in[u % RING], 16 * (u // RING + 1))
                    if hi_before[u] is not None:
                        act.wait_ge(filled["proj"], used[hi_before[u]])
                    act.activation(ring_hi[:, hi_slot[u], :, :].rearrange("p k n -> p (k n)"),
                                   ring[:, u % RING, :, :].rearrange("p k n -> p (k n)"), ACT.Copy)\
                        .then_inc(sem("w_hi_ready"), 1); note(sem("w_hi_ready"))
                elif k == "split":
                    _, tag, c = s
                    src, hi, lo, ready, _ = parts[tag]
                    act.wait_ge(sem(ready), source_count(tag, c))
                    act.activation(hi(c), src(c), ACT.Copy).then_inc(sem(f"hi_{tag}"), 1)
                    note(sem(f"hi_{tag}"))
                elif k == "ynorm":
                    ps = take(s)
                    act.activation(root[:, 0, :], ps, ACT.Sqrt, bias=small[:, 0:1], scale=0.5).then_inc(read["mean", "A"], 1); note(read["mean", "A"])
                elif k == "ln":
                    ps = take(s)
                    act.activation(root[:, 1, :], ps, ACT.Copy).then_inc(read["mean", "A"], 1); note(read["mean", "A"])
                elif k == "lnv":
                    ps = take(s)
                    act.activation(root[:, 0, :], ps, ACT.Sqrt, bias=small[:, 1:2]).then_inc(read["mean", "A"], 1); note(read["mean", "A"])
                elif k == "lnout":
                    c = s[1]
                    act.wait_ge(sem("ln_z"), c + 1)
                    link(act.activation(A(AC + c), A(AC + c), ACT.Identity, bias=half[:, 8 + c:9 + c],
                                        scale=half[:, c:c + 1]))
                    act.activation(A(SQ + c), A(AC + c), ACT.Tanh).then_inc(sem("ln_tanh"), 1); note(sem("ln_tanh"))
                elif k == "uroot":
                    h = s[1]
                    act.wait_ge(sem("r2_ready"), h + 1)
                    act.activation(A(U2 + h), A(U2 + h), ACT.Sqrt).then_inc(sem("usqrt"), 1); note(sem("usqrt"))
                elif k == "job" and s[1] not in ON_VECTOR:
                    _, name, j = s
                    act.wait_ge(filled["proj"], filled_at[s])
                    ps = slot(s)[:, 0:S]
                    done = read["proj", "A"]
                    if name == "pool":
                        act.activation(A(HF + j), ps, ACT.Identity, bias=half[:, 56 + j:57 + j],
                                       scale=col("pool_s", j)).then_inc(done, 1); note(done)
                    elif name == "iq":
                        act.activation(A(IQ + j), ps, ACT.Copy).then_inc(done, 1); note(done)
                    elif name == "ik":
                        act.wait_ge(sem("zeros"), ZEROS)
                        for a in range(4):
                            ins = act.activation(ikz[32 * a:32 * a + 32, a, :], ps[32 * a:32 * a + 32, :], ACT.Copy)
                        ins.then_inc(done, 1); note(done)
                    elif name in ("dk", "kc", "vc", "ks", "kw"):
                        to = {"dk": DK, "kc": KC, "vc": VC, "ks": KS, "kw": KW}[name]
                        act.activation(A(to), ps, ACT.Copy).then_inc(done, 1); note(done)
                    elif name in ("dq", "nq"):
                        n = j if name == "dq" else 8 + j
                        act.activation(A((DQ if name == "dq" else NQ) + j), ps, ACT.Copy)
                        if n >= 2:
                            act.wait_ge(sem("qm_done"), n - 1)
                        act.activation(sqb[:, n % 2, :], ps, ACT.Square).then_inc(done, 1); note(done)
                    elif name in ("xbc", "xr"):
                        n = j if name == "xbc" else 24 + j
                        if n >= 3:
                            act.wait_ge(sem("conv_done"), n - 2)
                        act.activation(raw[:, n % 3, 3:3 + S], ps, ACT.Copy).then_inc(done, 1); note(done)
                    elif name == "mg":
                        if j >= 16:
                            was_read(act, ("job", "br_nsa", j - 16), "D")
                        act.activation(A((MGA if j < 8 else MGB) + j % 8), ps, ACT.Tanh, scale=0.5).then_inc(done, 1); note(done)
                    elif name == "ff1":
                        if j >= 4:
                            act.wait_ge(sem("ffs_ready"), j - 3)
                        act.activation(A(FFR + j % 4), ps, ACT.Relu).then_inc(done, 1); note(done)
                    elif name == "val_glu":
                        c = j // 2
                        if j % 2 == 0:
                            act.activation(A(VA + c), ps, ACT.Copy, scale=0.5).then_inc(done, 1); note(done)
                        else:
                            act.activation(A(TA + c), ps, ACT.Tanh, scale=0.5).then_inc(done, 1); note(done)
                    elif name == "b_val":
                        if j == 0:
                            act.wait_ge(sem("pads_ready"), 2)
                        act.activation(A(DP + j), ps, ACT.Copy)
                        act.activation(bv[:, j, 16:16 + S], ps, ACT.Copy, scale=1.0 / WINDOWS[j // 2]).then_inc(done, 1); note(done)
                    elif name in ("sz", "a_gate", "b_gate", "gate"):
                        to = {"sz": SZ, "a_gate": GA, "b_gate": GB, "gate": GG}[name]
                        if name == "sz" and j == 0:
                            act.wait_ge(sem("kk_ready"), 4)
                        act.activation(A(to + j), ps, ACT.Copy, scale=0.5)
                        b = ths[0]
                        ths[0] += 1
                        if b == 0:
                            act.wait_ge(sem("silu_done"), 24)
                        if b >= 3:
                            act.wait_ge(sem("gated"), b - 2)
                        act.activation(th[:, b % 3, :], ps, ACT.Tanh, scale=0.5).then_inc(done, 1); note(done)
                    elif name == "rg_ig":
                        h = j // 2
                        if j % 2 == 0:
                            link(act.activation(A(U2 + h), ps, ACT.Tanh, bias=half[:, 16 + h:17 + h], scale=0.5))
                            act.activation(A(U2 + h), A(U2 + h), ACT.Tanh, bias=half[:, 40 + h:41 + h],
                                           scale=half[:, 40 + h:41 + h]).then_inc(done, 1); note(done)
                        else:
                            act.activation(A(TI + h), ps, ACT.Tanh, bias=half[:, 28 + h:29 + h], scale=0.5)\
                                .then_inc(done, 1); note(done)

        @block.vector
        def _(dve):
            counts, last = {}, []

            def note(semaphore):
                n = str(semaphore.name)
                counts[n] = counts.get(n, 0) + 1
                last[:] = [semaphore, counts[n]]

            def settle():
                if last:
                    dve.wait_ge(*last)

            def link(ins):
                ins.then_inc(sem("dve_chain"), 1)
                note(sem("dve_chain"))
                settle()

            def pair(ins):
                ins.then_inc(sem("dve_chain"), 1)
                note(sem("dve_chain"))
                dve.wait_ge(sem("dve_chain"), counts[str(sem("dve_chain").name)] - 1)

            def take(key):
                dve.wait_ge(filled[where[key][0]], turn(key) + 1)
                return slot(key)


            zeros = [0]

            def fill(ap, value):
                dve.memset(ap, value).then_inc(sem("zeros"), 1)
                note(sem("zeros"))
                zeros[0] += 1

            fill(mean_d[:, :], 1.0 / D)
            fill(small[:, 0:1], 1e-6)
            fill(small[:, 1:2], 1e-5)
            fill(ones[:, :], 1.0)
            fill(ident[:, :], 0.0)
            fill(caus[:, :, :], 0.0)
            fill(jneg[:, :], 0.0)
            fill(cneg[:, :, :], 0.0)
            fill(cvis[:, :, :], 1.0)
            fill(mean_h[:, 0:64], 0.0)
            fill(mean_h[:, 64:128], 0.0)
            dve.wait_ge(sem("zeros"), zeros[0])
            fill(mean_h[0:64, 0:64], 1.0 / HD)
            fill(mean_h[64:128, 64:128], 1.0 / HD)
            assert zeros[0] == SMALL_ZEROS
            dve.wait_ge(sem("par_in"), 16)
            link(dve.tensor_scalar(half[:, 0:16], par[:, AT["ln_g"]:AT["ln_g"] + 16], 0.5, None, ALU.mult))
            link(dve.tensor_scalar(half[:, 16:40], par[:, AT["b_rg"]:AT["b_rg"] + 24], 0.5, None, ALU.mult))
            link(dve.tensor_scalar(half[:, 64:160], par[:, AT["ssd_cw"]:AT["ssd_cw"] + 96], 0.5, None, ALU.mult))
            link(dve.tensor_scalar(par[:, AT["ssd_cb"]:AT["ssd_cb"] + 24], par[:, AT["ssd_cb"]:AT["ssd_cb"] + 24],
                                   0.5, None, ALU.mult))
            link(dve.tensor_tensor(half[:, 56:64], par[:, AT["pool_b"]:AT["pool_b"] + 8],
                                   par[:, AT["pool_s"]:AT["pool_s"] + 8], ALU.mult))
            link(dve.tensor_tensor(half[:, 52:53], col("dk_g"), col("dq_g"), ALU.mult))
            link(dve.tensor_scalar(half[:, 53:56], par[:, AT["nk_g"]:AT["nk_g"] + 3], col("nq_g"), None, ALU.mult))
            sq = sem("sq_ready")
            ths = [0]
            for s in steps:
                k = s[0]
                settle()
                if k == "norm":
                    q = s[1]
                    h = HF0 if q == 0 else HF
                    if q == 0:
                        dve.wait_ge(sem("x_in"), 16)
                    for c in range(8):
                        dve.tensor_tensor(A(h + c), A(XT + c), A(XT + c), ALU.mult).then_inc(sq, 1); note(sq)
                    was_read(dve, s)
                    link(dve.reciprocal(rinv[:, :], root[:, 0, :]))
                    g = ("norm1", "norm2", "even_g", "odd_g", "final_g")[q]
                    for c in range(8):
                        dve.scalar_tensor_tensor(out=A(h + c), in0=A(XT + c), scalar=col(g, c), in1=rinv[:, :],
                                                 op0=ALU.mult, op1=ALU.mult).then_inc(sem("hf_ready"), 1)
                        note(sem("hf_ready"))
                elif k == "wsplit" and not on_gpsimd(s[1]):
                    remainder(dve, s[1]).then_inc(sem("w_lo_dve"), 1); note(sem("w_lo_dve"))
                elif k == "split" and parts[s[1]][4] == "D":
                    part_remainder(dve, s[1], s[2]).then_inc(sem(f"lo_{s[1]}"), 1)
                    note(sem(f"lo_{s[1]}"))
                elif k == "ffsq":
                    j = s[1]
                    was_read(dve, ("job", "ff1", j))
                    if j >= 4:
                        dve.wait_ge(sem("hi_ff"), j - 3)
                    dve.tensor_tensor(A(FFS + j % 4), A(FFR + j % 4), A(FFR + j % 4), ALU.mult)\
                        .then_inc(sem("ffs_ready"), 1); note(sem("ffs_ready"))
                elif k == "fills":
                    for tile in (kcr, raw, kk_d, kk_s, kk_w, kk_c, vcl):
                        fill(tile[:], 0.0)
                    fill(ikz, 0.0)
                    assert zeros[0] == ZEROS
                elif k == "softplus":
                    dve.wait_ge(sem("zeros"), ZEROS)
                    was_read(dve, ("tok", 1))
                    dve.wait_ge(sem("row_in"), 16)
                    for t in range(NT):
                        dve.tensor_tensor(sp[:, 0, 32 * t:32 * t + 32], tok[:, t, TOK_DT:TOK_DT + 32], row[:, 0:32],
                                          ALU.add)
                    link(dve.tensor_scalar(sp[:, 0, 64:76], par[:, AT["lam"]:AT["lam"] + 12], -1.0, None, ALU.mult))
                    dve.scalar_tensor_tensor(out=sp[:, 1, :], in0=sp[:, 0, :], scalar=-1.0, in1=sp[:, 0, :],
                                             op0=ALU.mult, op1=ALU.max)\
                        .then_inc(sem("abs_ready"), 1); note(sem("abs_ready"))
                    dve.wait_ge(sem("gate_tanh"), 1)
                    dve.tensor_scalar(gates[:, :, :], gates[:, :, :], 0.5, 0.5, ALU.mult, ALU.add)\
                        .then_inc(sem("gates_ready"), 1); note(sem("gates_ready"))
                    z, y, y2, acc = sp[:, 1, :], sp[:, 2, :], sp[:, 3, :], sp[:, 4, :]
                    dve.wait_ge(sem("expabs_ready"), 1)
                    link(dve.tensor_scalar(y2, z, 2.0, None, ALU.add))
                    link(dve.reciprocal(y, y2))
                    link(dve.tensor_tensor(y, y, z, ALU.mult))
                    link(dve.tensor_tensor(y2, y, y, ALU.mult))
                    link(dve.tensor_scalar(acc, y2, 1.0 / 17, None, ALU.mult))
                    for m in (15, 13, 11, 9, 7, 5, 3):
                        link(dve.scalar_tensor_tensor(out=acc, in0=acc, scalar=1.0 / m, in1=y2,
                                                      op0=ALU.add, op1=ALU.mult))
                    link(dve.scalar_tensor_tensor(out=acc, in0=acc, scalar=1.0, in1=y, op0=ALU.add, op1=ALU.mult))
                    link(dve.tensor_scalar(y, sp[:, 0, :], 0.0, None, ALU.max))
                    link(dve.scalar_tensor_tensor(out=sp[:, 5, :], in0=acc, scalar=2.0, in1=y,
                                                  op0=ALU.mult, op1=ALU.add))
                    link(dve.tensor_scalar(half[:, 40:52], sp[:, 5, 64:76], 2.0, None, ALU.mult))
                    dve.wait_ge(sem("ea_ready"), 1)
                    for t in range(NT):
                        dve.scalar_tensor_tensor(out=dta[:, 32 * t:32 * t + 32], in0=sp[:, 5, 32 * t:32 * t + 32],
                                                 scalar=-1.0, in1=ea[:, :], op0=ALU.mult, op1=ALU.mult)\
                            .then_inc(sem("dta_ready"), 1); note(sem("dta_ready"))
                elif k == "acum":
                    was_read(dve, s)
                    dve.tensor_tensor(dec[:, :], ac[:, 64:96], ac[:, 0:32], ALU.subtract)\
                        .then_inc(sem("decarg_ready"), 1); note(sem("decarg_ready"))
                elif k == "cmp_in":
                    for v, src in ((0, KC), (1, VC)):
                        was_read(dve, ("job", ("kc", "vc")[v], 0))
                        view = A(src).rearrange("p (m b) -> p b m", b=16)
                        for a in range(2):
                            at = AT["cmp_pos"] + 32 * v + 16 * a
                            for g in range(2):
                                r = slice(64 * g, 64 * g + 64)
                                for odd in range(2):
                                    pos = par[r, at + odd:at + 16:2].unsqueeze(2).to_broadcast([64, 8, N_CMP])
                                    ins = dve.tensor_tensor(kcp[64 * odd:64 * odd + 64, v, 8 * a:8 * a + 8, g, :],
                                                            view[r, odd::2, a:a + N_CMP], pos, ALU.add)
                    ins.then_inc(sem("kcp_ready"), 1)
                    note(sem("kcp_ready"))
                elif k == "qsq":
                    i = s[1]
                    src, w, _ = qn[i]
                    was_read(dve, ("cmp_mm",) if i == 3 else ("job", ("dk", "ks", "kw")[i], 0))
                    dve.tensor_tensor(sqb[:, i % 2, 0:w], src, src, ALU.mult).then_inc(sem("qsq_ready"), 1); note(sem("qsq_ready"))
                elif k == "qap":
                    i = s[1]
                    src, w, gain = qn[i]
                    was_read(dve, ("qsq", i))
                    link(dve.reciprocal(rinv[:, 0:w], root[:, i % 2, 0:w]))
                    kk = (kk_d, kk_s, kk_w, kk_c)[i]
                    for half_in in range(2):
                        a = 64 * half_in
                        for half_out in ((half_in,) if i == 0 else (0, 1)):
                            b = 64 * half_out
                            dst = kk[b:b + 64, half_out, :] if i == 0 else kk[b:b + 64, half_in, half_out, :]
                            rows_in, cut = slice(a, a + 64), slice(0, w)
                            if i == 3:
                                rows_in, cut = slice(b, b + 64), slice(32 * half_in, 32 * half_in + 32)
                            ins = dve.scalar_tensor_tensor(
                                out=dst, in0=src[rows_in, cut], scalar=half[rows_in, gain:gain + 1],
                                in1=rinv[rows_in, cut], op0=ALU.mult, op1=ALU.mult)
                    ins.then_inc(sem("kk_ready"), 1); note(sem("kk_ready"))
                elif k == "idx":
                    i = s[1]
                    t = i // 4
                    kl = P * (t + 1)
                    was_read(dve, s)
                    for h in range(2):
                        head = 2 * (i % 4) + h
                        rl = arena[:, RL + 2 * (i % 2) + h, 0:kl]
                        iw = tok[:, t, TOK_IW + head:TOK_IW + head + 1]
                        acc = A(IDX + t)[:, 0:kl]
                        if head == 0:
                            ins = dve.tensor_scalar(acc, rl, iw, None, ALU.mult)
                        else:
                            ins = dve.scalar_tensor_tensor(out=acc, in0=rl, scalar=iw, in1=acc,
                                                           op0=ALU.mult, op1=ALU.add)
                        if h == 0:
                            link(ins)
                    ins.then_inc(sem("rl_used"), 1); note(sem("rl_used"))
                    dve.wait_ge(sem("rl_used"), i + 1)
                elif k == "select":
                    t = s[1]
                    kl = P * (t + 1)
                    dve.wait_ge(sem("consts"), CONSTS)
                    acc = A(IDX + t)[:, 0:kl]
                    link(dve.tensor_tensor(acc, acc, caus[:, t, 0:kl], ALU.add))
                    for _ in range(TOPK // 8):
                        link(dve.max(m8[:, :], acc))
                        link(dve.match_replace(acc, m8[:, :], acc, MARK))
                    link(dve.tensor_scalar(acc, acc, MARK, 1.0, ALU.is_equal, ALU.subtract))
                    dve.scalar_tensor_tensor(out=dmask[:, t, 0:kl], in0=acc, scalar=-NEG, in1=caus[:, t, 0:kl],
                                             op0=ALU.mult, op1=ALU.add).then_inc(sem("select_done"), 1); note(sem("select_done"))
                    dve.wait_ge(sem("select_done"), t + 1)
                elif k == "qroot":
                    was_read(dve, ("qroot",))
                    link(dve.reciprocal(rq[:, :], root[:, 0, 0:64]))
                elif k == "pA":
                    t = s[1]
                    if t == 0:
                        link(dve.memset(pc, 0.0))
                    ps = take(s).rearrange("p (h n) -> p h n", h=16)[:, :, 0:N_CMP]
                    e = ec[:, :, 0:N_CMP]
                    r = rq[:, 32 * t + 16:32 * t + 32]
                    dve.tensor_tensor(e, ps, r.unsqueeze(2).to_broadcast([P, 16, N_CMP]), ALU.mult)\
                        .then_inc(read["score", "D"], 1); note(read["score", "D"])
                    settle()
                    link(dve.tensor_tensor(e, e, cneg[:, t, 0:N_CMP].unsqueeze(1).to_broadcast([P, 16, N_CMP]),
                                           ALU.add))
                    link(dve.tensor_reduce(crow[:, 0, :], e, AX.X, ALU.max))
                    dve.tensor_tensor(e, e, crow[:, 0, :].unsqueeze(2).to_broadcast([P, 16, N_CMP]),
                                      ALU.subtract).then_inc(sem("carg_ready"), 1); note(sem("carg_ready"))
                elif k == "pB":
                    t = s[1]
                    e = ec[:, :, 0:N_CMP]
                    dve.wait_ge(sem("ce_ready"), t + 1)
                    link(dve.tensor_reduce(crow[:, 1, :], e, AX.X, ALU.add))
                    link(dve.reciprocal(crow[:, 2, :], crow[:, 1, :]))
                    link(dve.tensor_tensor(crow[:, 2, :], crow[:, 2, :],
                                           gates[:, t, :].rearrange("p (h j) -> p h j", j=3)[:, :, 0], ALU.mult))
                    link(dve.tensor_tensor(e, e, cvis[:, t, 0:N_CMP].unsqueeze(1).to_broadcast([P, 16, N_CMP]),
                                           ALU.mult))
                    if t == 1:
                        dve.wait_ge(filled["turn"], turn(("pB", 0)) + 1)
                    dve.tensor_tensor(pc[:, :, 0:N_CMP], e, crow[:, 2, :].unsqueeze(2).to_broadcast([P, 16, N_CMP]),
                                      ALU.mult).then_inc(sem("pc_ready"), 1); note(sem("pc_ready"))
                elif k == "sA":
                    i = s[1]
                    t, c, kk, q, mask, v, gate = soft(i)
                    kl = P * (t + 1)
                    ps = take(s).rearrange("p (h k) -> p h k", h=2)[:, :, 0:kl]
                    x = sbuf_s[:, i % 4, :].rearrange("p (h k) -> p h k", h=2)[:, :, 0:kl]
                    if i >= 4:
                        dve.wait_ge(filled["turn"], turn(("sB", i - 4)) + 1)
                    for h in range(2):
                        n = 32 * t + (0 if gate is None else 16) + 2 * c + h
                        ins = dve.scalar_tensor_tensor(out=x[:, h, :], in0=ps[:, h, :], scalar=rq[:, n:n + 1],
                                                       in1=mask[:, t, 0:kl], op0=ALU.mult, op1=ALU.add)
                    ins.then_inc(read["score", "D"], 1)
                    note(read["score", "D"])
                    settle()
                    link(dve.tensor_reduce(srow[:, i % 4, 0:2], x, AX.X, ALU.max))
                    dve.tensor_scalar(srow[:, i % 4, 2:4], srow[:, i % 4, 0:2], -SCALE, None, ALU.mult)\
                        .then_inc(sem("nmax_ready"), 1); note(sem("nmax_ready"))
                elif k == "sR":
                    i = s[1]
                    t, c, _, _, _, _, gate = soft(i)
                    dve.wait_ge(sem("e_ready"), i + 1)
                    ins = dve.reciprocal(srow[:, i % 4, 6:8], srow[:, i % 4, 4:6])
                    if gate is not None:
                        link(ins)
                        gt = gates[:, t, :].rearrange("p (h j) -> p h j", j=3)[:, 2 * c:2 * c + 2, gate]
                        ins = dve.tensor_tensor(srow[:, i % 4, 6:8], srow[:, i % 4, 6:8], gt, ALU.mult)
                    ins.then_inc(sem("scale_ready"), 1); note(sem("scale_ready"))
                elif k in ("xconv", "oconv"):
                    j = s[1]
                    n = j if k == "xconv" else 24 + j
                    was_read(dve, ("job", "xbc" if k == "xconv" else "xr", j))
                    dst = A((XB if k == "xconv" else XC) + j)
                    for tap in range(4):
                        w = half[:, 64 + 4 * j + tap:65 + 4 * j + tap] if k == "xconv" else col("odd_cw", 4 * j + tap)
                        src = raw[:, n % 3, tap:tap + S]
                        if tap == 0:
                            link(dve.tensor_scalar(dst, src, w, col("ssd_cb" if k == "xconv" else "odd_cb", j),
                                                   ALU.mult, ALU.add))
                        else:
                            ins = dve.scalar_tensor_tensor(out=dst, in0=src, scalar=w, in1=dst,
                                                           op0=ALU.mult, op1=ALU.add)
                            if tap < 3:
                                link(ins)
                    ins.then_inc(sem("conv_done"), 1); note(sem("conv_done"))
                elif k == "xsilu":
                    j = s[1]
                    dve.wait_ge(sem("xtanh"), j + 1)
                    dve.scalar_tensor_tensor(out=A(XB + j), in0=th[:, j % 3, :], scalar=1.0, in1=A(XB + j),
                                             op0=ALU.add, op1=ALU.mult).then_inc(sem("silu_done"), 1); note(sem("silu_done"))
                elif k == "xtr":
                    i = s[1]
                    t, q = i // 4, i % 4
                    ps = take(s)
                    dve.tensor_tensor(
                        xd[t][:, 512 * q:512 * q + 512].rearrange("p (h e) -> p h e", h=8),
                        ps[:, :].rearrange("p (h e) -> p h e", h=8),
                        sp[:, 5, 32 * t + 8 * q:32 * t + 8 * q + 8].unsqueeze(2).to_broadcast([P, 8, 64]),
                        ALU.mult).then_inc(read["turn", "D"], 1); note(read["turn", "D"])
                elif k == "uA":
                    i = s[1]
                    t, hq = i // 8, i % 8
                    ps = take(s).rearrange("p (h i) -> p h i", h=4)
                    x = sbuf_s[:, i % 4, :].rearrange("p (h i) -> p h i", h=4)
                    if i >= 4:
                        dve.wait_ge(sem("pv_done"), 48 + i - 3)
                    else:
                        dve.wait_ge(sem("pv_done"), 48)
                    dve.tensor_tensor(x, ps, ac[:, 32 * t + 4 * hq:32 * t + 4 * hq + 4].unsqueeze(2)
                                      .to_broadcast([P, 4, P]), ALU.subtract).then_inc(read["score", "D"], 1); note(read["score", "D"])
                    dve.wait_ge(read["score", "D"], sum("D" in r for r in turns["score"][:turn(s) + 1]))
                    dve.tensor_tensor(x, x, jneg[:, :].unsqueeze(1).to_broadcast([P, 4, P]), ALU.add)\
                        .then_inc(sem("seg_ready"), 1); note(sem("seg_ready"))
                elif k == "uB":
                    i = s[1]
                    t, hq = i // 8, i % 8
                    dve.wait_ge(sem("pv_done"), 48 + i + 1)
                    ps = slot(s)
                    if i == 0:
                        dve.wait_ge(sem("gated"), 16)
                    for cc in range(2):
                        c = 2 * hq + cc
                        xs = A(XB + c)[:, P * t:P * t + P]
                        ins = dve.scalar_tensor_tensor(out=ytmp[:, cc, :], in0=xs, scalar=col("ssd_d", c),
                                                       in1=ps[:, P * cc:P * cc + P], op0=ALU.mult, op1=ALU.add)
                    ins.then_inc(read["pv", "D"], 1); note(read["pv", "D"])
                    dve.wait_ge(read["pv", "D"], i + 1)
                    for cc in range(2):
                        c = 2 * hq + cc
                        ins = dve.tensor_tensor(A(XB + c)[:, P * t:P * t + P], ytmp[:, cc, :],
                                                A(SZ + c)[:, P * t:P * t + P], ALU.mult)
                    link(ins)
                elif k == "ynorm":
                    for c in range(16):
                        dve.tensor_tensor(A(XD + c), A(XB + c), A(XB + c), ALU.mult).then_inc(sem("ysq_ready"), 1); note(sem("ysq_ready"))
                    was_read(dve, s)
                    link(dve.reciprocal(rinv[:, :], root[:, 0, :]))
                    for c in range(16):
                        dve.scalar_tensor_tensor(out=A(SZ + c), in0=A(XB + c), scalar=col("ssd_g", c),
                                                 in1=rinv[:, :], op0=ALU.mult, op1=ALU.mult)\
                            .then_inc(sem("yf_ready"), 1); note(sem("yf_ready"))
                elif k == "econv":
                    c, eighth = s[1] // 8 * 2, s[1] % 8
                    if eighth == 0:
                        was_read(dve, ("job", "val_glu", 2 * c + 3))
                        if c == 0:
                            dve.wait_ge(sem("pads_ready"), 2)
                        for cc in (c, c + 1):
                            pair(dve.scalar_tensor_tensor(out=ub[:, cc, 30:30 + S], in0=A(TA + cc), scalar=1.0,
                                                          in1=A(VA + cc), op0=ALU.add, op1=ALU.mult))
                        for cc in (c, c + 1):
                            pair(dve.tensor_scalar(A(AC + cc), ub[:, cc, 0:S], col("even_cw", CONV_K * cc),
                                                   col("even_cb", cc), ALU.mult, ALU.add))
                    for tap in range(4 * eighth + (eighth == 0), min(4 * eighth + 4, CONV_K)):
                        if tap == CONV_K - 1:
                            settle()
                        for cc in (c, c + 1):
                            ins = dve.scalar_tensor_tensor(out=A(AC + cc), in0=ub[:, cc, tap:tap + S],
                                                           scalar=col("even_cw", CONV_K * cc + tap), in1=A(AC + cc),
                                                           op0=ALU.mult, op1=ALU.add)
                            if tap < CONV_K - 1:
                                pair(ins)
                            else:
                                ins.then_inc(sem("econv_done"), 1); note(sem("econv_done"))
                elif k == "ln":
                    was_read(dve, s)
                    for c in range(8):
                        ins = dve.tensor_tensor(A(AC + c), A(AC + c), root[:, 1, :], ALU.subtract)
                    link(ins)
                    for c in range(8):
                        dve.tensor_tensor(A(SQ + c), A(AC + c), A(AC + c), ALU.mult).then_inc(sem("lsq_ready"), 1); note(sem("lsq_ready"))
                elif k == "lnv":
                    was_read(dve, s)
                    link(dve.reciprocal(rinv[:, :], root[:, 0, :]))
                    for c in range(8):
                        dve.tensor_tensor(A(AC + c), A(AC + c), rinv[:, :], ALU.mult).then_inc(sem("ln_z"), 1); note(sem("ln_z"))
                elif k == "lnout":
                    c = s[1]
                    dve.wait_ge(sem("ln_tanh"), c + 1)
                    link(dve.scalar_tensor_tensor(out=A(SQ + c), in0=A(SQ + c), scalar=1.0, in1=A(AC + c),
                                                  op0=ALU.add, op1=ALU.mult))
                    dve.tensor_tensor(A(SQ + c), A(SQ + c), A(GA + c), ALU.mult)\
                        .then_inc(sem("yaf_ready"), 1); note(sem("yaf_ready"))
                elif k == "lru":
                    h = s[1]
                    was_read(dve, ("job", "rg_ig", 2 * h + 1))
                    link(dve.tensor_scalar(A(LA + h), A(U2 + h), 1.0, None, ALU.add))
                    dve.reciprocal(A(R2 + h), A(LA + h)).then_inc(sem("r2_ready"), 1); note(sem("r2_ready"))
                    dve.wait_ge(sem("r2_ready"), h + 1)
                    dve.tensor_scalar(A(LA + h), A(R2 + h), 2.0, -1.0, ALU.mult, ALU.add)
                    link(dve.scalar_tensor_tensor(out=A(W1 + h), in0=A(TI + h), scalar=1.0, in1=A(XC + h),
                                                  op0=ALU.add, op1=ALU.mult))
                elif k == "scanout":
                    h = s[1]
                    dve.wait_ge(sem("gated"), 32 + h + 1)
                    dve.tensor_tensor(A(GG + h), A(TI + h), A(GG + h), ALU.mult)\
                        .then_inc(sem("lyf_ready"), 1); note(sem("lyf_ready"))
                elif k == "scan":
                    h = s[1]
                    dve.wait_ge(sem("usqrt"), h + 1)
                    link(dve.tensor_tensor(A(R2 + h), A(R2 + h), A(U2 + h), ALU.mult))
                    link(dve.tensor_tensor(A(W1 + h), A(W1 + h), A(R2 + h), ALU.mult))
                    link(dve.tensor_tensor_scan(A(TI + h), A(LA + h), A(W1 + h), 0.0, ALU.mult, ALU.add))
                elif k == "job" and s[1] in ("sz", "a_gate", "b_gate", "gate"):
                    to = {"sz": SZ, "a_gate": GA, "b_gate": GB, "gate": GG}[s[1]] + s[2]
                    b = ths[0]
                    ths[0] += 1
                    was_read(dve, s)
                    dve.scalar_tensor_tensor(out=A(to), in0=th[:, b % 3, :], scalar=1.0, in1=A(to),
                                             op0=ALU.add, op1=ALU.mult).then_inc(sem("gated"), 1); note(sem("gated"))
                elif k == "job" and s[1] == "pool":
                    j = s[2]
                    was_read(dve, s)
                    dve.tensor_tensor(A(GB + j), A(HF + j), A(GB + j), ALU.mult)\
                        .then_inc(sem("ybf_ready"), 1); note(sem("ybf_ready"))
                elif k == "job" and s[1] in ON_VECTOR:
                    _, name, j = s
                    dve.wait_ge(filled["proj"], filled_at[s])
                    ps = slot(s)[:, 0:S]
                    done = read["proj", "D"]
                    mine = sum("D" in r for r in turns["proj"][:turn(s) + 1])
                    if name == "br_dsa":
                        dve.wait_ge(sem("mg_ready"), j + 1)
                        dve.tensor_tensor(A(MGA + j), ps, A(MGA + j), ALU.mult).then_inc(done, 1); note(done)
                    elif name in ("br_nsa", "br_ssd"):
                        dve.wait_ge(sem("mg_ready"), (9 if name == "br_nsa" else 17) + j)
                        dve.tensor_tensor(sqb[:, 0, :], ps, A(MGB + j), ALU.mult).then_inc(done, 1); note(done)
                        dve.wait_ge(done, mine)
                        ins = dve.tensor_tensor(A(MGA + j), A(MGA + j), sqb[:, 0, :], ALU.add)
                        if name == "br_nsa":
                            link(ins)
                        else:
                            ins.then_inc(sem("mixf_ready"), 1); note(sem("mixf_ready"))
                    else:
                        dve.tensor_tensor(A(XT + j), A(XT + j), ps, ALU.add).then_inc(done, 1); note(done)
                        dve.wait_ge(done, mine)

        @block.tensor
        def _(pe):
            pe.wait_ge(sem("zeros"), SMALL_ZEROS)


            for s in steps:
                k = s[0]
                if k == "norm":
                    q = s[1]
                    readers_done(pe, s)
                    for c in range(8):
                        pe.wait_ge(sem("sq_ready"), 8 * q + c + 1)
                        mm = pe.matmul(slot(s), mean_d[:, :], A((HF0 if q == 0 else HF) + c),
                                       start=(c == 0), stop=(c == 7))
                    mm.then_inc(filled["mean"], 1)
                elif k == "tok":
                    t = s[1]
                    readers_done(pe, s)
                    if t == 0:
                        pe.wait_ge(sem("wtok_in"), 16)
                    for c in range(8):
                        pe.wait_ge(sem("hf_ready"), c + 1)
                        mm = pe.matmul(slot(s)[:, 0:TOK], A(HF0 + c)[:, P * t:P * t + P], wtok[:, c, :],
                                       start=(c == 0), stop=(c == 7))
                    mm.then_inc(filled["score"], 1)
                elif k == "acum":
                    readers_done(pe, s)
                    pe.wait_ge(sem("consts"), CONSTS)
                    pe.wait_ge(sem("dta_ready"), 2)
                    ps = slot(s)
                    pe.matmul(ps[:, 0:64], upper[:, :], dta[:, :], start=True, stop=True)
                    pe.matmul(ps[:, 64:96], ones[:, :], dta[:, 0:32], start=True, stop=True)\
                        .then_inc(filled["mean"], 1)
                elif k == "cmp_mm":
                    readers_done(pe, s)
                    pe.wait_ge(sem("wcmp_in"), 16)
                    pe.wait_ge(sem("kcp_ready"), 1)
                    for v in range(2):
                        for m in range(16):
                            mm = pe.matmul(slot(s)[0:64, 256 * v:256 * v + 2 * N_CMP], wcmp[:, v, m, :],
                                           kcp[:, v, m, :, :].rearrange("p g n -> p (g n)"),
                                           start=(m == 0), stop=(m == 15))
                    mm.then_inc(filled["score"], 1)
                elif k == "qsq":
                    i = s[1]
                    w = qn[i][1]
                    readers_done(pe, s)
                    pe.wait_ge(sem("qsq_ready"), i + 1)
                    pe.matmul(slot(s)[:, 0:w], mean_h[:, :], sqb[:, i % 2, 0:w], start=True, stop=True)\
                        .then_inc(filled["mean"], 1)
                elif k == "idx":
                    i = s[1]
                    t, m, pair = i // 4, (i % 4) // 2, i % 2
                    kl = P * (t + 1)
                    readers_done(pe, s)
                    was_read(pe, ("job", "ik", 0))
                    ps = slot(s).rearrange("p (h k) -> p h k", h=2)[:, :, 0:kl]
                    pe.matmul(ps, A(IQ + m)[:, P * t:P * t + P], ikz[:, 2 * pair:2 * pair + 2, 0:kl],
                              start=True, stop=True).then_inc(filled["score"], 1)
                elif k == "vcmp":
                    readers_done(pe, s)
                    was_read(pe, ("cmp_mm",))
                    pe.transpose(slot(s)[0:64, 0:64], kcr[0:64, 1, :, :].rearrange("p g n -> p (g n)"),
                                 ident[0:64, 0:64]).then_inc(filled["turn"], 1)
                elif k == "qm":
                    n = s[1]
                    key = ("qroot",)
                    if n == 0:
                        readers_done(pe, key)
                    was_read(pe, ("job", "dq" if n < 8 else "nq", n % 8))
                    for t in range(NT):
                        mm = pe.matmul(slot(key)[:, 32 * t + 2 * n:32 * t + 2 * n + 2],
                                       sqb[:, n % 2, P * t:P * t + P], mean_h[:, 0:P:64], start=True, stop=True)
                    mm.then_inc(sem("qm_done") if n < 15 else filled["mean"], 1)
                elif k == "pA":
                    t = s[1]
                    readers_done(pe, s)
                    pe.wait_ge(sem("kk_ready"), 4)
                    for c in range(8):
                        mm = pe.matmul(slot(s)[:, 64 * c:64 * c + 64], A(NQ + c)[:, P * t:P * t + P],
                                       kk_c[:, c // 4, :, :].rearrange("p h n -> p (h n)"), start=True, stop=True)
                    mm.then_inc(filled["score"], 1)
                elif k == "pB":
                    t = s[1]
                    readers_done(pe, s)
                    pe.wait_ge(sem("pc_ready"), t + 1)
                    for m in range(4):
                        mm = pe.transpose(slot(s)[:, P * m:P * m + P],
                                          pc[:, 4 * m:4 * m + 4, :].rearrange("p h n -> p (h n)"), ident[:, :])
                    mm.then_inc(filled["turn"], 1)
                elif k == "sA":
                    i = s[1]
                    t, c, kk, q, mask, v, gate = soft(i)
                    kl = P * (t + 1)
                    readers_done(pe, s)
                    if i == 0:
                        pe.wait_ge(sem("kk_ready"), 4)
                    if i < 16 and i % 8 == 0:
                        pe.wait_ge(sem("select_done"), t + 1)
                    ps = slot(s).rearrange("p (h k) -> p h k", h=2)[:, :, 0:kl]
                    pe.matmul(ps, A(q + c)[:, P * t:P * t + P], kk[:, :, 0:kl], start=True, stop=True)\
                        .then_inc(filled["score"], 1)
                elif k == "sB":
                    i = s[1]
                    t = soft(i)[0]
                    readers_done(pe, s)
                    pe.wait_ge(sem("p_ready"), i + 1)
                    for kt in range(t + 1):
                        for h in range(2):
                            n = 2 * kt + h
                            mm = pe.transpose(slot(s)[:, P * n:P * n + P],
                                              sbuf_s[:, i % 4, 256 * h + P * kt:256 * h + P * kt + P], ident[:, :])
                    mm.then_inc(filled["turn"], 1)
                elif k == "sC":
                    i = s[1]
                    t, c, _, _, _, v, gate = soft(i)
                    closes = ("sC", i if i < 16 or i % 2 else i + 1)
                    ps = slot(closes)
                    if gate in (None, 1):
                        readers_done(pe, closes)
                    if gate == 1:
                        was_read(pe, ("pB", t))
                        pe.matmul(ps[:, 0:P], vcl[:, 2 * (c % 2) + c // 4, :], pct[:, t, P * (c // 2):P * (c // 2) + P],
                                  start=True, stop=False, skip_group_check=True)
                    was_read(pe, ("sB", i))
                    for h in range(2):
                        for kt in range(t + 1):
                            n = 2 * kt + h
                            mm = pe.matmul(ps[64 * h:64 * h + 64, 0:P], tok[:, kt, v:v + 64],
                                           sbuf_t[:, i % 2, P * n:P * n + P], start=(gate is None and kt == 0),
                                           stop=(kt == t and gate in (None, 2)), skip_group_check=True)
                    mm.then_inc(sem("pv_done"), 1)
                elif k == "xtr":
                    i = s[1]
                    t, q = i // 4, i % 4
                    readers_done(pe, s)
                    if i == 0:
                        pe.wait_ge(sem("silu_done"), 24)
                    for m in range(4):
                        mm = pe.transpose(slot(s)[:, P * m:P * m + P], A(XB + 4 * q + m)[:, P * t:P * t + P],
                                          ident[:, :])
                    mm.then_inc(filled["turn"], 1)
                elif k == "btr":
                    readers_done(pe, s)
                    for g in range(4):
                        mm = pe.transpose(slot(s)[:, P * g:P * g + P], A(XB + 16 + g)[:, 0:P], ident[:, :])
                    mm.then_inc(filled["turn"], 1)
                elif k == "cbt":
                    t = s[1]
                    readers_done(pe, s)
                    for g in range(4):
                        mm = pe.matmul(slot(s)[:, P * g:P * g + P], A(XB + 16 + g)[:, P * t:P * t + P],
                                       A(XB + 20 + g)[:, P * t:P * t + P], start=True, stop=True)
                    mm.then_inc(filled["score"], 1)
                elif k == "st":
                    g = s[1]
                    readers_done(pe, s)
                    was_read(pe, ("btr",))
                    pe.wait_ge(sem("xw_ready"), g + 1)
                    pe.matmul(slot(s)[:, :], bmt[:, g, :], xw[:, 512 * (g % 2):512 * (g % 2) + 512], start=True, stop=True)\
                        .then_inc(filled["score"], 1)
                elif k == "uA":
                    i = s[1]
                    t, hq = i // 8, i % 8
                    readers_done(pe, s)
                    for h in range(4):
                        n = 32 * t + 4 * hq + h
                        mm = pe.matmul(slot(s)[:, P * h:P * h + P], dta[:, n:n + 1].to_broadcast([P, P]),
                                       upper[:, :], start=True, stop=True)
                    mm.then_inc(filled["score"], 1)
                elif k == "uB":
                    i = s[1]
                    t, hq = i // 8, i % 8
                    readers_done(pe, s)
                    pe.wait_ge(sem("m_ready"), i + 1)
                    if i == 0:
                        was_read(pe, ("st", 3))
                        was_read(pe, ("xtr", 7), "D")
                    for h in range(4):
                        head = 4 * hq + h
                        o = slot(s)[64 * (h % 2):64 * (h % 2) + 64, P * (h // 2):P * (h // 2) + P]
                        mm = pe.matmul(o, xd[t][:, 64 * head:64 * head + 64], sbuf_s[:, i % 4, P * h:P * h + P],
                                       start=True, stop=(t == 0), skip_group_check=True)
                        if t == 1:
                            mm = pe.matmul(o, hst[:, 64 * head:64 * head + 64], sbuf_t[:, i % 2, P * h:P * h + P],
                                           start=False, stop=True, skip_group_check=True)
                    mm.then_inc(sem("pv_done"), 1)
                elif k == "ynorm":
                    readers_done(pe, s)
                    for c in range(16):
                        pe.wait_ge(sem("ysq_ready"), c + 1)
                        mm = pe.matmul(slot(s), mean_d[:, :], A(XD + c), start=(c == 0), stop=(c == 15))
                    mm.then_inc(filled["mean"], 1)
                elif k in ("ln", "lnv"):
                    readers_done(pe, s)
                    if k == "ln":
                        pe.wait_ge(sem("econv_done"), 8)
                    for c in range(8):
                        if k == "lnv":
                            pe.wait_ge(sem("lsq_ready"), c + 1)
                        mm = pe.matmul(slot(s), mean_d[:, :], A((AC if k == "ln" else SQ) + c),
                                       start=(c == 0), stop=(c == 7))
                    mm.then_inc(filled["mean"], 1)
                elif k == "job":
                    _, name, j = s
                    n, b0 = blocks[s], first[s]
                    readers_done(pe, s)
                    tag = {"br_ssd": "y", "w_out": "mix", "ff1": "h1", "ff2": "ff", "val_glu": "h2", "b_val": "h2",
                           "b_gate": "h2", "a_gate": "h2", "even_yb": "yb", "even_ya": "ya", "xr": "h3", "gate": "h3",
                           "odd_out": "ly"}.get(name, "h0")
                    if name == "br_dsa":
                        rhs = [A(DQ + c) for c in range(8)]
                        if j == 0:
                            was_read(pe, ("sC", 15))
                    elif name == "br_nsa":
                        rhs = [A(NQ + c) for c in range(8)]
                        if j == 0:
                            was_read(pe, ("sC", 47))
                    elif name == "b_val":
                        rhs = [A(HF + c) for c in range(8)]
                    elif name == "pool":
                        pe.wait_ge(sem("dp_ready"), 2 * (j // 2) + 2)
                        rhs = [A(DP + 2 * (j // 2)), A(DP + 2 * (j // 2) + 1)]
                    elif name == "rg_ig":
                        if j % 2 == 0:
                            pe.wait_ge(sem("conv_done"), 24 + j // 2 + 1)
                        rhs = [A(XC + j // 2)]
                    else:
                        rhs = [(parts[tag][1](c), parts[tag][2](c)) for c in range(n)]
                    for c in range(n):
                        b = b0 + c
                        u = b // 8
                        if name in PLAIN:
                            if b % 8 == 0:
                                pe.wait_ge(w_in[u % RING], 16 * (u // RING + 1))
                            mm = pe.matmul(slot(s)[:, 0:S], ring[:, u % RING, b % 8, :], rhs[c],
                                           start=(c == 0), stop=(c == n - 1))
                        else:
                            if j == 0:
                                pe.wait_ge(sem(f"lo_{tag}"), c + 1)
                            if b % 8 == 0:
                                pe.wait_ge(sem("w_lo_pool" if on_gpsimd(u) else "w_lo_dve"), lo_turn[u])
                            w_hi, w_lo = ring_hi[:, hi_slot[u], b % 8, :], ring_lo[:, u % RING, b % 8, :]
                            hi, lo = rhs[c]
                            pe.matmul(slot(s)[:, 0:S], w_hi, hi, start=(c == 0), stop=False)
                            pe.matmul(slot(s)[:, 0:S], w_hi, lo, start=False, stop=False)
                            mm = pe.matmul(slot(s)[:, 0:S], w_lo, hi, start=False, stop=(c == n - 1))
                        if b % 8 == 7 or c == n - 1:
                            mm.then_inc(filled["proj"], 1)


def kernel(**inputs):
    import numpy as np
    import concourse.bacc as bacc
    from concourse.bass_utils import run_bass_kernel_spmd

    a = {k: np.asarray(v) for k, v in inputs.items()}
    w = a["w_in"][0]
    cuts = np.cumsum([0, 1024, 64, 64, 256, 32, 8, 1024, 768, 48, 2048, 3072, 32, 3072])
    (dq, dk, dv, iq, ik, iw, nq, nkv, ng, sz, xbc, dt, mg) = [w[:, cuts[i]:cuts[i + 1]] for i in range(13)]
    kc, vc, ks, vs, kw, vw = [nkv[:, 128 * i:128 * i + 128] for i in range(6)]

    def tiles(m):
        K, N = m.shape
        return m.reshape(K // 128, 128, N // 128, 128).transpose(2, 0, 1, 3)

    even = a["w_in_even_2"][0]
    val, glu, a_gate, b_val, b_gate = [even[:, 1024 * i:1024 * i + 1024] for i in range(5)]
    odd = a["w_in_odd_2"][0]
    weights = {
        "iq": tiles(iq), "ik": tiles(np.concatenate([ik] * 4, axis=1)), "dk": tiles(np.concatenate([dk, dk], axis=1)),
        "kc": tiles(kc), "vc": tiles(vc), "ks": tiles(ks), "kw": tiles(kw), "dq": tiles(dq), "nq": tiles(nq),
        "xbc": tiles(xbc), "sz": tiles(sz), "mg": tiles(mg),
        "br_dsa": tiles(a["w_br_dsa"][0]), "br_nsa": tiles(a["w_br_nsa"][0]), "br_ssd": tiles(a["w_br_ssd"][0]),
        "w_out": tiles(a["w_out"][0]), "ff1": tiles(a["w_ff1"][0]), "ff2": tiles(a["w_ff2"][0]),
        "val_glu": np.stack([tiles(val), tiles(glu)], axis=1).reshape(16, 8, 128, 128),
        "b_val": tiles(b_val), "b_gate": tiles(b_gate), "a_gate": tiles(a_gate),
        "pool": a["pool_w_2"][0].reshape(4, 2, 128, 2, 128).transpose(0, 3, 1, 2, 4).reshape(8, 2, 128, 128),
        "even_ya": tiles(a["w_out_even_2"][0][:D]), "even_yb": tiles(a["w_out_even_2"][0][D:]), "xr": tiles(odd[:, :1536]), "gate": tiles(odd[:, 1536:]),
        "rg_ig": np.stack([a["w_rg_2"][0], a["w_ig_2"][0]], axis=1).reshape(24, 1, 128, 128),
        "odd_out": tiles(a["w_out_odd_2"][0]),
    }
    parts = []
    for s in schedule():
        if s[0] == "job":
            parts.append(weights[s[1]][s[2]])
    stream = np.concatenate(parts, axis=0)
    stream = np.ascontiguousarray(stream.reshape(-1, 8, 128, 128).transpose(0, 2, 1, 3)).reshape(-1, 128, 1024)

    w_tok = np.concatenate([iw, ng, dt, dv, vs, vw], axis=1).reshape(8, 128, TOK).transpose(1, 0, 2)
    w_cmp = a["nsa_cmp_w"][0].reshape(2, 16, 2, 64, 64).transpose(2, 3, 0, 1, 4).reshape(128, 2, 16, 64)

    def chunks(v):
        return v.reshape(-1, 128).T

    def twice(v):
        return np.concatenate([v, v]).reshape(128, 1)

    pos = a["nsa_cmp_pos"][0].reshape(64, 64).T
    columns = {
        "norm1": chunks(a["norm1_g"]), "dq_g": twice(a["dsa_q_norm"][0]), "dk_g": twice(a["dsa_k_norm"][0]),
        "nq_g": twice(a["nsa_q_norm"][0]),
        "nk_g": np.concatenate([twice(a["nsa_k_norm"][0, i]) for i in range(3)], axis=1),
        "cmp_pos": np.concatenate([pos, pos], axis=0),
        "ssd_cw": a["ssd_conv_w"][0].reshape(4, 24, 128).transpose(2, 1, 0).reshape(128, 96),
        "ssd_cb": chunks(a["ssd_conv_b"]), "ssd_d": chunks(np.repeat(a["ssd_d"][0], 64)),
        "ssd_g": chunks(a["ssd_norm_g"]), "norm2": chunks(a["norm2_g"]), "even_g": chunks(a["norm_even_2"]),
        "even_cw": a["conv_a_w_2"][0].reshape(31, 8, 128).transpose(2, 1, 0).reshape(128, 248),
        "even_cb": chunks(a["conv_a_b_2"]), "ln_g": chunks(a["ln_a_g_2"]), "ln_b": chunks(a["ln_a_b_2"]),
        "pool_b": chunks(a["pool_b_2"]), "pool_s": chunks(a["pool_scale_2"]), "odd_g": chunks(a["norm_odd_2"]),
        "odd_cw": a["conv_c_w_2"][0].reshape(4, 12, 128).transpose(2, 1, 0).reshape(128, 48),
        "odd_cb": chunks(a["conv_c_b_2"]), "b_rg": chunks(a["b_rg_2"]), "b_ig": chunks(a["b_ig_2"]),
        "lam": chunks(a["lru_lambda_2"]), "final_g": chunks(a["final_norm_2"]),
    }
    cols = np.concatenate([columns[name] for name, _ in COLUMNS], axis=1)
    rows = np.broadcast_to(np.concatenate([a["ssd_dt_bias"], a["ssd_a_log"]], axis=1), (128, 64))
    x_t = a["x"][0].T.reshape(8, 128, 256).transpose(1, 0, 2)
    arrays = {"x_t": x_t, "w_stream": stream, "w_tok": w_tok, "w_cmp": w_cmp, "cols": cols, "rows": rows}
    arrays = {k: np.ascontiguousarray(v) for k, v in arrays.items()}

    nc = bacc.Bacc("TRN2", target_bir_lowering=False, num_devices=1)
    aps = [nc.dram_tensor(k, v.shape, mybir.dt.from_np(v.dtype), kind="ExternalInput").ap() for k, v in arrays.items()]
    out = nc.dram_tensor("out_t", (128, 8, 256), F32, kind="ExternalOutput").ap()
    program(nc, *aps, out)
    r = run_bass_kernel_spmd(nc, [arrays], core_ids=[0])
    got = r.results[0]["out_t"]
    return np.ascontiguousarray(got.transpose(1, 0, 2).reshape(1024, 256).T)[None]
```
